# Optimizing a Trainium2 kernel written in Bass

```python
import math
import jax, jax.numpy as jnp
from jax import lax
import numpy as np

D_MODEL = 1024
BATCH = 1
SEQ = 256
DEPTH = 2

CHUNK = 64
N_EVEN = (DEPTH + 1) // 2
N_ODD = DEPTH // 2
EPS = 1e-6

ATT_HEADS = 8
ATT_HEAD_DIM = 64
ATT_WIDTH = ATT_HEADS * ATT_HEAD_DIM
ATT_LEFT_CHUNKS = 8
ATT_BAND = (ATT_LEFT_CHUNKS + 1) * CHUNK
ATT_MAX_REL = 128

POOL_WINDOWS = (2, 4, 8, 16)
POOL_GROUPS = 4
POOL_GROUP_DIM = 128
POOL_WIDTH = POOL_GROUPS * POOL_GROUP_DIM

SGU_BLOCK = 128
SGU_GROUPS = 4
SGU_GROUP_DIM = 128
SGU_WIDTH = SGU_GROUPS * SGU_GROUP_DIM

SB_HEADS = 8
SB_HEAD_DIM = 64
SB_WIDTH = SB_HEADS * SB_HEAD_DIM
SB_QBLOCK = 128

EVEN_IN = 3 * ATT_WIDTH + POOL_WIDTH
EVEN_MIX = ATT_WIDTH + POOL_WIDTH
ODD_IN = 2 * SGU_WIDTH + 3 * SB_WIDTH
ODD_MIX = SGU_WIDTH + SB_WIDTH

N_GROUPS = 4
N_EXP_PER_GROUP = 8
TOP_K = 2
EXPERT_FF = 256

kernel_name = "hybrid_chunk_stream_hmoe"

def rms_norm(x, g):
    xf = x.astype(jnp.float32)
    y = xf * lax.rsqrt(jnp.mean(xf * xf, axis=-1, keepdims=True) + EPS)
    return (y * g.astype(jnp.float32)).astype(x.dtype)

def chunk_band_attention(q, k, v, q_gain, k_gain, rel_bias):
    b, s, h, dh = q.shape
    nc = s // CHUNK
    L = ATT_LEFT_CHUNKS
    q = rms_norm(q, q_gain)
    k = rms_norm(k, k_gain)
    pad = ((0, 0), (L * CHUNK, 0), (0, 0), (0, 0))
    kp = jnp.pad(k, pad).reshape(b, nc + L, CHUNK, h, dh)
    vp = jnp.pad(v, pad).reshape(b, nc + L, CHUNK, h, dh)
    band_idx = jnp.arange(nc)[:, None] + jnp.arange(L + 1)[None, :]
    kb = kp[:, band_idx].reshape(b, nc, ATT_BAND, h, dh)
    vb = vp[:, band_idx].reshape(b, nc, ATT_BAND, h, dh)
    qc = q.reshape(b, nc, CHUNK, h, dh)
    scores = jnp.einsum('bcihd,bcjhd->bhcij', qc, kb,
                        preferred_element_type=jnp.float32) * (1.0 / math.sqrt(dh))
    dist = (jnp.arange(CHUNK)[:, None] + L * CHUNK) - jnp.arange(ATT_BAND)[None, :]
    ridx = jnp.clip(dist, -ATT_MAX_REL, ATT_MAX_REL) + ATT_MAX_REL
    bias = rel_bias[:, ridx].astype(jnp.float32)
    key_chunk = jnp.arange(nc)[:, None] - L + jnp.arange(ATT_BAND)[None, :] // CHUNK
    valid = key_chunk >= 0
    scores = jnp.where(valid[None, None, :, None, :], scores + bias[None, :, None], -1e30)
    probs = jax.nn.softmax(scores, axis=-1)
    out = jnp.einsum('bhcij,bcjhd->bcihd', probs.astype(v.dtype), vb)
    return out.reshape(b, s, h * dh)

def multiscale_pool(p, w_group, scale):
    b, s, _ = p.shape
    pg = p.reshape(b, s, POOL_GROUPS, POOL_GROUP_DIM).astype(jnp.float32)
    cs = jnp.pad(jnp.cumsum(pg, axis=1), ((0, 0), (1, 0), (0, 0), (0, 0)))
    t = jnp.arange(s)[:, None]
    win = jnp.array(POOL_WINDOWS, dtype=jnp.int32)[None, :]
    lo = jnp.maximum(t + 1 - win, 0)
    gidx = jnp.arange(POOL_GROUPS)[None, :]
    win_sum = cs[:, 1:] - cs[:, lo, gidx]
    count = jnp.minimum(t + 1, win).astype(jnp.float32)
    mixed = (win_sum / count[None, :, :, None] - pg).astype(p.dtype)
    y = jnp.einsum('bsgc,gcd->bsgd', mixed, w_group).reshape(b, s, POOL_WIDTH)
    return y * scale

def spatial_gating(u, vv, v_gain, w_s, b_s):
    b, s, _ = u.shape
    nb = s // SGU_BLOCK
    vv = rms_norm(vv, v_gain)
    vb = vv.reshape(b, nb, SGU_BLOCK, SGU_GROUPS, SGU_GROUP_DIM)
    tri = jnp.tril(jnp.ones((SGU_BLOCK, SGU_BLOCK), dtype=bool))
    ws = jnp.where(tri[None], w_s, jnp.zeros_like(w_s))
    mixed = jnp.einsum('gts,bnsgc->bntgc', ws, vb) + b_s.T[:, :, None]
    return u * mixed.reshape(b, s, SGU_WIDTH)

def stick_breaking_attention(q, k, v):
    b, s, h, dh = q.shape
    nq = s // SB_QBLOCK
    qb = q.reshape(b, nq, SB_QBLOCK, h, dh).transpose(1, 0, 2, 3, 4)
    kpos = jnp.arange(s)
    inv = 1.0 / math.sqrt(dh)

    def block(args):
        qblk, i = args
        z = jnp.einsum('bthd,bshd->bhts', qblk, k,
                       preferred_element_type=jnp.float32) * inv
        qpos = i * SB_QBLOCK + jnp.arange(SB_QBLOCK)
        causal = kpos[None, :] < qpos[:, None]
        log_beta = jax.nn.log_sigmoid(z)
        log_rest = jnp.where(causal, jax.nn.log_sigmoid(-z), 0.0)
        tail = lax.cumsum(log_rest, axis=3, reverse=True) - log_rest
        a = jnp.where(causal, jnp.exp(log_beta + tail), 0.0)
        return jnp.einsum('bhts,bshd->bthd', a.astype(v.dtype), v)

    out = lax.map(block, (qb, jnp.arange(nq)))
    return out.transpose(1, 0, 2, 3, 4).reshape(b, s, h * dh)

def hierarchical_moe(x, w_rg, w_re, w_gate, w_up, w_down):
    b, s, d = x.shape
    xt = x.reshape(-1, d)
    n = xt.shape[0]
    g_logits = jnp.einsum('nd,dg->ng', xt, w_rg, preferred_element_type=jnp.float32)
    g_prob = jax.nn.softmax(g_logits, axis=-1)
    g_sel = jnp.argmax(g_logits, axis=-1)
    g_weight = jnp.take_along_axis(g_prob, g_sel[:, None], axis=-1)
    e_logits = jnp.einsum('nd,de->ne', xt, w_re,
                          preferred_element_type=jnp.float32).reshape(n, N_GROUPS, N_EXP_PER_GROUP)
    e_in_group = jnp.take_along_axis(e_logits, g_sel[:, None, None], axis=1)[:, 0]
    top_val, top_idx = lax.top_k(e_in_group, TOP_K)
    top_w = jax.nn.softmax(top_val, axis=-1) * g_weight
    flat_idx = g_sel[:, None] * N_EXP_PER_GROUP + top_idx
    combine = jnp.einsum('nk,nke->ne', top_w,
                         jax.nn.one_hot(flat_idx, N_GROUPS * N_EXP_PER_GROUP, dtype=jnp.float32))
    combine = combine.reshape(n, N_GROUPS, N_EXP_PER_GROUP)
    out = jnp.zeros((n, d), jnp.float32)
    for g in range(N_GROUPS):
        hid = jax.nn.silu(jnp.einsum('nd,edf->nef', xt, w_gate[g])) * \
            jnp.einsum('nd,edf->nef', xt, w_up[g])
        hid = hid * combine[:, g, :, None].astype(hid.dtype)
        out = out + jnp.einsum('nef,efd->nd', hid, w_down[g],
                               preferred_element_type=jnp.float32)
    return out.astype(x.dtype).reshape(b, s, d)

def setup_inputs(seed: int = 0) -> dict:
    key = jax.random.key(seed)
    ks = jax.random.split(key, 24)
    f32 = jnp.float32

    def nrm(k, shape, scale):
        return jax.random.normal(k, shape, f32) * scale

    def gain(k, shape):
        return 1.0 + 0.1 * jax.random.normal(k, shape, f32)

    G, E, F = N_GROUPS, N_EXP_PER_GROUP, EXPERT_FF
    return {
        "x": jax.random.normal(ks[0], (BATCH, SEQ, D_MODEL), f32),
        "mix_norm_even": gain(ks[1], (N_EVEN, D_MODEL)),
        "w_in_even": nrm(ks[2], (N_EVEN, D_MODEL, EVEN_IN), D_MODEL ** -0.5),
        "att_q_norm": gain(ks[3], (N_EVEN, ATT_HEAD_DIM)),
        "att_k_norm": gain(ks[4], (N_EVEN, ATT_HEAD_DIM)),
        "att_rel_bias": nrm(ks[5], (N_EVEN, ATT_HEADS, 2 * ATT_MAX_REL + 1), 0.5),
        "pool_w": nrm(ks[6], (N_EVEN, POOL_GROUPS, POOL_GROUP_DIM, POOL_GROUP_DIM), POOL_GROUP_DIM ** -0.5),
        "pool_scale": gain(ks[7], (N_EVEN, POOL_WIDTH)),
        "w_out_even": nrm(ks[8], (N_EVEN, EVEN_MIX, D_MODEL), EVEN_MIX ** -0.5),
        "mix_norm_odd": gain(ks[9], (N_ODD, D_MODEL)),
        "w_in_odd": nrm(ks[10], (N_ODD, D_MODEL, ODD_IN), D_MODEL ** -0.5),
        "sgu_v_norm": gain(ks[11], (N_ODD, SGU_WIDTH)),
        "sgu_w": nrm(ks[12], (N_ODD, SGU_GROUPS, SGU_BLOCK, SGU_BLOCK), SGU_BLOCK ** -0.5),
        "sgu_b": gain(ks[13], (N_ODD, SGU_GROUPS, SGU_BLOCK)),
        "w_out_odd": nrm(ks[14], (N_ODD, ODD_MIX, D_MODEL), ODD_MIX ** -0.5),
        "ffn_norm": gain(ks[15], (DEPTH, D_MODEL)),
        "w_router_group": nrm(ks[16], (DEPTH, D_MODEL, G), D_MODEL ** -0.5),
        "w_router_expert": nrm(ks[17], (DEPTH, D_MODEL, G * E), D_MODEL ** -0.5),
        "w_exp_gate": nrm(ks[18], (DEPTH, G, E, D_MODEL, F), D_MODEL ** -0.5),
        "w_exp_up": nrm(ks[19], (DEPTH, G, E, D_MODEL, F), D_MODEL ** -0.5),
        "w_exp_down": nrm(ks[20], (DEPTH, G, E, F, D_MODEL), F ** -0.5),
    }

def reference(x, mix_norm_even, w_in_even, att_q_norm, att_k_norm, att_rel_bias,
              pool_w, pool_scale, w_out_even, mix_norm_odd, w_in_odd, sgu_v_norm,
              sgu_w, sgu_b, w_out_odd, ffn_norm, w_router_group, w_router_expert,
              w_exp_gate, w_exp_up, w_exp_down):
    b, s, _ = x.shape
    h = x
    for layer in range(DEPTH):
        i = layer // 2
        if layer % 2 == 0:
            hn = rms_norm(h, mix_norm_even[i])
            proj = jnp.einsum('bsd,de->bse', hn, w_in_even[i])
            q, k, v, p = jnp.split(proj, [ATT_WIDTH, 2 * ATT_WIDTH, 3 * ATT_WIDTH], axis=-1)
            hs = (b, s, ATT_HEADS, ATT_HEAD_DIM)
            ya = chunk_band_attention(q.reshape(hs), k.reshape(hs), v.reshape(hs),
                                      att_q_norm[i], att_k_norm[i], att_rel_bias[i])
            yb = multiscale_pool(p, pool_w[i], pool_scale[i])
            mixed = jnp.concatenate([ya, yb], axis=-1)
            h = h + jnp.einsum('bse,ed->bsd', mixed, w_out_even[i])
        else:
            hn = rms_norm(h, mix_norm_odd[i])
            proj = jnp.einsum('bsd,de->bse', hn, w_in_odd[i])
            u, vv, q, k, v = jnp.split(
                proj, [SGU_WIDTH, 2 * SGU_WIDTH, 2 * SGU_WIDTH + SB_WIDTH,
                       2 * SGU_WIDTH + 2 * SB_WIDTH], axis=-1)
            yc = spatial_gating(jax.nn.gelu(u, approximate=False),
                                jax.nn.gelu(vv, approximate=False),
                                sgu_v_norm[i], sgu_w[i], sgu_b[i])
            hs = (b, s, SB_HEADS, SB_HEAD_DIM)
            yd = stick_breaking_attention(q.reshape(hs), k.reshape(hs), v.reshape(hs))
            mixed = jnp.concatenate([yc, yd], axis=-1)
            h = h + jnp.einsum('bse,ed->bsd', mixed, w_out_odd[i])
        h = h + hierarchical_moe(rms_norm(h, ffn_norm[layer]), w_router_group[layer],
                                 w_router_expert[layer], w_exp_gate[layer],
                                 w_exp_up[layer], w_exp_down[layer])
    return h


_drawn_inputs = setup_inputs


def setup_inputs(seed=0):
    import zlib

    import numpy as np

    out = dict(_drawn_inputs(seed))
    spreads = {}
    factors = {}
    for name, (base, spread) in spreads.items():
        noise = np.random.default_rng([zlib.crc32(name.encode()), seed]).standard_normal(out[name].shape)
        drawn = base * np.exp(spread * noise) if base else spread * noise
        out[name] = __import__('jax').numpy.asarray(drawn.astype(out[name].dtype))
    for name, factor in factors.items():
        out[name] = (out[name] * factor).astype(out[name].dtype)
    return out
```

```python
from collections import namedtuple
from contextlib import ExitStack

import concourse.bass as bass
from concourse import mybir
import numpy as np

F32 = mybir.dt.float32
F32R = mybir.dt.float32r
I32 = mybir.dt.int32
U32 = mybir.dt.uint32
ALU = mybir.AluOpType
ACT = mybir.ActivationFunctionType
AX = mybir.AxisListType

P = 128
S = 256
T = S // P
D = 1024
KD = D // P
HEADS, DH = 8, 64
PAIRS = HEADS // 2
W4 = 512
EPS = 1e-6
WINDOWS = (2, 4, 8, 16)
GROUPS, EXPERTS, FF = 4, 8, 256
NEG = -1e30

CH = 2048
RAW = 12
SPLIT = 3
AHEAD = SPLIT - 1
EVEN_BLOCKS = ("p", "q", "k", "v")
ODD_BLOCKS = ("vv", "u", "q", "k", "v")
PER_GROUP = 3 * EXPERTS
MOE_CHUNKS = GROUPS * PER_GROUP
PROJ0, OUT0 = 0, 2 * len(EVEN_BLOCKS)
MOE0 = OUT0 + 4
PROJ1 = MOE0 + MOE_CHUNKS
OUT1 = PROJ1 + 2 * len(ODD_BLOCKS)
MOE1 = OUT1 + 4
CHUNKS = MOE1 + MOE_CHUNKS


def gu_at(e, half):
    return half if e == 0 else 3 * e - 1 + half


def down_at(e):
    return 3 * e + 4 if e < EXPERTS - 1 else PER_GROUP - 1


C_ID, C_NTRI, C_NONE, C_LT, C_IOTA, C_EPS = 0, 128, 256, 384, 512, 640
C_N = 641


def hybrid_kernel(nc, x, stream, gains, consts, even_pool, even_bias, even_cols, odd_sgu, odd_vgain,
                  routers, out):
    ctx = ExitStack()
    with ctx:
        def sem(name):
            return ctx.enter_context(nc.semaphore(name))

        def sems(tag, *names):
            return namedtuple(tag, names)(*[sem(f"{tag}_{n}") for n in names])

        base = -(-nc.sbuf_base // 32) * 32
        taken = [base]

        def fixed(name, shape, dt=F32):
            t = nc.alloc_sbuf_tensor_at(name, shape, dt, offset=taken[0])
            taken[0] += -(-4 * int(np.prod(shape[1:])) // 32) * 32
            return t

        raw = fixed("raw", [P, RAW, CH])
        whi = fixed("whi", [P, SPLIT, CH], F32R)
        wlo = fixed("wlo", [P, SPLIT, CH], F32R)
        h = fixed("h", [P, T, D])
        gain = fixed("gain", [P, D])
        cst = fixed("cst", [P, C_N])
        stat = fixed("stat", [P, 176])
        arena = taken[0]

        def at(name, shape, kib, dt=F32):
            return nc.alloc_sbuf_tensor_at(name, shape, dt, offset=arena + int(kib * 1024))

        ident = cst[:, C_ID:C_ID + P]
        negtri = cst[:, C_NTRI:C_NTRI + P]
        negones = cst[:, C_NONE:C_NONE + P]
        before = cst[:, C_LT:C_LT + P]
        iota = cst[:, C_IOTA:C_IOTA + P]
        eps = cst[:, C_EPS:C_EPS + 1]

        psum = ctx.enter_context(nc.psum_tensor("psum", [P, 8, W4], F32))

        def bank(b, n=W4):
            return psum[:, b, 0:n]

        raw_landed = [sem(f"raw_landed{i}") for i in range(RAW)]
        hi_done, lo_done, w_used = sem("hi_done"), sem("lo_done"), sem("w_used")
        x_landed, cst_landed, gain_landed, out_written = (
            sem("x_landed"), sem("cst_landed"), sem("gain_landed"), sem("out_written"))

        def load_chunk(sp, c, wait=None):
            slot, index = c
            if wait is not None:
                sp.wait_ge(lo_done, wait)
            sp.dma_start(raw[:, slot, :], stream[bass.ds(index, 1)].rearrange("a p n -> (a p) n")
                         ).then_inc(raw_landed[slot], 16)

        def split_hi(act, c, g=0):
            act.wait_ge(raw_landed[c % RAW], 16 * (c // RAW + 1) + g * (16 * PER_GROUP // RAW))
            if c >= SPLIT:
                act.wait_ge(w_used, c - SPLIT + 1 + g * PER_GROUP)
            nc.scalar.copy(whi[:, c % SPLIT, :], raw[:, c % RAW, :]).then_inc(hi_done, 1)

        def split_lo(dve, c, g=0):
            dve.wait_ge(hi_done, c + 1 + g * PER_GROUP)
            nc.vector.tensor_tensor(wlo[:, c % SPLIT, :], raw[:, c % RAW, :],
                                    whi[:, c % SPLIT, :].bitcast(F32), ALU.subtract).then_inc(lo_done, 1)

        def three(out_ap, hi, lo, c, cols, first, last):
            nc.tensor.matmul(out_ap, hi, whi[:, c % SPLIT, cols], start=first, stop=False)
            nc.tensor.matmul(out_ap, lo, whi[:, c % SPLIT, cols], start=False, stop=False)
            return nc.tensor.matmul(out_ap, hi, wlo[:, c % SPLIT, cols], start=False, stop=last)

        dve_chain, dve_count = sem("dve_chain"), [0]

        def link(ins):
            dve_count[0] += 1
            ins.then_inc(dve_chain, 1)
            nc.vector.wait_ge(dve_chain, dve_count[0])

        ssq, rms, rstd = stat[:, 0:2], stat[:, 2:4], stat[:, 4:6]
        norm = sems("norm", "ssq_ready", "rms_ready", "hn_ready", "turned", "hi_ready", "lo_ready")

        def norm_act(act, ph, hn, h_ready):
            act.wait_ge(*h_ready)
            for t in range(T):
                nc.scalar.activation(hn[:, t, :], h[:, t, :], ACT.Square,
                                     accum_out=ssq[:, t:t + 1]).then_inc(norm.ssq_ready, 1)
            act.wait_ge(norm.ssq_ready, T * (ph + 1))
            if ph == 0:
                act.wait_ge(cst_landed, 16)
            nc.scalar.activation(rms, ssq, ACT.Sqrt, bias=eps, scale=1.0 / D).then_inc(norm.rms_ready, 1)

        def norm_dve(dve, ph, hn):
            dve.wait_ge(norm.rms_ready, ph + 1)
            link(nc.vector.reciprocal(rstd, rms))
            dve.wait_ge(gain_landed, 16 * (ph + 1))
            for t in range(T):
                nc.vector.scalar_tensor_tensor(hn[:, t, :], h[:, t, :], rstd[:, t:t + 1], gain[:],
                                               ALU.mult, ALU.mult).then_inc(norm.hn_ready, 1)

        def norm_pe(pe, ph, hn):
            pe.wait_ge(norm.hn_ready, T * (ph + 1))
            for b in range(4):
                for j in range(2):
                    for t in range(T):
                        k = 2 * b + j
                        mm = nc.tensor.transpose(psum[:, b, j * S + t * P:j * S + (t + 1) * P],
                                                 hn[:, t, k * P:(k + 1) * P], ident)
                mm.then_inc(norm.turned, 1)

        def turned_hi(act, ph, hi):
            for b in range(4):
                act.wait_ge(norm.turned, 4 * ph + b + 1)
                nc.scalar.copy(hi[:, 2 * b:2 * b + 2, :], bank(b).rearrange("p (j s) -> p j s", j=2)
                               ).then_inc(norm.hi_ready, 1)

        def turned_lo(dve, ph, hi, lo):
            for b in range(4):
                dve.wait_ge(norm.hi_ready, 4 * (ph // 2) + b + 1)
                nc.vector.tensor_tensor(lo[:, 2 * b:2 * b + 2, :], bank(b).rearrange("p (j s) -> p j s", j=2),
                                        hi[:, 2 * b:2 * b + 2, :].bitcast(F32), ALU.subtract
                                        ).then_inc(norm.lo_ready, 1)

        proj_out = [sem("proj_out0"), sem("proj_out1")]

        def project(pe, ph, layer, hi, lo, c0, nb):
            if nb == 0:
                pe.wait_ge(norm.lo_ready, 4 * (layer + 1))
            for kh in range(2):
                c = c0 + 2 * nb + kh
                pe.wait_ge(lo_done, c + 1)
                if nb >= 2 and kh == 0:
                    pe.wait_ge(proj_out[layer], 2 * (nb - 1))
                for t in range(T):
                    for kk in range(4):
                        k = 4 * kh + kk
                        mm = three(bank(2 * (nb % 2) + t), hi[:, k, t * P:(t + 1) * P],
                                   lo[:, k, t * P:(t + 1) * P], c, slice(kk * W4, (kk + 1) * W4),
                                   k == 0, k == KD - 1)
                mm.then_inc(w_used, 1)

        def block_out(act, layer, c0, nb, dst, func=None):
            act.wait_ge(w_used, c0 + 2 * nb + 2)
            for t in range(T):
                src = bank(2 * (nb % 2) + t)
                if func is None:
                    ins = nc.scalar.copy(dst[:, t, :], src)
                else:
                    ins = nc.scalar.activation(dst[:, t, :], src, func)
                ins.then_inc(proj_out[layer], 1)

        res_added = [sem("res_added0"), sem("res_added1")]

        def out_project(pe, c0, parts):
            for nb in range(2):
                for kh in range(2):
                    c = c0 + 2 * nb + kh
                    pe.wait_ge(lo_done, c + 1)
                    hi, lo = parts[kh]
                    for t in range(T):
                        for kk in range(4):
                            mm = three(bank(2 * nb + t), hi[:, kk, t * P:(t + 1) * P],
                                       lo[:, kk, t * P:(t + 1) * P], c, slice(kk * W4, (kk + 1) * W4),
                                       kh == 0 and kk == 0, kh == 1 and kk == 3)
                    mm.then_inc(w_used, 1)

        def residual(dve, layer, c0, nb):
            dve.wait_ge(w_used, c0 + 2 * nb + 2)
            for t in range(T):
                cols = slice(nb * W4, (nb + 1) * W4)
                nc.vector.tensor_tensor(h[:, t, cols], bank(2 * nb + t), h[:, t, cols], ALU.add
                                        ).then_inc(res_added[layer], 1)

        hnT_hi0, hnT_lo0 = at("hnT_hi0", [P, KD, S], 0, F32R), at("hnT_lo0", [P, KD, S], 8, F32R)
        qT0, kT0 = at("qT0", [P, PAIRS, S], 0), at("kT0", [P, PAIRS, S], 4)
        mixA_hi, mixA_lo = at("mixA_hi", [P, 4, S], 0, F32R), at("mixA_lo", [P, 4, S], 4, F32R)
        pt0, att = at("pt0", [P, HEADS, P], 8), at("att", [P, T, W4], 12)
        hn0 = at("hn0", [P, T, D], 16)
        p_in, q_in = at("p_in", [P, T, W4], 16), at("q_in", [P, T, W4], 20)
        k_in, v_in = at("k_in", [P, T, W4], 24), at("v_in", [P, T, W4], 28)
        mixP_hi, mixP_lo = at("mixP_hi", [P, 4, S], 16, F32R), at("mixP_lo", [P, 4, S], 32, F32R)
        pt1 = at("pt1", [P, 2, HEADS, P], 20)
        squares = at("squares", [P, T, W4], 32)
        pool_c = at("pool_c", [P, 4, 256 + 128 + 128], 36)
        pooled = at("pooled", [P, 4, S], 44)
        pb = [at("pb0", [P, HEADS, P], 36), at("pb1", [P, HEADS, S], 40)]
        cols0 = stat[:, 8:14]
        hss, hrms, hrs = stat[:, 16:48], stat[:, 48:80], stat[:, 80:112]
        nmax, rsum, rinv = stat[:, 112:128], stat[:, 128:144], stat[:, 144:160]
        ev = sems("even", "pool_c_landed", "cols_landed", "banded", "pooled_ready", "pool_done", "mixP_hi_ready",
                  "mixP_lo_ready", "bias_landed", "bias_masked", "ss_ready", "rms_ready", "qk_ready",
                  "qk_turned", "qT_ready", "scored", "biased", "nmax_ready", "probs_ready", "probs_turned",
                  "pt_act", "pt_dve", "pv_done", "att_ready", "att_turned", "mixA_hi_ready", "mixA_lo_ready")

        def even_pool_loads(pool):
            pool.dma_start(cst[:], consts).then_inc(cst_landed, 16)
            pool.dma_start(gain[:], gains[0].partition_broadcast(P)).then_inc(gain_landed, 16)
            pool.dma_start(pool_c[:], even_pool).then_inc(ev.pool_c_landed, 16)
            pool.dma_start(cols0, even_cols).then_inc(ev.cols_landed, 16)
            pool.wait_ge(norm.hn_ready, T)
            pool.dma_start(gain[:], gains[1].partition_broadcast(P)).then_inc(gain_landed, 16)
            pool.wait_ge(ev.pool_done, 2)
            pool.dma_start(pb[0][:], even_bias[:, 0:HEADS * P].rearrange("p (j k) -> p j k", j=HEADS)
                           ).then_inc(ev.bias_landed, 16)
            pool.dma_start(pb[1][:], even_bias[:, HEADS * P:].rearrange("p (j k) -> p j k", j=HEADS)
                           ).then_inc(ev.bias_landed, 16)
            pool.wait_ge(ev.bias_landed, 32)
            nc.gpsimd.memset(pb[0][0:64, :, 64:128], NEG).then_inc(ev.bias_masked, 1)
            nc.gpsimd.memset(pb[1][0:64, :, 192:256], NEG).then_inc(ev.bias_masked, 1)

        def pool_band_pe(pe):
            pe.wait_ge(ev.pool_c_landed, 16)
            pe.wait_ge(proj_out[0], 2)
            for g in range(4):
                dst = psum[:, 4 + g // 2, (g % 2) * S:(g % 2 + 1) * S]
                nc.tensor.matmul(dst, p_in[:, 0, g * P:(g + 1) * P], pool_c[:, g, 0:256],
                                 start=True, stop=False, skip_group_check=True)
                mm = nc.tensor.matmul(dst[:, P:S], p_in[:, 1, g * P:(g + 1) * P], pool_c[:, g, 256:384],
                                      start=False, stop=True, skip_group_check=True)
                if g % 2:
                    mm.then_inc(ev.banded, 1)

        def pool_weight_pe(pe):
            pe.wait_ge(ev.pooled_ready, 2)
            for g in range(4):
                mm = nc.tensor.matmul(psum[:, 6 + g // 2, (g % 2) * S:(g % 2 + 1) * S],
                                      pool_c[:, g, 384:512], pooled[:, g, :], start=True, stop=True,
                                      skip_group_check=True)
                if g % 2:
                    mm.then_inc(ev.pool_done, 1)

        def heads(ap):
            return ap.rearrange("p (h d) -> p h d", d=DH)

        def head_squares(dve, src, i, out_count):
            dve.wait_ge(proj_out[0], out_count)
            link(nc.vector.tensor_tensor(squares[:], src[:], src[:], ALU.mult))
            nc.vector.tensor_reduce(hss[:, 16 * i:16 * i + 16], squares[:].rearrange("p t (h d) -> p (t h) d", d=DH),
                                    AX.X, ALU.add).then_inc(ev.ss_ready, 1)

        def head_rms(act, i):
            act.wait_ge(ev.ss_ready, i + 1)
            nc.scalar.activation(hrms[:, 16 * i:16 * i + 16], hss[:, 16 * i:16 * i + 16], ACT.Sqrt, bias=eps,
                                 scale=1.0 / DH).then_inc(ev.rms_ready, 1)

        def head_norm(dve, src, i):
            dve.wait_ge(ev.rms_ready, i + 1)
            r = hrs[:, 16 * i:16 * i + 16]
            link(nc.vector.reciprocal(r, hrms[:, 16 * i:16 * i + 16]))
            view = src[:].rearrange("p t (h d) -> p (t h) d", d=DH)
            nc.vector.tensor_tensor(view, view, r.unsqueeze(2).to_broadcast([P, 16, DH]), ALU.mult
                                    ).then_inc(ev.qk_ready, 1)

        def turn_pairs(pe, src, b0, signal):
            for t in range(T):
                for j in range(PAIRS):
                    mm = nc.tensor.transpose(psum[:, b0 + t, j * P:(j + 1) * P], src[:, t, j * P:(j + 1) * P], ident)
                mm.then_inc(signal, 1)

        def pairs_view(b):
            return bank(b).rearrange("p (j s) -> p j s", j=PAIRS)

        def scores_pe(pe, t):
            n = (t + 1) * P
            per = W4 // n
            for par in range(2):
                rows = slice(64 * par, 64 * par + 64)
                for i in range(PAIRS):
                    b = (par if t == 0 else 2 + 2 * par + i // per)
                    mm = nc.tensor.matmul(psum[:, b, (i % per) * n:(i % per + 1) * n], qT0[rows, i, t * P:(t + 1) * P],
                                          kT0[rows, i, 0:n], start=True, stop=True, skip_group_check=True)
                    if i % per == per - 1:
                        mm.then_inc(ev.scored, 1)

        def softmax_dve(dve, t):
            n = (t + 1) * P
            per = W4 // n
            banks = [0, 1] if t == 0 else [2, 3, 4, 5]
            for m, b in enumerate(banks):
                dve.wait_ge(ev.scored, (0 if t == 0 else 2) + m + 1)
                view = pb[t][:, m * per:(m + 1) * per, :]
                nc.vector.tensor_tensor(view, bank(b).rearrange("p (j k) -> p j k", k=n), view, ALU.add
                                        ).then_inc(ev.biased, 1)
            dve.wait_ge(ev.biased, 2 if t == 0 else 6)
            nc.vector.tensor_reduce(nmax[:, 8 * t:8 * t + 8], pb[t][:], AX.X, ALU.max, negate=True
                                    ).then_inc(ev.nmax_ready, 1)

        def softmax_act(act, t):
            act.wait_ge(ev.nmax_ready, t + 1)
            for j in range(HEADS):
                nc.scalar.activation(pb[t][:, j, :], pb[t][:, j, :], ACT.Exp, bias=nmax[:, 8 * t + j:8 * t + j + 1],
                                     accum_out=rsum[:, 8 * t + j:8 * t + j + 1]).then_inc(ev.probs_ready, 1)

        def turn_probs(pe, t):
            for kt in range(t + 1):
                for j in range(HEADS):
                    b = 6 + j // 4 if t == 0 else 2 * kt + j // 4
                    if kt == 0:
                        pe.wait_ge(ev.probs_ready, 8 * t + j + 1)
                    mm = nc.tensor.transpose(psum[:, b, (j % 4) * P:(j % 4 + 1) * P],
                                             pb[t][:, j, kt * P:(kt + 1) * P], ident)
                    if j % 4 == 3:
                        mm.then_inc(ev.probs_turned, 1)

        def pt_copy(eng, signal, t, m):
            eng.wait_ge(ev.probs_turned, (0 if t == 0 else 2) + m + 1)
            if t == 0:
                src, dst = 6 + m, pt0[:, 4 * m:4 * m + 4, :]
            else:
                src, dst = m, pt1[:, m // 2, 4 * (m % 2):4 * (m % 2) + 4, :]
            copy = nc.scalar.copy if eng is nc.scalar else nc.vector.tensor_copy
            copy(dst, bank(src).rearrange("p (j s) -> p j s", j=4)).then_inc(signal, 1)

        def pv_pe(pe, t):
            for j in range(HEADS):
                hd = 2 * (j % 4) + j // 4
                for kt in range(t + 1):
                    lhs = pt0[:, j, :] if t == 0 else pt1[:, kt, j, :]
                    mm = nc.tensor.matmul(psum[:, 4 + t, hd * DH:(hd + 1) * DH], lhs, v_in[:, kt, hd * DH:(hd + 1) * DH],
                                          start=(kt == 0), stop=(kt == t), skip_group_check=True)
            mm.then_inc(ev.pv_done, 1)

        def att_dve(dve, t):
            link(nc.vector.reciprocal(rinv[:, 8 * t:8 * t + 8], rsum[:, 8 * t:8 * t + 8]))
            dve.wait_ge(ev.pv_done, t + 1)
            for par in range(2):
                r = rinv[:, 8 * t + 4 * par:8 * t + 4 * par + 4]
                nc.vector.tensor_tensor(att[:, t, :].rearrange("p (i a d) -> p a i d", a=2, d=DH)[:, par],
                                        bank(4 + t).rearrange("p (i a d) -> p a i d", a=2, d=DH)[:, par],
                                        r.unsqueeze(2).to_broadcast([P, 4, DH]), ALU.mult).then_inc(ev.att_ready, 1)

        def even_pe(pe):
            pe.wait_ge(cst_landed, 16)
            norm_pe(pe, 0, hn0)
            project(pe, 0, 0, hnT_hi0, hnT_lo0, PROJ0, 0)
            project(pe, 0, 0, hnT_hi0, hnT_lo0, PROJ0, 1)
            pool_band_pe(pe)
            project(pe, 0, 0, hnT_hi0, hnT_lo0, PROJ0, 2)
            pool_weight_pe(pe)
            project(pe, 0, 0, hnT_hi0, hnT_lo0, PROJ0, 3)
            pe.wait_ge(ev.pooled_ready, 2)
            pe.wait_ge(ev.qk_ready, 1)
            turn_pairs(pe, q_in, 4, ev.qk_turned)
            pe.wait_ge(ev.qk_ready, 2)
            pe.wait_ge(ev.mixP_lo_ready, 2)
            turn_pairs(pe, k_in, 6, ev.qk_turned)
            pe.wait_ge(ev.qT_ready, 4)
            scores_pe(pe, 0)
            pe.wait_ge(proj_out[0], 8)
            scores_pe(pe, 1)
            turn_probs(pe, 0)
            pe.wait_ge(ev.biased, 6)
            pe.wait_ge(ev.pt_act, 1)
            pe.wait_ge(ev.pt_dve, 1)
            pv_pe(pe, 0)
            turn_probs(pe, 1)
            pe.wait_ge(ev.att_ready, 2)
            for j in range(4):
                mm = nc.tensor.transpose(psum[:, 6, j * P:(j + 1) * P], att[:, 0, j * P:(j + 1) * P], ident)
            mm.then_inc(ev.att_turned, 1)
            pe.wait_ge(ev.pt_act, 3)
            pe.wait_ge(ev.pt_dve, 3)
            pv_pe(pe, 1)
            pe.wait_ge(ev.att_ready, 4)
            for j in range(4):
                mm = nc.tensor.transpose(psum[:, 7, j * P:(j + 1) * P], att[:, 1, j * P:(j + 1) * P], ident)
            mm.then_inc(ev.att_turned, 1)
            pe.wait_ge(ev.mixA_lo_ready, 2)
            out_project(pe, OUT0, [(mixA_hi, mixA_lo), (mixP_hi, mixP_lo)])

        def even_act(act):
            for c in range(AHEAD):
                split_hi(act, c)
            norm_act(act, 0, hn0, (x_landed, 16))
            turned_hi(act, 0, hnT_hi0)
            dst = {"p": p_in, "q": q_in, "k": k_in, "v": v_in}
            for c in range(2 * len(EVEN_BLOCKS)):
                if c % 2 == 0 and c > 0:
                    block_out(act, 0, PROJ0, c // 2 - 1, dst[EVEN_BLOCKS[c // 2 - 1]])
                if c in (5, 7):
                    head_rms(act, (c - 5) // 2)
                if c == 6:
                    act.wait_ge(ev.cols_landed, 16)
                    for b in range(2):
                        act.wait_ge(ev.pool_done, b + 1)
                        for g in (2 * b, 2 * b + 1):
                            nc.scalar.activation(mixP_hi[:, g, :], psum[:, 6 + b, (g % 2) * S:(g % 2 + 1) * S],
                                                 ACT.Copy, scale=cols0[:, 2 + g:3 + g]).then_inc(ev.mixP_hi_ready, 1)
                split_hi(act, PROJ0 + c + AHEAD)
            block_out(act, 0, PROJ0, 3, v_in)
            softmax_act(act, 0)
            softmax_act(act, 1)
            pt_copy(act, ev.pt_act, 0, 0)
            pt_copy(act, ev.pt_act, 1, 0)
            pt_copy(act, ev.pt_act, 1, 2)
            for t in range(T):
                act.wait_ge(ev.att_turned, t + 1)
                nc.scalar.copy(mixA_hi[:, :, t * P:(t + 1) * P], pairs_view(6 + t)).then_inc(ev.mixA_hi_ready, 1)
            for c in range(OUT0, OUT0 + 4):
                split_hi(act, c + AHEAD)

        def even_dve(dve):
            for c in range(AHEAD):
                split_lo(dve, c)
            norm_dve(dve, 0, hn0)
            turned_lo(dve, 0, hnT_hi0, hnT_lo0)
            for c in range(2 * len(EVEN_BLOCKS)):
                if c == 4:
                    for b in range(2):
                        dve.wait_ge(ev.banded, b + 1)
                        nc.vector.tensor_copy(pooled[:, 2 * b:2 * b + 2, :],
                                              bank(4 + b).rearrange("p (j s) -> p j s", j=2)
                                              ).then_inc(ev.pooled_ready, 1)
                    head_squares(dve, q_in, 0, 4)
                if c == 5:
                    head_norm(dve, q_in, 0)
                if c == 6:
                    head_squares(dve, k_in, 1, 6)
                    dve.wait_ge(ev.ss_ready, 2)
                    for g in range(4):
                        dve.wait_ge(ev.mixP_hi_ready, 2 * (g // 2) + 2)
                        ins = nc.vector.scalar_tensor_tensor(
                            mixP_lo[:, g, :], psum[:, 6 + g // 2, (g % 2) * S:(g % 2 + 1) * S], cols0[:, 2 + g:3 + g],
                            mixP_hi[:, g, :].bitcast(F32), ALU.mult, ALU.subtract)
                        if g % 2:
                            ins.then_inc(ev.mixP_lo_ready, 1)
                if c == 7:
                    head_norm(dve, k_in, 1)
                split_lo(dve, PROJ0 + c + AHEAD)
            for t in range(T):
                dve.wait_ge(ev.qk_turned, t + 1)
                nc.vector.tensor_scalar(qT0[:, :, t * P:(t + 1) * P], pairs_view(4 + t), cols0[:, 0:1], DH ** -0.5,
                                        ALU.mult, ALU.mult).then_inc(ev.qT_ready, 1)
            for t in range(T):
                dve.wait_ge(ev.qk_turned, t + 3)
                nc.vector.tensor_scalar(kT0[:, :, t * P:(t + 1) * P], pairs_view(6 + t), cols0[:, 1:2], None,
                                        ALU.mult).then_inc(ev.qT_ready, 1)
            dve.wait_ge(ev.bias_masked, 2)
            softmax_dve(dve, 0)
            softmax_dve(dve, 1)
            pt_copy(dve, ev.pt_dve, 0, 1)
            att_dve(dve, 0)
            pt_copy(dve, ev.pt_dve, 1, 1)
            pt_copy(dve, ev.pt_dve, 1, 3)
            att_dve(dve, 1)
            for t in range(T):
                dve.wait_ge(ev.mixA_hi_ready, t + 1)
                nc.vector.tensor_tensor(mixA_lo[:, :, t * P:(t + 1) * P], pairs_view(6 + t),
                                        mixA_hi[:, :, t * P:(t + 1) * P].bitcast(F32), ALU.subtract
                                        ).then_inc(ev.mixA_lo_ready, 1)
            for c in range(OUT0, OUT0 + 4):
                if c == OUT0 + 2:
                    residual(dve, 0, OUT0, 0)
                split_lo(dve, c + AHEAD)
            residual(dve, 0, OUT0, 1)

        hnT_hi1, hnT_lo1 = at("hnT_hi1", [P, KD, S], 0, F32R), at("hnT_lo1", [P, KD, S], 8, F32R)
        qT1, kT1 = at("qT1", [P, PAIRS, S], 0), at("kT1", [P, PAIRS, S], 4)
        mixD_hi, mixD_lo = at("mixD_hi", [P, 4, S], 0, F32R), at("mixD_lo", [P, 4, S], 4, F32R)
        HALF = 4 * S + 4 * P
        rest = at("rest", [P, HALF], 8)
        hn2 = at("hn2", [P, T, D], 16)
        u_in, vv_in = at("u_in", [P, T, W4], 16), at("vv_in", [P, T, W4], 20)
        mixC_hi, mixC_lo = at("mixC_hi", [P, 4, S], 20, F32R), at("mixC_lo", [P, 4, S], 16, F32R)
        q1_in, k1_in, v1_in = at("q1_in", [P, T, W4], 24), at("k1_in", [P, T, W4], 28), at("v1_in", [P, T, W4], 32)
        stick = at("stick", [P, HALF], 24)
        sgu = at("sgu", [P, 4 * P + 4], 36)
        vgain = at("vgain", [P, W4], 38.25)
        bigid = at("bigid", [P, P], 40.25)
        soft = at("soft", [P, HALF], 41)
        ssv, rmsv, rsv = stat[:, 16:18], stat[:, 18:20], stat[:, 20:22]
        od = sems("odd", "sgu_landed", "vgain_landed", "ssv_ready", "rmsv_ready", "vn_ready", "gated", "yc_ready",
                  "yc_turned", "mixC_hi_ready", "mixC_lo_ready", "qk_turned", "qT_ready", "z_done", "abs_ready",
                  "exp_ready", "ln_ready", "rest_ready", "sum_done", "stick_ready", "av_done", "mixD_hi_ready",
                  "mixD_lo_ready", "big_ready", "tril_ready")

        def odd_pool_loads(pool):
            pool.wait_ge(res_added[0], 4)
            pool.wait_ge(norm.hn_ready, 2 * T)
            pool.dma_start(gain[:], gains[2].partition_broadcast(P)).then_inc(gain_landed, 16)
            pool.wait_ge(norm.hn_ready, 3 * T)
            pool.dma_start(gain[:], gains[3].partition_broadcast(P)).then_inc(gain_landed, 16)
            pool.dma_start(sgu[:], odd_sgu).then_inc(od.sgu_landed, 16)
            pool.dma_start(vgain[:], odd_vgain.partition_broadcast(P)).then_inc(od.vgain_landed, 16)
            pool.wait_ge(od.sgu_landed, 16)
            view = sgu[:, 0:4 * P].rearrange("p (g t) -> p g t", g=4)
            nc.gpsimd.affine_select(out=view, in_=view, pattern=[[0, 4], [1, P]], compare_op=ALU.is_ge, fill=0.0,
                                    base=0, channel_multiplier=-1).then_inc(od.tril_ready, 1)

        def gating_pe(pe):
            pe.wait_ge(od.tril_ready, 1)
            for n in range(T):
                pe.wait_ge(od.vn_ready, n + 1)
                for g in range(4):
                    mm = nc.tensor.matmul(psum[:, 4 + n, g * P:(g + 1) * P], sgu[:, g * P:(g + 1) * P],
                                          vv_in[:, n, g * P:(g + 1) * P], start=True, stop=True, skip_group_check=True)
                mm.then_inc(od.gated, 1)

        def half_parts(view):
            return (view[:, 0:4 * S].rearrange("p (i s) -> p i s", i=4),
                    view[:, 4 * S:HALF].rearrange("p (i s) -> p i s", i=4))

        def half_banks(par):
            return psum[:, 3 * par:3 * par + 3, :].rearrange("p b n -> p (b n)")

        def z_pe(pe, par):
            rows = slice(64 * par, 64 * par + 64)
            z0, z1 = half_parts(half_banks(par))
            for i in range(PAIRS):
                nc.tensor.matmul(z0[:, i, :], kT1[rows, i, 0:P], qT1[rows, i, :], start=(i % 2 == 0), stop=False,
                                 skip_group_check=True)
            for i in range(PAIRS):
                mm = nc.tensor.matmul(z1[:, i, :], kT1[rows, i, P:S], qT1[rows, i, P:S], start=(i == 0), stop=False,
                                      skip_group_check=True)
            mm.then_inc(od.z_done, 1)

        def sum_pe(pe, par):
            z0, z1 = half_parts(half_banks(par))
            r0, r1 = half_parts(rest[:])
            pe.wait_ge(od.rest_ready, 3 * (par + 1))
            for m in range(2):
                hd = slice(2 * m, 2 * m + 2)
                nc.tensor.matmul(z0[:, hd, :], negtri, r0[:, hd, :], start=False, stop=False, skip_group_check=True)
                nc.tensor.matmul(z0[:, hd, P:S], negones, r1[:, hd, :], start=False, stop=False, skip_group_check=True)
            nc.tensor.matmul(z1[:, :, :], negtri, r1[:, :, :], start=False, stop=False, skip_group_check=True)
            if par == 0:
                pe.wait_ge(od.big_ready, 1)
            for i in range(PAIRS):
                nc.tensor.matmul(z0[:, i, 0:P], bigid[:], negtri, start=False, stop=True, skip_group_check=True)
                mm = nc.tensor.matmul(z1[:, i, :], bigid[:], negtri, start=False, stop=True, skip_group_check=True)
            mm.then_inc(od.sum_done, 1)

        def av_pe(pe, par):
            pe.wait_ge(od.stick_ready, par + 1)
            a0, a1 = half_parts(stick[:])
            rows = slice(64 * par, 64 * par + 64)
            for i in range(PAIRS):
                hd = 2 * i + par
                dst = psum[rows, 6 + i // 2, (i % 2) * S:(i % 2 + 1) * S]
                nc.tensor.matmul(dst, v1_in[:, 0, hd * DH:(hd + 1) * DH], a0[:, i, :], start=True, stop=False,
                                 skip_group_check=True)
                mm = nc.tensor.matmul(dst[:, P:S], v1_in[:, 1, hd * DH:(hd + 1) * DH], a1[:, i, :],
                                      start=False, stop=True, skip_group_check=True)
            mm.then_inc(od.av_done, 1)

        def odd_pe(pe):
            norm_pe(pe, 2, hn2)
            for nb in range(3):
                project(pe, 2, 1, hnT_hi1, hnT_lo1, PROJ1, nb)
            gating_pe(pe)
            project(pe, 2, 1, hnT_hi1, hnT_lo1, PROJ1, 3)
            pe.wait_ge(od.yc_ready, 8)
            turn_pairs(pe, u_in, 6, od.yc_turned)
            project(pe, 2, 1, hnT_hi1, hnT_lo1, PROJ1, 4)
            pe.wait_ge(proj_out[1], 8)
            turn_pairs(pe, q1_in, 4, od.qk_turned)
            pe.wait_ge(od.mixC_lo_ready, 2)
            turn_pairs(pe, k1_in, 6, od.qk_turned)
            pe.wait_ge(proj_out[1], 10)
            pe.wait_ge(od.qT_ready, 4)
            z_pe(pe, 0)
            z_pe(pe, 1)
            for par in range(2):
                sum_pe(pe, par)
                av_pe(pe, par)
            pe.wait_ge(od.mixD_lo_ready, 2)
            out_project(pe, OUT1, [(mixC_hi, mixC_lo), (mixD_hi, mixD_lo)])

        def stick_act(act, par):
            z = half_banks(par)
            act.wait_ge(od.z_done, par + 1)
            if par:
                act.wait_ge(od.rest_ready, 3)
            nc.scalar.activation(soft[:], z, ACT.Abs).then_inc(od.abs_ready, 1)
            act.wait_ge(od.abs_ready, par + 1)
            nc.scalar.activation(soft[:], soft[:], ACT.Exp, scale=-1.0).then_inc(od.exp_ready, 1)
            act.wait_ge(od.exp_ready, par + 1)
            nc.scalar.activation(soft[:], soft[:], ACT.Ln, bias=1.0).then_inc(od.ln_ready, 1)

        def stick_dve(dve, par):
            z = half_banks(par)
            r0, r1 = half_parts(rest[:])
            dve.wait_ge(od.ln_ready, par + 1)
            if par:
                dve.wait_ge(od.sum_done, 1)
            nc.vector.scalar_tensor_tensor(rest[:], z, 0.0, soft[:], ALU.max, ALU.add).then_inc(od.rest_ready, 1)
            dve.wait_ge(od.rest_ready, 3 * par + 1)
            mask = before.unsqueeze(1).to_broadcast([P, 4, P])
            nc.vector.tensor_tensor(r0[:, :, 0:P], r0[:, :, 0:P], mask, ALU.mult).then_inc(od.rest_ready, 1)
            nc.vector.tensor_tensor(r1, r1, mask, ALU.mult).then_inc(od.rest_ready, 1)

        def weights_act(act, par):
            act.wait_ge(od.sum_done, par + 1)
            if par:
                act.wait_ge(od.av_done, 1)
            nc.scalar.activation(stick[:], half_banks(par), ACT.Exp).then_inc(od.stick_ready, 1)

        def odd_act(act):
            norm_act(act, 2, hn2, (m.h_added, 4 * GROUPS))
            turned_hi(act, 2, hnT_hi1)
            dst = {"vv": vv_in, "u": u_in, "q": q1_in, "k": k1_in, "v": v1_in}
            for c in range(2 * len(ODD_BLOCKS)):
                if c % 2 == 0 and c > 0:
                    name = ODD_BLOCKS[c // 2 - 1]
                    block_out(act, 1, PROJ1, c // 2 - 1, dst[name], ACT.Gelu if name in ("vv", "u") else None)
                if c == 5:
                    act.wait_ge(od.ssv_ready, 2)
                    nc.scalar.activation(rmsv, ssv, ACT.Sqrt, bias=eps, scale=1.0 / W4).then_inc(od.rmsv_ready, 1)
                if c == 9:
                    for t in range(T):
                        act.wait_ge(od.yc_turned, T)
                        nc.scalar.copy(mixC_hi[:, :, t * P:(t + 1) * P], pairs_view(6 + t)).then_inc(od.mixC_hi_ready, 1)
                split_hi(act, PROJ1 + c + AHEAD)
            block_out(act, 1, PROJ1, 4, v1_in)
            stick_act(act, 0)
            stick_act(act, 1)
            weights_act(act, 0)
            weights_act(act, 1)
            for b in range(2):
                act.wait_ge(od.av_done, 2)
                nc.scalar.copy(mixD_hi[:, 2 * b:2 * b + 2, :], bank(6 + b).rearrange("p (j s) -> p j s", j=2)
                               ).then_inc(od.mixD_hi_ready, 1)
            for c in range(OUT1, OUT1 + 4):
                split_hi(act, c + AHEAD)

        def odd_dve(dve):
            norm_dve(dve, 2, hn2)
            nc.vector.tensor_scalar(bigid[:], ident, -NEG, None, ALU.mult).then_inc(od.big_ready, 1)
            turned_lo(dve, 2, hnT_hi1, hnT_lo1)
            for c in range(2 * len(ODD_BLOCKS)):
                if c == 4:
                    dve.wait_ge(proj_out[1], 2)
                    for t in range(T):
                        nc.vector.tensor_tensor_reduce(soft[:, t * W4:(t + 1) * W4], vv_in[:, t, :], vv_in[:, t, :], 1.0, 0.0,
                                                       ALU.mult, ALU.add, ssv[:, t:t + 1]).then_inc(od.ssv_ready, 1)
                if c == 5:
                    dve.wait_ge(od.rmsv_ready, 1)
                    link(nc.vector.reciprocal(rsv, rmsv))
                    dve.wait_ge(od.vgain_landed, 16)
                    for t in range(T):
                        nc.vector.scalar_tensor_tensor(vv_in[:, t, :], vv_in[:, t, :], rsv[:, t:t + 1], vgain[:],
                                                       ALU.mult, ALU.mult).then_inc(od.vn_ready, 1)
                if c == 7:
                    dve.wait_ge(proj_out[1], 4)
                    for n in range(T):
                        dve.wait_ge(od.gated, n + 1)
                        for g in range(4):
                            cs = slice(g * P, (g + 1) * P)
                            nc.vector.scalar_tensor_tensor(u_in[:, n, cs], psum[:, 4 + n, cs],
                                                           sgu[:, 4 * P + g:4 * P + g + 1], u_in[:, n, cs],
                                                           ALU.add, ALU.mult).then_inc(od.yc_ready, 1)
                if c == 9:
                    for t in range(T):
                        dve.wait_ge(od.mixC_hi_ready, t + 1)
                        nc.vector.tensor_tensor(mixC_lo[:, :, t * P:(t + 1) * P], pairs_view(6 + t),
                                                mixC_hi[:, :, t * P:(t + 1) * P].bitcast(F32), ALU.subtract
                                                ).then_inc(od.mixC_lo_ready, 1)
                split_lo(dve, PROJ1 + c + AHEAD)
            for t in range(T):
                dve.wait_ge(od.qk_turned, t + 1)
                nc.vector.tensor_scalar(qT1[:, :, t * P:(t + 1) * P], pairs_view(4 + t), DH ** -0.5, None,
                                        ALU.mult).then_inc(od.qT_ready, 1)
            for t in range(T):
                dve.wait_ge(od.qk_turned, t + 3)
                nc.vector.tensor_copy(kT1[:, :, t * P:(t + 1) * P], pairs_view(6 + t)).then_inc(od.qT_ready, 1)
            stick_dve(dve, 0)
            stick_dve(dve, 1)
            for b in range(2):
                dve.wait_ge(od.mixD_hi_ready, b + 1)
                nc.vector.tensor_tensor(mixD_lo[:, 2 * b:2 * b + 2, :], bank(6 + b).rearrange("p (j s) -> p j s", j=2),
                                        mixD_hi[:, 2 * b:2 * b + 2, :].bitcast(F32), ALU.subtract
                                        ).then_inc(od.mixD_lo_ready, 1)
            for c in range(OUT1, OUT1 + 4):
                if c == OUT1 + 2:
                    residual(dve, 1, OUT1, 0)
                split_lo(dve, c + AHEAD)
            residual(dve, 1, OUT1, 1)

        hn_hi, hn_lo = at("hn_hi", [P, T, D], 0, F32R), at("hn_lo", [P, T, D], 8, F32R)
        hnT = at("hnT", [P, KD, S], 16)
        y_hi, y_lo = at("y_hi", [P, D], 16, F32R), at("y_lo", [P, D], 20, F32R)
        hn1 = at("hn1", [P, T, D], 24)
        x_hi, x_lo = at("x_hi", [P, KD, P], 24, F32R), at("x_lo", [P, KD, P], 28, F32R)
        pick, pickT = at("pick", [P, T, P], 32, F32R), at("pickT", [P, S], 33, F32R)
        gate, hid = at("gate", [P, FF], 34), at("hid", [P, FF], 35)
        hidT_hi, hidT_lo = at("hidT_hi", [P, 2, 2, P], 36, F32R), at("hidT_lo", [P, 2, 2, P], 38, F32R)
        rw = at("rw", [P, KD, 36], 40)
        r_small = at("r_small", [P, 512], 41.25)
        top_idx = at("top_idx", [P, 4, 8], 43.5, U32)
        spill = at("spill", [P, 2], 43.75, I32)

        def rs(a, n):
            return r_small[:, a:a + n]
        logits = rs(0, 72).rearrange("p (t n) -> p t n", t=T)
        g8 = rs(72, 16).rearrange("p (t n) -> p t n", t=T)
        gmax = rs(88, 16).rearrange("p (t n) -> p t n", t=T)
        onehot = rs(104, 8).rearrange("p (t n) -> p t n", t=T)
        noh = rs(112, 8).rearrange("p (t n) -> p t n", t=T)
        e_of_g = rs(120, 64).rearrange("p (t e g) -> p t e g", t=T, e=EXPERTS)
        e8 = rs(184, 16).rearrange("p (t n) -> p t n", t=T)
        emax = rs(200, 16).rearrange("p (t n) -> p t n", t=T)
        idx = rs(216, 32).rearrange("p (t n) -> p t n", t=4)
        ngmax, gexp, gsum = rs(248, 2), rs(250, 8), rs(258, 2)
        ediff, eexp, esum, w1, w2 = rs(260, 2), rs(262, 2), rs(264, 2), rs(266, 2), rs(268, 2)
        comb = rs(270, 16).rearrange("p (t n) -> p t n", t=T)
        comb2 = rs(286, 16).rearrange("p (t n) -> p t n", t=T)
        ranks = rs(302, 12)
        pos = rs(314, 2)
        pos_tmp = rs(316, 8).rearrange("p (t n) -> p t n", t=T)
        slot_of = rs(324, 10).rearrange("p (g t) -> p g t", t=T)
        over, over_g = rs(334, 4), rs(338, 2)
        cg = rs(340, 8)

        moe_names = ("rw_landed", "hn_hi_ready", "hn_lo_ready", "hnT_act", "hnT_dve", "routed", "pad_ready",
                     "ngmax_ready", "gsum_ready", "ediff_ready", "eexp_ready", "onehot_ready", "ranked", "comb_ready",
                     "spill_ready", "pick_ready", "gathered", "x_hi_ready", "x_lo_ready", "pickT_turned",
                     "pickT_ready", "cg_done", "cg_ready", "gate_ready", "hid_ready", "hid_turned", "hidT_hi_ready",
                     "hidT_lo_ready", "y_hi_ready", "y_lo_ready", "scattered", "h_added")
        m = sems("moe", *moe_names)
        def group_no(layer, g):
            return g + GROUPS * layer

        def pass_no(layer, gi):
            return gi + (GROUPS + 1) * layer

        sp_names = ("landed", "gu_done", "gate_ready", "hid_ready", "hid_turned", "hidT_hi_ready", "hidT_lo_ready",
                    "used", "y_hi_ready", "y_lo_ready", "scattered", "h_added")
        spill_sems = [sems(f"spill{i}", *sp_names) for i in range(2)]
        MOE_C0 = (MOE0, MOE1)

        def moe_pool_loads(pool, layer):
            pool.wait_ge(norm.hn_ready, (2 * layer + 2) * T)
            pool.dma_start(rw[:], routers[layer]).then_inc(m.rw_landed, 16)

        def route_pe(pe, layer):
            ph = 2 * layer + 1
            norm_pe(pe, ph, hn1)
            pe.wait_ge(m.rw_landed, 16 * (layer + 1))
            pe.wait_ge(m.hnT_act, 2 * (layer + 1))
            pe.wait_ge(m.hnT_dve, 2 * (layer + 1))
            for t in range(T):
                for k in range(KD):
                    mm = nc.tensor.matmul(psum[:, 4, t * 36:(t + 1) * 36], hnT[:, k, t * P:(t + 1) * P], rw[:, k, :],
                                          start=(k == 0), stop=(k == KD - 1), skip_group_check=True)
            mm.then_inc(m.routed, 1)
            pe.wait_ge(m.onehot_ready, 3 * (layer + 1))
            nc.tensor.matmul(psum[:, 5, 0:4], before, onehot[:, 0, :], start=True, stop=True, skip_group_check=True)
            nc.tensor.matmul(psum[:, 5, 4:8], before, onehot[:, 1, :], start=True, stop=False, skip_group_check=True)
            nc.tensor.matmul(psum[:, 5, 4:8], negones, noh[:, 0, :], start=False, stop=True, skip_group_check=True)
            for t in range(T):
                mm = nc.tensor.matmul(psum[:, 5, 8:12], negones, noh[:, t, :], start=(t == 0), stop=(t == 1),
                                      skip_group_check=True)
            mm.then_inc(m.ranked, 1)

        def route_act(act, layer, h_ready):
            ph = 2 * layer + 1
            norm_act(act, ph, hn1, h_ready)
            for b in (0, 2):
                act.wait_ge(norm.turned, 4 * ph + b + 1)
                nc.scalar.copy(hnT[:, 2 * b:2 * b + 2, :], bank(b).rearrange("p (j s) -> p j s", j=2)
                               ).then_inc(m.hnT_act, 1)
            nc.scalar.copy(hn_hi[:], hn1[:]).then_inc(m.hn_hi_ready, 1)
            act.wait_ge(m.ngmax_ready, 2 * (layer + 1))
            for t in range(T):
                nc.scalar.activation(gexp[:, 4 * t:4 * t + 4], logits[:, t, 0:4], ACT.Exp, bias=ngmax[:, t:t + 1],
                                     accum_out=gsum[:, t:t + 1]).then_inc(m.gsum_ready, 1)
            act.wait_ge(m.ediff_ready, layer + 1)
            nc.scalar.activation(eexp, ediff, ACT.Exp).then_inc(m.eexp_ready, 1)

        def route_dve(dve, layer):
            ph = 2 * layer + 1
            norm_dve(dve, ph, hn1)
            for b in (1, 3):
                dve.wait_ge(norm.turned, 4 * ph + b + 1)
                nc.vector.tensor_copy(hnT[:, 2 * b:2 * b + 2, :], bank(b).rearrange("p (j s) -> p j s", j=2)
                                      ).then_inc(m.hnT_dve, 1)
            link(nc.vector.memset(g8, -3e38))
            dve.wait_ge(m.routed, layer + 1)
            link(nc.vector.tensor_copy(logits, psum[:, 4, 0:72].rearrange("p (t n) -> p t n", t=T)))
            link(nc.vector.tensor_copy(g8[:, :, 0:4], logits[:, :, 0:4]))
            for t in range(T):
                link(nc.vector.max(gmax[:, t, :], g8[:, t, :]))
                link(nc.vector.max_index(top_idx[:, t, :], gmax[:, t, :], g8[:, t, :]))
                nc.vector.tensor_scalar(ngmax[:, t:t + 1], gmax[:, t, 0:1], -1.0, None, ALU.mult
                                        ).then_inc(m.ngmax_ready, 1)
            link(nc.vector.tensor_copy(idx[:, 0:2, :], top_idx[:, 0:2, :]))
            for t in range(T):
                nc.vector.tensor_scalar(onehot[:, t, :], iota[:, 0:4], idx[:, t, 0:1], None, ALU.is_equal
                                        ).then_inc(m.onehot_ready, 1)
            dve.wait_ge(m.onehot_ready, 3 * layer + 2)
            nc.vector.tensor_scalar(noh, onehot, -1.0, None, ALU.mult).then_inc(m.onehot_ready, 1)
            link(nc.vector.tensor_tensor(e_of_g, logits[:, :, 4:36].rearrange("p t (g e) -> p t e g", g=GROUPS),
                                         onehot.unsqueeze(2).to_broadcast([P, T, EXPERTS, GROUPS]), ALU.mult))
            link(nc.vector.tensor_reduce(e8, e_of_g, AX.X, ALU.add))
            for t in range(T):
                link(nc.vector.max(emax[:, t, :], e8[:, t, :]))
                link(nc.vector.max_index(top_idx[:, 2 + t, :], emax[:, t, :], e8[:, t, :]))
            link(nc.vector.tensor_copy(idx[:, 2:4, :], top_idx[:, 2:4, :]))
            nc.vector.tensor_tensor(ediff, emax[:, :, 1], emax[:, :, 0], ALU.subtract).then_inc(m.ediff_ready, 1)
            dve.wait_ge(m.ranked, layer + 1)
            link(nc.vector.tensor_copy(ranks, psum[:, 5, 0:12]))
            link(nc.vector.tensor_tensor(pos_tmp, ranks[:, 0:8].rearrange("p (t n) -> p t n", t=T), onehot, ALU.mult))
            link(nc.vector.tensor_reduce(pos, pos_tmp, AX.X, ALU.add))
            link(nc.vector.tensor_scalar(slot_of[:, GROUPS, :], pos, -float(P), None, ALU.add))
            link(nc.vector.tensor_scalar(pos, pos, 1.0, None, ALU.add))
            for t in range(T):
                link(nc.vector.tensor_scalar(slot_of[:, 0:GROUPS, t], onehot[:, t, :], pos[:, t:t + 1], -1.0,
                                             ALU.mult, ALU.add))
            pick_dve(dve, layer, 0)
            link(nc.vector.tensor_scalar(over, ranks[:, 8:12], float(P), None, ALU.is_gt))
            link(nc.vector.scalar_tensor_tensor(over, iota[:, 0:4], 1.0, over, ALU.add, ALU.mult))
            link(nc.vector.tensor_reduce(over_g[:, 0:1], over, AX.X, ALU.add))
            link(nc.vector.tensor_scalar(over_g[:, 1:2], over_g[:, 0:1], -1.0, 0.0, ALU.add, ALU.max))
            nc.vector.tensor_copy(spill[:], over_g).then_inc(m.spill_ready, 1)
            dve.wait_ge(m.hn_hi_ready, layer + 1)
            nc.vector.tensor_tensor(hn_lo[:], hn1[:], hn_hi[:].bitcast(F32), ALU.subtract).then_inc(m.hn_lo_ready, 1)
            dve.wait_ge(m.eexp_ready, layer + 1)
            dve.wait_ge(m.gsum_ready, 2 * (layer + 1))
            link(nc.vector.scalar_tensor_tensor(esum, eexp, 1.0, gsum, ALU.add, ALU.mult))
            link(nc.vector.reciprocal(w1, esum))
            link(nc.vector.tensor_tensor(w2, eexp, w1, ALU.mult))
            for t in range(T):
                link(nc.vector.tensor_scalar(comb[:, t, :], iota[:, 0:8], idx[:, 2 + t, 0:1], w1[:, t:t + 1],
                                             ALU.is_equal, ALU.mult))
                link(nc.vector.tensor_scalar(comb2[:, t, :], iota[:, 0:8], idx[:, 2 + t, 1:2], w2[:, t:t + 1],
                                             ALU.is_equal, ALU.mult))
            nc.vector.tensor_tensor(comb, comb, comb2, ALU.add).then_inc(m.comb_ready, 1)

        def pick_dve(dve, layer, gi):
            if not (layer == 0 and isinstance(gi, int)):
                dve.wait_ge(m.cg_done, pass_no(layer, gi))
            for t in range(T):
                nc.vector.tensor_scalar(pick[:, t, :], iota,
                                        slot_of[:, bass.ds(gi, 1), t:t + 1].rearrange("p a t -> p (a t)"), None,
                                        ALU.is_equal).then_inc(m.pick_ready, 1)

        GATHER = ((5, "hi", 0), (6, "lo", 0), (7, "hi", 1), (5, "lo", 1))

        def gather_pe(pe, layer, gi):
            pe.wait_ge(m.pick_ready, 2 * pass_no(layer, gi) + 2)
            for n, (b, part, half) in enumerate(GATHER):
                if n == 3:
                    pe.wait_ge(m.x_hi_ready, 2 * pass_no(layer, gi) + 1)
                src = hn_hi if part == "hi" else hn_lo
                for kk in range(4):
                    k = 4 * half + kk
                    for t in range(T):
                        mm = nc.tensor.matmul(psum[:, b, kk * P:(kk + 1) * P], src[:, t, k * P:(k + 1) * P],
                                              pick[:, t, :], start=(t == 0), stop=(t == 1), skip_group_check=True)
                mm.then_inc(m.gathered, 1)

        def x_copy(eng, layer, gi, part, half):
            n = [i for i, (_, p_, h_) in enumerate(GATHER) if (p_, h_) == (part, half)][0]
            eng.wait_ge(m.gathered, 4 * pass_no(layer, gi) + n + 1)
            src = bank(GATHER[n][0]).rearrange("p (k s) -> p k s", k=4)
            ks = slice(4 * half, 4 * half + 4)
            if part == "hi":
                nc.scalar.copy(x_hi[:, ks, :], src).then_inc(m.x_hi_ready, 1)
            else:
                nc.vector.tensor_copy(x_lo[:, ks, :], src).then_inc(m.x_lo_ready, 1)

        def pickT_pe(pe, layer, gi):
            for t in range(T):
                mm = nc.tensor.transpose(psum[:, 4, S + t * P:S + (t + 1) * P], pick[:, t, :].bitcast(F32), ident)
            mm.then_inc(m.pickT_turned, 1)
            if isinstance(gi, int) and gi == 0:
                pe.wait_ge(m.comb_ready, layer + 1)
                pe.wait_ge(m.x_hi_ready, 2 * pass_no(layer, 0) + 2)
            else:
                pe.wait_ge(m.h_added, 4 * group_no(layer, gi) - 2)
            for t in range(T):
                mm = nc.tensor.matmul(psum[:, 7, 0:8], pick[:, t, :].bitcast(F32), comb[:, t, :], start=(t == 0),
                                      stop=(t == 1), skip_group_check=True)
            mm.then_inc(m.cg_done, 1)

        def pickT_act(act, layer, gi):
            act.wait_ge(m.pickT_turned, pass_no(layer, gi) + 1)
            nc.scalar.copy(pickT[:], psum[:, 4, S:2 * S]).then_inc(m.pickT_ready, 1)

        def cg_dve(dve, layer, gi):
            dve.wait_ge(m.cg_done, pass_no(layer, gi) + 1)
            nc.vector.tensor_copy(cg, psum[:, 7, 0:8]).then_inc(m.cg_ready, 1)

        def gate_up_pe(pe, layer, g, e, half):
            c = MOE_C0[layer] + gu_at(e, half)
            pe.wait_ge(lo_done, c + 1 + g * PER_GROUP)
            for kk in range(4):
                k = 4 * half + kk
                mm = three(bank(e % 2), x_hi[:, k, :], x_lo[:, k, :], c, slice(kk * W4, (kk + 1) * W4),
                           k == 0, k == KD - 1)
            mm.then_inc(w_used, 1)

        def gate_act(act, layer, g, e):
            act.wait_ge(w_used, MOE_C0[layer] + gu_at(e, 1) + 1 + g * PER_GROUP)
            nc.scalar.activation(gate[:], psum[:, e % 2, 0:FF], ACT.Silu).then_inc(m.gate_ready, 1)

        def hid_dve(dve, layer, g, e):
            dve.wait_ge(m.gate_ready, group_no(layer, g) * EXPERTS + e + 1)
            if e == 0:
                dve.wait_ge(m.cg_ready, pass_no(layer, g) + 1)
            nc.vector.scalar_tensor_tensor(hid[:], psum[:, e % 2, FF:2 * FF], cg[:, e:e + 1], gate[:], ALU.mult,
                                           ALU.mult).then_inc(m.hid_ready, 1)

        def turn_hid(pe, layer, g, e):
            pe.wait_ge(m.hid_ready, group_no(layer, g) * EXPERTS + e + 1)
            if e == 0:
                pe.wait_ge(m.pickT_ready, pass_no(layer, g) + 1)
            for j in range(2):
                mm = nc.tensor.transpose(psum[:, 4, j * P:(j + 1) * P], hid[:, j * P:(j + 1) * P], ident)
            mm.then_inc(m.hid_turned, 1)

        def hidT_act(act, layer, g, e):
            act.wait_ge(m.hid_turned, group_no(layer, g) * EXPERTS + e + 1)
            nc.scalar.copy(hidT_hi[:, e % 2], psum[:, 4, 0:2 * P].rearrange("p (j s) -> p j s", j=2)
                           ).then_inc(m.hidT_hi_ready, 1)

        def hidT_dve(dve, layer, g, e):
            dve.wait_ge(m.hidT_hi_ready, group_no(layer, g) * EXPERTS + e + 1)
            nc.vector.tensor_tensor(hidT_lo[:, e % 2], psum[:, 4, 0:2 * P].rearrange("p (j s) -> p j s", j=2),
                                    hidT_hi[:, e % 2].bitcast(F32), ALU.subtract).then_inc(m.hidT_lo_ready, 1)

        def down_pe(pe, layer, g, e, blocks=(0, 1)):
            c = MOE_C0[layer] + down_at(e)
            if blocks[0] == 0:
                pe.wait_ge(lo_done, c + 1 + g * PER_GROUP)
                pe.wait_ge(m.hidT_lo_ready, group_no(layer, g) * EXPERTS + e + 1)
            for n in blocks:
                for j in range(2):
                    mm = three(bank(2 + n), hidT_hi[:, e % 2, j, :], hidT_lo[:, e % 2, j, :], c,
                               slice(j * D + n * W4, j * D + (n + 1) * W4), e == 0 and j == 0,
                               e == EXPERTS - 1 and j == 1)
            if blocks[-1] == 1:
                mm.then_inc(w_used, 1)

        SCATTER = ((0, 0, 6), (0, 1, 7), (1, 0, 5), (1, 1, 6))

        def scatter_pe(pe, layer, g):
            pe.wait_ge(m.y_lo_ready, 2 * group_no(layer, g) + 2)
            pe.wait_ge(m.x_lo_ready, 2 * pass_no(layer, g) + 4)
            pe.wait_ge(m.x_hi_ready, 2 * pass_no(layer, g) + 4)
            for n, (t, blk, b) in enumerate(SCATTER):
                if n == 3:
                    pe.wait_ge(m.h_added, 4 * group_no(layer, g) + 1)
                cols = slice(blk * W4, (blk + 1) * W4)
                nc.tensor.matmul(bank(b), pickT[:, t * P:(t + 1) * P], y_hi[:, cols], start=True, stop=False)
                nc.tensor.matmul(bank(b), pickT[:, t * P:(t + 1) * P], y_lo[:, cols], start=False, stop=True
                                 ).then_inc(m.scattered, 1)

        def y_act(act, layer, g, n):
            act.wait_ge(w_used, MOE_C0[layer] + PER_GROUP + g * PER_GROUP)
            nc.scalar.copy(y_hi[:, n * W4:(n + 1) * W4], bank(2 + n)).then_inc(m.y_hi_ready, 1)

        def y_dve(dve, layer, g, n):
            cols = slice(n * W4, (n + 1) * W4)
            dve.wait_ge(m.y_hi_ready, 2 * group_no(layer, g) + n + 1)
            nc.vector.tensor_tensor(y_lo[:, cols], bank(2 + n), y_hi[:, cols].bitcast(F32), ALU.subtract
                                    ).then_inc(m.y_lo_ready, 1)

        def h_dve(dve, layer, g):
            for n, (t, blk, b) in enumerate(SCATTER):
                dve.wait_ge(m.scattered, 4 * group_no(layer, g) + n + 1)
                cols = slice(blk * W4, (blk + 1) * W4)
                nc.vector.tensor_tensor(h[:, t, cols], bank(b), h[:, t, cols], ALU.add).then_inc(m.h_added, 1)

        LASTE = EXPERTS - 1

        def group_pe(pe, layer, g, more):
            pe.wait_ge(m.x_hi_ready, 2 * pass_no(layer, g) + 2)
            pe.wait_ge(m.x_lo_ready, 2 * pass_no(layer, g) + 2)
            for e in range(EXPERTS):
                gate_up_pe(pe, layer, g, e, 0)
                if e > 0:
                    turn_hid(pe, layer, g, e - 1)
                gate_up_pe(pe, layer, g, e, 1)
                if 0 < e < LASTE:
                    down_pe(pe, layer, g, e - 1)
            down_pe(pe, layer, g, LASTE - 1, (0,))
            turn_hid(pe, layer, g, LASTE)
            down_pe(pe, layer, g, LASTE - 1, (1,))
            down_pe(pe, layer, g, LASTE)
            gather_pe(pe, layer, g + 1)
            scatter_pe(pe, layer, g)
            pickT_pe(pe, layer, g + 1)

        def group_steps(eng, layer, g, more, silu, turned, split):
            for i in range(PER_GROUP):
                for e in range(EXPERTS):
                    if i == gu_at(e, 1) + 1:
                        silu(eng, layer, g, e)
                    if e < LASTE and i == gu_at(e + 1, 1):
                        turned(eng, layer, g, e)
                if more or i + AHEAD < PER_GROUP:
                    split(eng, MOE_C0[layer] + i + AHEAD, g)
                if i == down_at(LASTE - 1):
                    turned(eng, layer, g, LASTE)

        def group_act(act, layer, g, more):
            group_steps(act, layer, g, more, gate_act, hidT_act, split_hi)
            y_act(act, layer, g, 0)
            y_act(act, layer, g, 1)
            x_copy(act, layer, g + 1, "hi", 0)
            x_copy(act, layer, g + 1, "hi", 1)
            pickT_act(act, layer, g + 1)

        def group_dve(dve, layer, g, more):
            pick_dve(dve, layer, g + 1)
            group_steps(dve, layer, g, more, hid_dve, hidT_dve, split_lo)
            y_dve(dve, layer, g, 0)
            y_dve(dve, layer, g, 1)
            x_copy(dve, layer, g + 1, "lo", 0)
            x_copy(dve, layer, g + 1, "lo", 1)
            h_dve(dve, layer, g)
            cg_dve(dve, layer, g + 1)

        def groups(eng, layer, body):
            looped = GROUPS if layer == 0 else GROUPS - 1
            with eng.Fori(0, looped) as g:
                body(eng, layer, g, True)
            if looped < GROUPS:
                body(eng, layer, GROUPS - 1, False)

        SPILL_SLOT = [(MOE_CHUNKS + MOE0 + AHEAD + n) % RAW for n in range(3)]

        def spill_flag(eng, layer):
            eng.wait_ge(m.spill_ready, layer + 1)
            return eng.value_load(spill[0:1, 0:1], min_val=0, max_val=GROUPS)

        def spill_sp(sp, layer):
            flag = spill_flag(sp, layer)
            spl = spill_sems[layer]
            full = sp.value_load(spill[0:1, 1:2], min_val=0, max_val=GROUPS - 1)
            with sp.If(flag > 0):
                sp.wait_ge(lo_done, MOE_C0[layer] + MOE_CHUNKS)
                for e in range(EXPERTS):
                    if e:
                        sp.wait_ge(spl.used, e)
                    for n, at_ in enumerate((gu_at(e, 0), gu_at(e, 1), down_at(e))):
                        index = full * PER_GROUP + (MOE_C0[layer] + at_)
                        sp.dma_start(raw[:, SPILL_SLOT[n], :], stream[bass.ds(index, 1)].rearrange("a p n -> (a p) n")
                                     ).then_inc(spl.landed, 16)
                sp.wait_ge(spl.h_added, 4)
            with sp.Else():
                pass

        def spill_pe(pe, layer):
            flag = spill_flag(pe, layer)
            spl = spill_sems[layer]
            with pe.If(flag > 0):
                pe.wait_ge(m.x_hi_ready, 2 * pass_no(layer, GROUPS) + 2)
                pe.wait_ge(m.x_lo_ready, 2 * pass_no(layer, GROUPS) + 2)
                pe.wait_ge(m.pickT_ready, pass_no(layer, GROUPS) + 1)
                pe.wait_ge(m.h_added, 4 * GROUPS * (layer + 1))
                for e in range(EXPERTS):
                    pe.wait_ge(spl.landed, 48 * (e + 1))
                    for k in range(KD):
                        rhs = raw[:, SPILL_SLOT[k // 4], (k % 4) * W4:(k % 4 + 1) * W4]
                        nc.tensor.matmul(bank(0), x_hi[:, k, :].bitcast(F32), rhs, start=(k == 0), stop=False)
                        mm = nc.tensor.matmul(bank(0), x_lo[:, k, :].bitcast(F32), rhs, start=False, stop=(k == KD - 1))
                    mm.then_inc(spl.gu_done, 1)
                    pe.wait_ge(spl.hid_ready, e + 1)
                    for j in range(2):
                        mm = nc.tensor.transpose(psum[:, 4, j * P:(j + 1) * P], hid[:, j * P:(j + 1) * P], ident)
                    mm.then_inc(spl.hid_turned, 1)
                    pe.wait_ge(spl.hidT_lo_ready, e + 1)
                    for n in range(2):
                        for j in range(2):
                            rhs = raw[:, SPILL_SLOT[2], j * D + n * W4:j * D + (n + 1) * W4]
                            nc.tensor.matmul(bank(2 + n), hidT_hi[:, 0, j, :].bitcast(F32), rhs,
                                             start=(e == 0 and j == 0), stop=False)
                            mm = nc.tensor.matmul(bank(2 + n), hidT_lo[:, 0, j, :].bitcast(F32), rhs, start=False,
                                                  stop=(e == LASTE and j == 1))
                    mm.then_inc(spl.used, 1)
                pe.wait_ge(spl.y_lo_ready, 2)
                for n, (t, blk, b) in enumerate(SCATTER):
                    cols = slice(blk * W4, (blk + 1) * W4)
                    if n == 3:
                        pe.wait_ge(spl.h_added, 1)
                    nc.tensor.matmul(bank(b), pickT[:, t * P:(t + 1) * P], y_hi[:, cols], start=True, stop=False)
                    nc.tensor.matmul(bank(b), pickT[:, t * P:(t + 1) * P], y_lo[:, cols], start=False, stop=True
                                     ).then_inc(spl.scattered, 1)
                pe.wait_ge(spl.h_added, 4)
            with pe.Else():
                pass

        def spill_act(act, layer):
            flag = spill_flag(act, layer)
            spl = spill_sems[layer]
            with act.If(flag > 0):
                for e in range(EXPERTS):
                    act.wait_ge(spl.gu_done, e + 1)
                    nc.scalar.activation(gate[:], psum[:, 0, 0:FF], ACT.Silu).then_inc(spl.gate_ready, 1)
                    act.wait_ge(spl.hid_turned, e + 1)
                    if e:
                        act.wait_ge(spl.used, e)
                    nc.scalar.copy(hidT_hi[:, 0], psum[:, 4, 0:2 * P].rearrange("p (j s) -> p j s", j=2)
                                   ).then_inc(spl.hidT_hi_ready, 1)
                act.wait_ge(spl.used, EXPERTS)
                for n in range(2):
                    nc.scalar.copy(y_hi[:, n * W4:(n + 1) * W4], bank(2 + n)).then_inc(spl.y_hi_ready, 1)
                act.wait_ge(spl.h_added, 4)
            with act.Else():
                pass

        def spill_dve(dve, layer):
            flag = spill_flag(dve, layer)
            spl = spill_sems[layer]
            with dve.If(flag > 0):
                dve.wait_ge(m.cg_ready, pass_no(layer, GROUPS) + 1)
                for e in range(EXPERTS):
                    dve.wait_ge(spl.gate_ready, e + 1)
                    nc.vector.scalar_tensor_tensor(hid[:], psum[:, 0, FF:2 * FF], cg[:, e:e + 1], gate[:], ALU.mult,
                                                   ALU.mult).then_inc(spl.hid_ready, 1)
                    dve.wait_ge(spl.hidT_hi_ready, e + 1)
                    nc.vector.tensor_tensor(hidT_lo[:, 0], psum[:, 4, 0:2 * P].rearrange("p (j s) -> p j s", j=2),
                                            hidT_hi[:, 0].bitcast(F32), ALU.subtract).then_inc(spl.hidT_lo_ready, 1)
                for n in range(2):
                    cols = slice(n * W4, (n + 1) * W4)
                    dve.wait_ge(spl.y_hi_ready, n + 1)
                    nc.vector.tensor_tensor(y_lo[:, cols], bank(2 + n), y_hi[:, cols].bitcast(F32), ALU.subtract
                                            ).then_inc(spl.y_lo_ready, 1)
                dve.wait_ge(m.h_added, 4 * GROUPS * (layer + 1))
                for n, (t, blk, b) in enumerate(SCATTER):
                    dve.wait_ge(spl.scattered, n + 1)
                    cols = slice(blk * W4, (blk + 1) * W4)
                    nc.vector.tensor_tensor(h[:, t, cols], bank(b), h[:, t, cols], ALU.add).then_inc(spl.h_added, 1)
                dve.wait_ge(spl.h_added, 4)
            with dve.Else():
                pass

        block = ctx.enter_context(nc.Block())

        @block.sync
        def _(sp):
            sp.dma_start(h[:], x.rearrange("a (t p) d -> p (a t) d", p=P)).then_inc(x_landed, 16)
            for c in range(RAW):
                load_chunk(sp, (c, c))
            with sp.Fori(1, PROJ1 // RAW) as turn:
                for i in range(RAW):
                    load_chunk(sp, (i, turn * RAW + i), turn * RAW + (i - RAW + 1))
            for c in range(PROJ1, PROJ1 + AHEAD):
                load_chunk(sp, (c % RAW, c), c - RAW + 1)
            spill_sp(sp, 0)
            for c in range(PROJ1 + AHEAD, PROJ1 + RAW):
                load_chunk(sp, (c % RAW, c), c - RAW + 1)
            with sp.Fori(PROJ1 // RAW + 1, CHUNKS // RAW) as turn:
                for i in range(RAW):
                    load_chunk(sp, (i, turn * RAW + i), turn * RAW + (i - RAW + 1))
            for c in range(CHUNKS // RAW * RAW, CHUNKS):
                load_chunk(sp, (c % RAW, c), c - RAW + 1)
            spill_sp(sp, 1)
            sp.wait_ge(m.h_added, 2 * 4 * GROUPS)
            sp.dma_start(out.rearrange("a (t p) d -> p (a t) d", p=P), h[:]).then_inc(out_written, 16)
            sp.wait_ge(out_written, 16)

        @block.gpsimd
        def _(pool):
            even_pool_loads(pool)
            moe_pool_loads(pool, 0)
            odd_pool_loads(pool)
            moe_pool_loads(pool, 1)

        @block.tensor
        def _(pe):
            even_pe(pe)
            for layer in range(2):
                if layer:
                    odd_pe(pe)
                route_pe(pe, layer)
                pe.wait_ge(m.hn_lo_ready, layer + 1)
                gather_pe(pe, layer, 0)
                pickT_pe(pe, layer, 0)
                groups(pe, layer, group_pe)
                spill_pe(pe, layer)

        @block.scalar
        def _(act):
            even_act(act)
            for layer in range(2):
                if layer:
                    odd_act(act)
                route_act(act, layer, (res_added[layer], 4))
                x_copy(act, layer, 0, "hi", 0)
                x_copy(act, layer, 0, "hi", 1)
                pickT_act(act, layer, 0)
                groups(act, layer, group_act)
                spill_act(act, layer)

        @block.vector
        def _(dve):
            even_dve(dve)
            for layer in range(2):
                if layer:
                    odd_dve(dve)
                route_dve(dve, layer)
                x_copy(dve, layer, 0, "lo", 0)
                x_copy(dve, layer, 0, "lo", 1)
                cg_dve(dve, layer, 0)
                groups(dve, layer, group_dve)
                spill_dve(dve, layer)


def shape_constants():
    r = np.arange(P)
    c = np.zeros((P, C_N), np.float32)
    c[:, C_ID:C_ID + P] = np.eye(P)
    c[:, C_NTRI:C_NTRI + P] = -(r[:, None] >= r[None, :]).astype(np.float32)
    c[:, C_NONE:C_NONE + P] = -1
    c[:, C_LT:C_LT + P] = r[:, None] < r[None, :]
    c[:, C_IOTA:C_IOTA + P] = r[None, :]
    c[:, C_EPS] = EPS
    return c


def band_constants():
    s, t = np.arange(S)[:, None], np.arange(S)[None, :]
    full = np.stack([((s <= t) & (s > t - w)) / np.minimum(t + 1, w) - (s == t) for w in WINDOWS], 1)
    full = full.astype(np.float32)
    return full[:P], full[P:, :, P:]


_INS = ["x", "stream", "gains", "consts", "even_pool", "even_bias", "even_cols", "odd_sgu", "odd_vgain", "routers"]


def laid_out(a):
    def tiles(w):
        n = w.shape[1] // W4
        return w.reshape(2, 4, P, n, W4).transpose(3, 0, 2, 1, 4).reshape(n, 2, P, CH)

    stream = np.empty((CHUNKS, P, CH), np.float32)

    def mixer(c0, w_in, order, names, w_out):
        t = tiles(w_in)
        for nb, name in enumerate(order):
            stream[c0 + 2 * nb:c0 + 2 * nb + 2] = t[names.index(name)]
        c1 = c0 + 2 * len(order)
        stream[c1:c1 + 4] = tiles(w_out).reshape(4, P, CH)

    mixer(PROJ0, a["w_in_even"][0], EVEN_BLOCKS, ("q", "k", "v", "p"), a["w_out_even"][0])
    mixer(PROJ1, a["w_in_odd"][0], ODD_BLOCKS, ("u", "vv", "q", "k", "v"), a["w_out_odd"][0])
    for layer, c0 in enumerate((MOE0, MOE1)):
        moe = stream[c0:c0 + MOE_CHUNKS].reshape(GROUPS, PER_GROUP, P, CH)
        for e in range(EXPERTS):
            for half in range(2):
                dst = moe[:, gu_at(e, half)].reshape(GROUPS, P, 4, 2, FF)
                for n, name in enumerate(("w_exp_gate", "w_exp_up")):
                    src = a[name][layer, :, e, half * 512:(half + 1) * 512, :]
                    dst[:, :, :, n, :] = src.reshape(GROUPS, 4, P, FF).transpose(0, 2, 1, 3)
            moe[:, down_at(e)].reshape(GROUPS, P, 2, D)[:] = (
                a["w_exp_down"][layer, :, e].reshape(GROUPS, 2, P, D).transpose(0, 2, 1, 3))

    order = [0, 2, 4, 6, 1, 3, 5, 7]
    q, k = np.arange(S)[:, None], np.arange(S)[None, :]
    bias = a["att_rel_bias"][0][:, np.clip(q - k, -128, 128) + 128][order]
    even_bias = np.concatenate([bias[:, :P, :P].transpose(1, 0, 2).reshape(P, -1),
                                bias[:, P:, :].transpose(1, 0, 2).reshape(P, -1)], 1)
    band0, band1 = band_constants()
    return {
        "x": a["x"],
        "stream": stream,
        "gains": np.stack([a["mix_norm_even"][0], a["ffn_norm"][0], a["mix_norm_odd"][0], a["ffn_norm"][1]]),
        "consts": shape_constants(),
        "even_pool": np.concatenate([band0, band1, a["pool_w"][0].transpose(1, 0, 2)], 2),
        "even_bias": even_bias,
        "even_cols": np.concatenate([np.tile(a["att_q_norm"][0], 2)[:, None], np.tile(a["att_k_norm"][0], 2)[:, None],
                                     a["pool_scale"][0].reshape(4, P).T], 1),
        "odd_sgu": np.concatenate([a["sgu_w"][0].transpose(2, 0, 1).reshape(P, 4 * P), a["sgu_b"][0].T], 1),
        "odd_vgain": a["sgu_v_norm"][0],
        "routers": np.concatenate([a["w_router_group"], a["w_router_expert"]], 2).reshape(2, KD, P, 36)
                   .transpose(0, 2, 1, 3),
    }


def kernel(**inputs):
    import concourse.bacc as _bacc
    from concourse.bass_utils import run_bass_kernel_spmd as _run

    nc = _bacc.Bacc("TRN2", target_bir_lowering=False, num_devices=1)
    data = laid_out({k: np.asarray(v) for k, v in inputs.items()})
    arrays, args = {}, []
    for name in _INS:
        arrays[name] = np.ascontiguousarray(data[name])
        args.append(nc.dram_tensor(name, arrays[name].shape, F32, kind="ExternalInput").ap())
    out = nc.dram_tensor("out", (1, S, D), F32, kind="ExternalOutput").ap()
    hybrid_kernel(nc, *args, out)
    r = _run(nc, [arrays], core_ids=[0])
    return r.results[0]["out"]
```

```python
from collections import namedtuple
from contextlib import ExitStack

import concourse.bass as bass
from concourse import mybir
import numpy as np

F32 = mybir.dt.float32
F32R = mybir.dt.float32r
I32 = mybir.dt.int32
U32 = mybir.dt.uint32
ALU = mybir.AluOpType
ACT = mybir.ActivationFunctionType
AX = mybir.AxisListType

P = 128
S = 256
T = S // P
D = 1024
KD = D // P
HEADS, DH = 8, 64
PAIRS = HEADS // 2
W4 = 512
EPS = 1e-6
WINDOWS = (2, 4, 8, 16)
GROUPS, EXPERTS, FF = 4, 8, 256
NEG = -1e30

CH = 2048
RAW = 12
SPLIT = 3
AHEAD = SPLIT - 1
EVEN_BLOCKS = ("p", "q", "k", "v")
ODD_BLOCKS = ("vv", "u", "q", "k", "v")
PER_GROUP = 3 * EXPERTS
MOE_CHUNKS = GROUPS * PER_GROUP
PROJ0, OUT0 = 0, 2 * len(EVEN_BLOCKS)
MOE0 = OUT0 + 4
PROJ1 = MOE0 + MOE_CHUNKS
OUT1 = PROJ1 + 2 * len(ODD_BLOCKS)
MOE1 = OUT1 + 4
CHUNKS = MOE1 + MOE_CHUNKS


def gu_at(e, half):
    return half if e == 0 else 3 * e - 1 + half


def down_at(e):
    return 3 * e + 4 if e < EXPERTS - 1 else PER_GROUP - 1


C_ID, C_NTRI, C_NONE, C_LT, C_IOTA, C_EPS, C_REV = 0, 128, 256, 384, 512, 640, 641
C_N = 645


def hybrid_kernel(nc, x, stream, gains, consts, even_pool, even_bias, even_cols, odd_sgu, odd_vgain,
                  routers, out):
    ctx = ExitStack()
    with ctx:
        def sem(name):
            return ctx.enter_context(nc.semaphore(name))

        def sems(tag, *names):
            return namedtuple(tag, names)(*[sem(f"{tag}_{n}") for n in names])

        base = -(-nc.sbuf_base // 32) * 32
        taken = [base]

        def fixed(name, shape, dt=F32):
            t = nc.alloc_sbuf_tensor_at(name, shape, dt, offset=taken[0])
            taken[0] += -(-4 * int(np.prod(shape[1:])) // 32) * 32
            return t

        raw = fixed("raw", [P, RAW, CH])
        whi = fixed("whi", [P, SPLIT, CH], F32R)
        wlo = fixed("wlo", [P, SPLIT, CH], F32R)
        h = fixed("h", [P, T, D])
        gain = fixed("gain", [P, D])
        cst = fixed("cst", [P, C_N])
        stat = fixed("stat", [P, 176])
        arena = taken[0]

        def at(name, shape, kib, dt=F32):
            return nc.alloc_sbuf_tensor_at(name, shape, dt, offset=arena + int(kib * 1024))

        ident = cst[:, C_ID:C_ID + P]
        negtri = cst[:, C_NTRI:C_NTRI + P]
        negones = cst[:, C_NONE:C_NONE + P]
        before = cst[:, C_LT:C_LT + P]
        iota = cst[:, C_IOTA:C_IOTA + P]
        eps = cst[:, C_EPS:C_EPS + 1]
        falling = cst[:, C_REV:C_REV + GROUPS]

        psum = ctx.enter_context(nc.psum_tensor("psum", [P, 8, W4], F32))

        def bank(b, n=W4):
            return psum[:, b, 0:n]

        raw_landed = [sem(f"raw_landed{i}") for i in range(RAW)]
        hi_done, lo_done, w_used = sem("hi_done"), sem("lo_done"), sem("w_used")
        x_landed, cst_landed, gain_landed, out_written = (
            sem("x_landed"), sem("cst_landed"), sem("gain_landed"), sem("out_written"))

        def load_chunk(sp, c, wait=None):
            slot, index = c
            if wait is not None:
                sp.wait_ge(lo_done, wait)
            sp.dma_start(raw[:, slot, :], stream[bass.ds(index, 1)].rearrange("a p n -> (a p) n")
                         ).then_inc(raw_landed[slot], 16)

        def split_hi(act, c, g=0):
            act.wait_ge(raw_landed[c % RAW], 16 * (c // RAW + 1) + g * (16 * PER_GROUP // RAW))
            if c >= SPLIT:
                act.wait_ge(w_used, c - SPLIT + 1 + g * PER_GROUP)
            nc.scalar.copy(whi[:, c % SPLIT, :], raw[:, c % RAW, :]).then_inc(hi_done, 1)

        def split_lo(dve, c, g=0):
            dve.wait_ge(hi_done, c + 1 + g * PER_GROUP)
            nc.vector.tensor_tensor(wlo[:, c % SPLIT, :], raw[:, c % RAW, :],
                                    whi[:, c % SPLIT, :].bitcast(F32), ALU.subtract).then_inc(lo_done, 1)

        def three(out_ap, hi, lo, c, cols, first, last):
            nc.tensor.matmul(out_ap, hi, whi[:, c % SPLIT, cols], start=first, stop=False)
            nc.tensor.matmul(out_ap, lo, whi[:, c % SPLIT, cols], start=False, stop=False)
            return nc.tensor.matmul(out_ap, hi, wlo[:, c % SPLIT, cols], start=False, stop=last)

        dve_chain, dve_count = sem("dve_chain"), [0]

        def link(ins):
            dve_count[0] += 1
            ins.then_inc(dve_chain, 1)
            nc.vector.wait_ge(dve_chain, dve_count[0])

        ssq, ss, rms, rstd = stat[:, 0:4], stat[:, 4:6], stat[:, 6:8], stat[:, 160:162]
        squared = at("squared", [P, W4], 46)
        norm = sems("norm", "ssq_ready", "ss_ready", "rms_ready", "rstd_ready", "hg_ready", "turned", "hi_ready",
                    "lo_ready")

        def cols_of(nb):
            return slice(nb * W4, (nb + 1) * W4)

        def square_act(act, ph, nb, h_sem, h_before):
            for t in range(T):
                n = 2 * nb + t
                act.wait_ge(h_sem, h_before + n + 1 if ph else h_before + 16)
                if ph or n:
                    act.wait_ge(norm.ssq_ready, 4 * ph + n)
                nc.scalar.activation(squared[:], h[:, t, cols_of(nb)], ACT.Square, accum_out=ssq[:, n:n + 1]
                                     ).then_inc(norm.ssq_ready, 1)

        def rms_act(act, ph):
            act.wait_ge(norm.ss_ready, ph + 1)
            if ph == 0:
                act.wait_ge(cst_landed, 16)
            nc.scalar.activation(rms, ss, ACT.Sqrt, bias=eps, scale=1.0 / D).then_inc(norm.rms_ready, 1)

        def rstd_dve(dve, ph):
            dve.wait_ge(norm.ssq_ready, 4 * (ph + 1))
            nc.vector.tensor_tensor(ss, ssq[:, 0:2], ssq[:, 2:4], ALU.add).then_inc(norm.ss_ready, 1)
            dve.wait_ge(norm.rms_ready, ph + 1)
            nc.vector.reciprocal(rstd, rms).then_inc(norm.rstd_ready, 1)

        def hg_dve(dve, ph, nb, hg, h_sem=None, h_before=0):
            if h_sem is not None:
                dve.wait_ge(h_sem, h_before + 2 * nb + 2)
            if nb == 0:
                dve.wait_ge(gain_landed, 16 * (ph + 1))
            for t in range(T):
                nc.vector.tensor_tensor(hg[:, t, cols_of(nb)], h[:, t, cols_of(nb)], gain[:, cols_of(nb)], ALU.mult
                                        ).then_inc(norm.hg_ready, 1)

        def turn_pe(pe, ph, hg):
            for b in range(4):
                if b % 2 == 0:
                    pe.wait_ge(norm.hg_ready, 4 * ph + b + 2)
                for j in range(2):
                    for t in range(T):
                        k = 2 * b + j
                        mm = nc.tensor.transpose(psum[:, 4 + b, j * S + t * P:j * S + (t + 1) * P],
                                                 hg[:, t, k * P:(k + 1) * P], ident)
                mm.then_inc(norm.turned, 1)

        def turned_hi(act, ph, hi):
            for b in range(4):
                act.wait_ge(norm.turned, 4 * ph + b + 1)
                nc.scalar.copy(hi[:, 2 * b:2 * b + 2, :], bank(4 + b).rearrange("p (j s) -> p j s", j=2)
                               ).then_inc(norm.hi_ready, 1)

        def turned_lo(dve, ph, hi, lo):
            for b in range(4):
                dve.wait_ge(norm.hi_ready, 4 * (ph // 2) + b + 1)
                nc.vector.tensor_tensor(lo[:, 2 * b:2 * b + 2, :], bank(4 + b).rearrange("p (j s) -> p j s", j=2),
                                        hi[:, 2 * b:2 * b + 2, :].bitcast(F32), ALU.subtract
                                        ).then_inc(norm.lo_ready, 1)

        proj_out = [sem("proj_out0"), sem("proj_out1")]

        def project(pe, ph, layer, hi, lo, c0, nb):
            for kh in range(2):
                c = c0 + 2 * nb + kh
                if nb == 0:
                    pe.wait_ge(norm.lo_ready, 4 * layer + 2 * kh + 2)
                pe.wait_ge(lo_done, c + 1)
                if nb >= 2 and kh == 0:
                    pe.wait_ge(proj_out[layer], 2 * (nb - 1))
                for t in range(T):
                    for kk in range(4):
                        k = 4 * kh + kk
                        mm = three(bank(2 * (nb % 2) + t), hi[:, k, t * P:(t + 1) * P],
                                   lo[:, k, t * P:(t + 1) * P], c, slice(kk * W4, (kk + 1) * W4),
                                   k == 0, k == KD - 1)
                mm.then_inc(w_used, 1)

        def block_out(act, layer, c0, nb, dst, func=ACT.Copy):
            act.wait_ge(w_used, c0 + 2 * nb + 2)
            if nb == 0:
                act.wait_ge(norm.rstd_ready, 2 * layer + 1)
            for t in range(T):
                nc.scalar.activation(dst[:, t, :], bank(2 * (nb % 2) + t), func, scale=rstd[:, t:t + 1]
                                     ).then_inc(proj_out[layer], 1)

        res_added = [sem("res_added0"), sem("res_added1")]

        def out_project(pe, c0, parts):
            for nb in range(2):
                for kh in range(2):
                    c = c0 + 2 * nb + kh
                    pe.wait_ge(lo_done, c + 1)
                    hi, lo = parts[kh]
                    for t in range(T):
                        for kk in range(4):
                            mm = three(bank(2 * nb + t), hi[:, kk, t * P:(t + 1) * P],
                                       lo[:, kk, t * P:(t + 1) * P], c, slice(kk * W4, (kk + 1) * W4),
                                       kh == 0 and kk == 0, kh == 1 and kk == 3)
                    mm.then_inc(w_used, 1)

        def residual(dve, layer, c0, nb):
            dve.wait_ge(w_used, c0 + 2 * nb + 2)
            for t in range(T):
                cols = slice(nb * W4, (nb + 1) * W4)
                nc.vector.tensor_tensor(h[:, t, cols], bank(2 * nb + t), h[:, t, cols], ALU.add
                                        ).then_inc(res_added[layer], 1)

        hnT_hi0, hnT_lo0 = at("hnT_hi0", [P, KD, S], 0, F32R), at("hnT_lo0", [P, KD, S], 8, F32R)
        qT0, kT0 = at("qT0", [P, PAIRS, S], 0), at("kT0", [P, PAIRS, S], 4)
        mixA_hi, mixA_lo = at("mixA_hi", [P, 4, S], 0, F32R), at("mixA_lo", [P, 4, S], 4, F32R)
        pt0, att = at("pt0", [P, HEADS, P], 8), at("att", [P, T, W4], 12)
        hg0 = at("hg0", [P, T, D], 16)
        p_in, q_in = at("p_in", [P, T, W4], 16), at("q_in", [P, T, W4], 20)
        k_in, v_in = at("k_in", [P, T, W4], 24), at("v_in", [P, T, W4], 28)
        mixP_hi, mixP_lo = at("mixP_hi", [P, 4, S], 16, F32R), at("mixP_lo", [P, 4, S], 32, F32R)
        pt1 = at("pt1", [P, 2, HEADS, P], 20)
        squares = at("squares", [P, T, W4], 32)
        pool_c = at("pool_c", [P, 4, 256 + 128 + 128], 36)
        pooled = at("pooled", [P, 4, S], 44)
        pb = [at("pb0", [P, HEADS, P], 36), at("pb1", [P, HEADS, S], 40)]
        cols0 = stat[:, 8:14]
        hss, hrms, hrs = stat[:, 16:48], stat[:, 48:80], stat[:, 80:112]
        nmax, rsum, rinv = stat[:, 112:128], stat[:, 128:144], stat[:, 144:160]
        ev = sems("even", "pool_c_landed", "cols_landed", "banded", "pooled_ready", "pool_done", "mixP_hi_ready",
                  "mixP_lo_ready", "bias_landed", "bias_masked", "ss_ready", "rms_ready", "qk_ready",
                  "qk_turned", "qT_ready", "scored", "biased", "nmax_ready", "probs_ready", "probs_turned",
                  "pt_act", "pt_dve", "pv_done", "att_ready", "att_turned", "mixA_hi_ready", "mixA_lo_ready")

        def even_pool_loads(pool):
            pool.dma_start(gain[:], gains[0].partition_broadcast(P)).then_inc(gain_landed, 16)
            pool.dma_start(pool_c[:], even_pool).then_inc(ev.pool_c_landed, 16)
            pool.dma_start(cols0, even_cols).then_inc(ev.cols_landed, 16)
            pool.wait_ge(norm.hg_ready, 4)
            pool.dma_start(gain[:], gains[1].partition_broadcast(P)).then_inc(gain_landed, 16)
            pool.wait_ge(ev.pool_done, 2)
            pool.dma_start(pb[0][:], even_bias[:, 0:HEADS * P].rearrange("p (j k) -> p j k", j=HEADS)
                           ).then_inc(ev.bias_landed, 16)
            pool.dma_start(pb[1][:], even_bias[:, HEADS * P:].rearrange("p (j k) -> p j k", j=HEADS)
                           ).then_inc(ev.bias_landed, 16)
            pool.wait_ge(ev.bias_landed, 32)
            nc.gpsimd.memset(pb[0][0:64, :, 64:128], NEG).then_inc(ev.bias_masked, 1)
            nc.gpsimd.memset(pb[1][0:64, :, 192:256], NEG).then_inc(ev.bias_masked, 1)

        def pool_band_pe(pe):
            pe.wait_ge(ev.pool_c_landed, 16)
            pe.wait_ge(proj_out[0], 2)
            for g in range(4):
                dst = psum[:, 4 + g // 2, (g % 2) * S:(g % 2 + 1) * S]
                nc.tensor.matmul(dst, p_in[:, 0, g * P:(g + 1) * P], pool_c[:, g, 0:256],
                                 start=True, stop=False, skip_group_check=True)
                mm = nc.tensor.matmul(dst[:, P:S], p_in[:, 1, g * P:(g + 1) * P], pool_c[:, g, 256:384],
                                      start=False, stop=True, skip_group_check=True)
                if g % 2:
                    mm.then_inc(ev.banded, 1)

        def pool_weight_pe(pe):
            pe.wait_ge(ev.pooled_ready, 2)
            for g in range(4):
                mm = nc.tensor.matmul(psum[:, 6 + g // 2, (g % 2) * S:(g % 2 + 1) * S],
                                      pool_c[:, g, 384:512], pooled[:, g, :], start=True, stop=True,
                                      skip_group_check=True)
                if g % 2:
                    mm.then_inc(ev.pool_done, 1)

        def heads(ap):
            return ap.rearrange("p (h d) -> p h d", d=DH)

        def head_squares(dve, src, i, out_count):
            dve.wait_ge(proj_out[0], out_count)
            link(nc.vector.tensor_tensor(squares[:], src[:], src[:], ALU.mult))
            nc.vector.tensor_reduce(hss[:, 16 * i:16 * i + 16], squares[:].rearrange("p t (h d) -> p (t h) d", d=DH),
                                    AX.X, ALU.add).then_inc(ev.ss_ready, 1)

        def head_rms(act, i):
            act.wait_ge(ev.ss_ready, i + 1)
            nc.scalar.activation(hrms[:, 16 * i:16 * i + 16], hss[:, 16 * i:16 * i + 16], ACT.Sqrt, bias=eps,
                                 scale=1.0 / DH).then_inc(ev.rms_ready, 1)

        def head_norm(dve, src, i):
            dve.wait_ge(ev.rms_ready, i + 1)
            r = hrs[:, 16 * i:16 * i + 16]
            link(nc.vector.reciprocal(r, hrms[:, 16 * i:16 * i + 16]))
            view = src[:].rearrange("p t (h d) -> p (t h) d", d=DH)
            nc.vector.tensor_tensor(view, view, r.unsqueeze(2).to_broadcast([P, 16, DH]), ALU.mult
                                    ).then_inc(ev.qk_ready, 1)

        def turn_pairs(pe, src, b0, signal):
            for t in range(T):
                for j in range(PAIRS):
                    mm = nc.tensor.transpose(psum[:, b0 + t, j * P:(j + 1) * P], src[:, t, j * P:(j + 1) * P], ident)
                mm.then_inc(signal, 1)

        def pairs_view(b):
            return bank(b).rearrange("p (j s) -> p j s", j=PAIRS)

        def scores_pe(pe, t):
            n = (t + 1) * P
            per = W4 // n
            for par in range(2):
                rows = slice(64 * par, 64 * par + 64)
                for i in range(PAIRS):
                    b = (par if t == 0 else 2 + 2 * par + i // per)
                    mm = nc.tensor.matmul(psum[:, b, (i % per) * n:(i % per + 1) * n], qT0[rows, i, t * P:(t + 1) * P],
                                          kT0[rows, i, 0:n], start=True, stop=True, skip_group_check=True)
                    if i % per == per - 1:
                        mm.then_inc(ev.scored, 1)

        def softmax_dve(dve, t):
            n = (t + 1) * P
            per = W4 // n
            banks = [0, 1] if t == 0 else [2, 3, 4, 5]
            for m, b in enumerate(banks):
                dve.wait_ge(ev.scored, (0 if t == 0 else 2) + m + 1)
                view = pb[t][:, m * per:(m + 1) * per, :]
                nc.vector.tensor_tensor(view, bank(b).rearrange("p (j k) -> p j k", k=n), view, ALU.add
                                        ).then_inc(ev.biased, 1)
            dve.wait_ge(ev.biased, 2 if t == 0 else 6)
            nc.vector.tensor_reduce(nmax[:, 8 * t:8 * t + 8], pb[t][:], AX.X, ALU.max, negate=True
                                    ).then_inc(ev.nmax_ready, 1)

        def softmax_act(act, t):
            act.wait_ge(ev.nmax_ready, t + 1)
            for j in range(HEADS):
                nc.scalar.activation(pb[t][:, j, :], pb[t][:, j, :], ACT.Exp, bias=nmax[:, 8 * t + j:8 * t + j + 1],
                                     accum_out=rsum[:, 8 * t + j:8 * t + j + 1]).then_inc(ev.probs_ready, 1)

        def turn_probs(pe, t):
            for kt in range(t + 1):
                for j in range(HEADS):
                    b = 6 + j // 4 if t == 0 else 2 * kt + j // 4
                    if kt == 0:
                        pe.wait_ge(ev.probs_ready, 8 * t + j + 1)
                    mm = nc.tensor.transpose(psum[:, b, (j % 4) * P:(j % 4 + 1) * P],
                                             pb[t][:, j, kt * P:(kt + 1) * P], ident)
                    if j % 4 == 3:
                        mm.then_inc(ev.probs_turned, 1)

        def pt_copy(eng, signal, t, m):
            eng.wait_ge(ev.probs_turned, (0 if t == 0 else 2) + m + 1)
            if t == 0:
                src, dst = 6 + m, pt0[:, 4 * m:4 * m + 4, :]
            else:
                src, dst = m, pt1[:, m // 2, 4 * (m % 2):4 * (m % 2) + 4, :]
            copy = nc.scalar.copy if eng is nc.scalar else nc.vector.tensor_copy
            copy(dst, bank(src).rearrange("p (j s) -> p j s", j=4)).then_inc(signal, 1)

        def pv_pe(pe, t):
            for j in range(HEADS):
                hd = 2 * (j % 4) + j // 4
                for kt in range(t + 1):
                    lhs = pt0[:, j, :] if t == 0 else pt1[:, kt, j, :]
                    mm = nc.tensor.matmul(psum[:, 4 + t, hd * DH:(hd + 1) * DH], lhs, v_in[:, kt, hd * DH:(hd + 1) * DH],
                                          start=(kt == 0), stop=(kt == t), skip_group_check=True)
            mm.then_inc(ev.pv_done, 1)

        def att_dve(dve, t):
            link(nc.vector.reciprocal(rinv[:, 8 * t:8 * t + 8], rsum[:, 8 * t:8 * t + 8]))
            dve.wait_ge(ev.pv_done, t + 1)
            for par in range(2):
                r = rinv[:, 8 * t + 4 * par:8 * t + 4 * par + 4]
                nc.vector.tensor_tensor(att[:, t, :].rearrange("p (i a d) -> p a i d", a=2, d=DH)[:, par],
                                        bank(4 + t).rearrange("p (i a d) -> p a i d", a=2, d=DH)[:, par],
                                        r.unsqueeze(2).to_broadcast([P, 4, DH]), ALU.mult).then_inc(ev.att_ready, 1)

        def even_pe(pe):
            pe.wait_ge(cst_landed, 16)
            turn_pe(pe, 0, hg0)
            project(pe, 0, 0, hnT_hi0, hnT_lo0, PROJ0, 0)
            project(pe, 0, 0, hnT_hi0, hnT_lo0, PROJ0, 1)
            pool_band_pe(pe)
            project(pe, 0, 0, hnT_hi0, hnT_lo0, PROJ0, 2)
            pool_weight_pe(pe)
            project(pe, 0, 0, hnT_hi0, hnT_lo0, PROJ0, 3)
            pe.wait_ge(ev.pooled_ready, 2)
            pe.wait_ge(ev.qk_ready, 1)
            turn_pairs(pe, q_in, 4, ev.qk_turned)
            pe.wait_ge(ev.qk_ready, 2)
            pe.wait_ge(ev.mixP_lo_ready, 2)
            turn_pairs(pe, k_in, 6, ev.qk_turned)
            pe.wait_ge(ev.qT_ready, 4)
            scores_pe(pe, 0)
            pe.wait_ge(proj_out[0], 8)
            scores_pe(pe, 1)
            turn_probs(pe, 0)
            pe.wait_ge(ev.biased, 6)
            pe.wait_ge(ev.pt_act, 1)
            pe.wait_ge(ev.pt_dve, 1)
            pv_pe(pe, 0)
            turn_probs(pe, 1)
            pe.wait_ge(ev.att_ready, 2)
            for j in range(4):
                mm = nc.tensor.transpose(psum[:, 6, j * P:(j + 1) * P], att[:, 0, j * P:(j + 1) * P], ident)
            mm.then_inc(ev.att_turned, 1)
            pe.wait_ge(ev.pt_act, 3)
            pe.wait_ge(ev.pt_dve, 3)
            pv_pe(pe, 1)
            pe.wait_ge(ev.att_ready, 4)
            for j in range(4):
                mm = nc.tensor.transpose(psum[:, 7, j * P:(j + 1) * P], att[:, 1, j * P:(j + 1) * P], ident)
            mm.then_inc(ev.att_turned, 1)
            pe.wait_ge(ev.mixA_lo_ready, 2)
            out_project(pe, OUT0, [(mixA_hi, mixA_lo), (mixP_hi, mixP_lo)])

        def even_act(act):
            square_act(act, 0, 0, x_landed, 0)
            square_act(act, 0, 1, x_landed, 0)
            turned_hi(act, 0, hnT_hi0)
            for c in range(AHEAD):
                split_hi(act, c)
            rms_act(act, 0)
            dst = {"p": p_in, "q": q_in, "k": k_in, "v": v_in}
            for c in range(2 * len(EVEN_BLOCKS)):
                if c % 2 == 0 and c > 0:
                    block_out(act, 0, PROJ0, c // 2 - 1, dst[EVEN_BLOCKS[c // 2 - 1]])
                if c in (5, 7):
                    head_rms(act, (c - 5) // 2)
                if c == 6:
                    act.wait_ge(ev.cols_landed, 16)
                    for b in range(2):
                        act.wait_ge(ev.pool_done, b + 1)
                        for g in (2 * b, 2 * b + 1):
                            nc.scalar.activation(mixP_hi[:, g, :], psum[:, 6 + b, (g % 2) * S:(g % 2 + 1) * S],
                                                 ACT.Copy, scale=cols0[:, 2 + g:3 + g]).then_inc(ev.mixP_hi_ready, 1)
                split_hi(act, PROJ0 + c + AHEAD)
            block_out(act, 0, PROJ0, 3, v_in)
            softmax_act(act, 0)
            softmax_act(act, 1)
            pt_copy(act, ev.pt_act, 0, 0)
            pt_copy(act, ev.pt_act, 1, 0)
            pt_copy(act, ev.pt_act, 1, 2)
            for t in range(T):
                act.wait_ge(ev.att_turned, t + 1)
                nc.scalar.copy(mixA_hi[:, :, t * P:(t + 1) * P], pairs_view(6 + t)).then_inc(ev.mixA_hi_ready, 1)
            for c in range(OUT0, OUT0 + 4):
                if c == OUT0 + 3:
                    square_act(act, 1, 0, res_added[0], 0)
                split_hi(act, c + AHEAD)
            square_act(act, 1, 1, res_added[0], 0)

        def even_dve(dve):
            dve.wait_ge(x_landed, 16)
            hg_dve(dve, 0, 0, hg0)
            hg_dve(dve, 0, 1, hg0)
            turned_lo(dve, 0, hnT_hi0, hnT_lo0)
            for c in range(AHEAD):
                split_lo(dve, c)
            rstd_dve(dve, 0)
            for c in range(2 * len(EVEN_BLOCKS)):
                if c == 4:
                    for b in range(2):
                        dve.wait_ge(ev.banded, b + 1)
                        nc.vector.tensor_copy(pooled[:, 2 * b:2 * b + 2, :],
                                              bank(4 + b).rearrange("p (j s) -> p j s", j=2)
                                              ).then_inc(ev.pooled_ready, 1)
                    head_squares(dve, q_in, 0, 4)
                if c == 5:
                    head_norm(dve, q_in, 0)
                if c == 6:
                    head_squares(dve, k_in, 1, 6)
                    dve.wait_ge(ev.ss_ready, 2)
                    for g in range(4):
                        dve.wait_ge(ev.mixP_hi_ready, 2 * (g // 2) + 2)
                        ins = nc.vector.scalar_tensor_tensor(
                            mixP_lo[:, g, :], psum[:, 6 + g // 2, (g % 2) * S:(g % 2 + 1) * S], cols0[:, 2 + g:3 + g],
                            mixP_hi[:, g, :].bitcast(F32), ALU.mult, ALU.subtract)
                        if g % 2:
                            ins.then_inc(ev.mixP_lo_ready, 1)
                if c == 7:
                    head_norm(dve, k_in, 1)
                split_lo(dve, PROJ0 + c + AHEAD)
            for t in range(T):
                dve.wait_ge(ev.qk_turned, t + 1)
                nc.vector.tensor_scalar(qT0[:, :, t * P:(t + 1) * P], pairs_view(4 + t), cols0[:, 0:1], DH ** -0.5,
                                        ALU.mult, ALU.mult).then_inc(ev.qT_ready, 1)
            for t in range(T):
                dve.wait_ge(ev.qk_turned, t + 3)
                nc.vector.tensor_scalar(kT0[:, :, t * P:(t + 1) * P], pairs_view(6 + t), cols0[:, 1:2], None,
                                        ALU.mult).then_inc(ev.qT_ready, 1)
            dve.wait_ge(ev.bias_masked, 2)
            softmax_dve(dve, 0)
            softmax_dve(dve, 1)
            pt_copy(dve, ev.pt_dve, 0, 1)
            att_dve(dve, 0)
            pt_copy(dve, ev.pt_dve, 1, 1)
            pt_copy(dve, ev.pt_dve, 1, 3)
            att_dve(dve, 1)
            for t in range(T):
                dve.wait_ge(ev.mixA_hi_ready, t + 1)
                nc.vector.tensor_tensor(mixA_lo[:, :, t * P:(t + 1) * P], pairs_view(6 + t),
                                        mixA_hi[:, :, t * P:(t + 1) * P].bitcast(F32), ALU.subtract
                                        ).then_inc(ev.mixA_lo_ready, 1)
            for c in range(OUT0, OUT0 + 4):
                if c == OUT0 + 2:
                    residual(dve, 0, OUT0, 0)
                    hg_dve(dve, 1, 0, hg1, res_added[0])
                split_lo(dve, c + AHEAD)
            residual(dve, 0, OUT0, 1)
            hg_dve(dve, 1, 1, hg1, res_added[0])

        hnT_hi1, hnT_lo1 = at("hnT_hi1", [P, KD, S], 0, F32R), at("hnT_lo1", [P, KD, S], 8, F32R)
        qT1, kT1 = at("qT1", [P, PAIRS, S], 0), at("kT1", [P, PAIRS, S], 4)
        mixD_hi, mixD_lo = at("mixD_hi", [P, 4, S], 0, F32R), at("mixD_lo", [P, 4, S], 4, F32R)
        HALF = 4 * S + 4 * P
        rest = at("rest", [P, HALF], 8)
        hg2 = at("hg2", [P, T, D], 16)
        u_in, vv_in = at("u_in", [P, T, W4], 16), at("vv_in", [P, T, W4], 20)
        mixC_hi, mixC_lo = at("mixC_hi", [P, 4, S], 20, F32R), at("mixC_lo", [P, 4, S], 16, F32R)
        q1_in, k1_in, v1_in = at("q1_in", [P, T, W4], 24), at("k1_in", [P, T, W4], 28), at("v1_in", [P, T, W4], 32)
        stick = at("stick", [P, HALF], 24)
        sgu = at("sgu", [P, 4 * P + 4], 36)
        vgain = at("vgain", [P, W4], 38.25)
        bigid = at("bigid", [P, P], 40.25)
        soft = at("soft", [P, HALF], 41)
        ssv, rmsv, rsv = stat[:, 16:18], stat[:, 18:20], stat[:, 20:22]
        od = sems("odd", "sgu_landed", "vgain_landed", "ssv_ready", "rmsv_ready", "vn_ready", "gated", "yc_ready",
                  "yc_turned", "mixC_hi_ready", "mixC_lo_ready", "qk_turned", "qT_ready", "z_done", "abs_ready",
                  "exp_ready", "ln_ready", "rest_ready", "sum_done", "stick_ready", "av_done", "mixD_hi_ready",
                  "mixD_lo_ready", "big_ready", "tril_ready")

        def odd_pool_loads(pool):
            pool.wait_ge(res_added[0], 4)
            pool.wait_ge(norm.hg_ready, 8)
            pool.dma_start(gain[:], gains[2].partition_broadcast(P)).then_inc(gain_landed, 16)
            pool.wait_ge(norm.hg_ready, 12)
            pool.dma_start(gain[:], gains[3].partition_broadcast(P)).then_inc(gain_landed, 16)
            pool.dma_start(sgu[:], odd_sgu).then_inc(od.sgu_landed, 16)
            pool.dma_start(vgain[:], odd_vgain.partition_broadcast(P)).then_inc(od.vgain_landed, 16)
            pool.wait_ge(od.sgu_landed, 16)
            view = sgu[:, 0:4 * P].rearrange("p (g t) -> p g t", g=4)
            nc.gpsimd.affine_select(out=view, in_=view, pattern=[[0, 4], [1, P]], compare_op=ALU.is_ge, fill=0.0,
                                    base=0, channel_multiplier=-1).then_inc(od.tril_ready, 1)

        def gating_pe(pe):
            pe.wait_ge(od.tril_ready, 1)
            for n in range(T):
                pe.wait_ge(od.vn_ready, n + 1)
                for g in range(4):
                    mm = nc.tensor.matmul(psum[:, 4 + n, g * P:(g + 1) * P], sgu[:, g * P:(g + 1) * P],
                                          vv_in[:, n, g * P:(g + 1) * P], start=True, stop=True, skip_group_check=True)
                mm.then_inc(od.gated, 1)

        def half_parts(view):
            return (view[:, 0:4 * S].rearrange("p (i s) -> p i s", i=4),
                    view[:, 4 * S:HALF].rearrange("p (i s) -> p i s", i=4))

        def half_banks(par):
            return psum[:, 3 * par:3 * par + 3, :].rearrange("p b n -> p (b n)")

        def z_pe(pe, par):
            rows = slice(64 * par, 64 * par + 64)
            z0, z1 = half_parts(half_banks(par))
            for i in range(PAIRS):
                nc.tensor.matmul(z0[:, i, :], kT1[rows, i, 0:P], qT1[rows, i, :], start=(i % 2 == 0), stop=False,
                                 skip_group_check=True)
            for i in range(PAIRS):
                mm = nc.tensor.matmul(z1[:, i, :], kT1[rows, i, P:S], qT1[rows, i, P:S], start=(i == 0), stop=False,
                                      skip_group_check=True)
            mm.then_inc(od.z_done, 1)

        def sum_pe(pe, par):
            z0, z1 = half_parts(half_banks(par))
            r0, r1 = half_parts(rest[:])
            pe.wait_ge(od.rest_ready, 3 * (par + 1))
            for m in range(2):
                hd = slice(2 * m, 2 * m + 2)
                nc.tensor.matmul(z0[:, hd, :], negtri, r0[:, hd, :], start=False, stop=False, skip_group_check=True)
                nc.tensor.matmul(z0[:, hd, P:S], negones, r1[:, hd, :], start=False, stop=False, skip_group_check=True)
            nc.tensor.matmul(z1[:, :, :], negtri, r1[:, :, :], start=False, stop=False, skip_group_check=True)
            if par == 0:
                pe.wait_ge(od.big_ready, 1)
            for i in range(PAIRS):
                nc.tensor.matmul(z0[:, i, 0:P], bigid[:], negtri, start=False, stop=True, skip_group_check=True)
                mm = nc.tensor.matmul(z1[:, i, :], bigid[:], negtri, start=False, stop=True, skip_group_check=True)
            mm.then_inc(od.sum_done, 1)

        def av_pe(pe, par):
            pe.wait_ge(od.stick_ready, par + 1)
            a0, a1 = half_parts(stick[:])
            rows = slice(64 * par, 64 * par + 64)
            for i in range(PAIRS):
                hd = 2 * i + par
                dst = psum[rows, 6 + i // 2, (i % 2) * S:(i % 2 + 1) * S]
                nc.tensor.matmul(dst, v1_in[:, 0, hd * DH:(hd + 1) * DH], a0[:, i, :], start=True, stop=False,
                                 skip_group_check=True)
                mm = nc.tensor.matmul(dst[:, P:S], v1_in[:, 1, hd * DH:(hd + 1) * DH], a1[:, i, :],
                                      start=False, stop=True, skip_group_check=True)
            mm.then_inc(od.av_done, 1)

        def odd_pe(pe):
            turn_pe(pe, 2, hg2)
            for nb in range(3):
                project(pe, 2, 1, hnT_hi1, hnT_lo1, PROJ1, nb)
            gating_pe(pe)
            project(pe, 2, 1, hnT_hi1, hnT_lo1, PROJ1, 3)
            pe.wait_ge(od.yc_ready, 8)
            turn_pairs(pe, u_in, 6, od.yc_turned)
            project(pe, 2, 1, hnT_hi1, hnT_lo1, PROJ1, 4)
            pe.wait_ge(proj_out[1], 8)
            turn_pairs(pe, q1_in, 4, od.qk_turned)
            pe.wait_ge(od.mixC_lo_ready, 2)
            turn_pairs(pe, k1_in, 6, od.qk_turned)
            pe.wait_ge(proj_out[1], 10)
            pe.wait_ge(od.qT_ready, 4)
            z_pe(pe, 0)
            z_pe(pe, 1)
            for par in range(2):
                sum_pe(pe, par)
                av_pe(pe, par)
            pe.wait_ge(od.mixD_lo_ready, 2)
            out_project(pe, OUT1, [(mixC_hi, mixC_lo), (mixD_hi, mixD_lo)])

        def stick_act(act, par):
            z = half_banks(par)
            act.wait_ge(od.z_done, par + 1)
            if par:
                act.wait_ge(od.rest_ready, 3)
            nc.scalar.activation(soft[:], z, ACT.Abs).then_inc(od.abs_ready, 1)
            act.wait_ge(od.abs_ready, par + 1)
            nc.scalar.activation(soft[:], soft[:], ACT.Exp, scale=-1.0).then_inc(od.exp_ready, 1)
            act.wait_ge(od.exp_ready, par + 1)
            nc.scalar.activation(soft[:], soft[:], ACT.Ln, bias=1.0).then_inc(od.ln_ready, 1)

        def stick_dve(dve, par):
            z = half_banks(par)
            r0, r1 = half_parts(rest[:])
            dve.wait_ge(od.ln_ready, par + 1)
            if par:
                dve.wait_ge(od.sum_done, 1)
            nc.vector.scalar_tensor_tensor(rest[:], z, 0.0, soft[:], ALU.max, ALU.add).then_inc(od.rest_ready, 1)
            dve.wait_ge(od.rest_ready, 3 * par + 1)
            mask = before.unsqueeze(1).to_broadcast([P, 4, P])
            nc.vector.tensor_tensor(r0[:, :, 0:P], r0[:, :, 0:P], mask, ALU.mult).then_inc(od.rest_ready, 1)
            nc.vector.tensor_tensor(r1, r1, mask, ALU.mult).then_inc(od.rest_ready, 1)

        def weights_act(act, par):
            act.wait_ge(od.sum_done, par + 1)
            if par:
                act.wait_ge(od.av_done, 1)
            nc.scalar.activation(stick[:], half_banks(par), ACT.Exp).then_inc(od.stick_ready, 1)

        def odd_act(act):
            square_act(act, 2, 0, m.h_added, 4 * GROUPS - 4)
            square_act(act, 2, 1, m.h_added, 4 * GROUPS - 4)
            turned_hi(act, 2, hnT_hi1)
            rms_act(act, 2)
            dst = {"vv": vv_in, "u": u_in, "q": q1_in, "k": k1_in, "v": v1_in}
            for c in range(2 * len(ODD_BLOCKS)):
                if c % 2 == 0 and c > 0:
                    name = ODD_BLOCKS[c // 2 - 1]
                    block_out(act, 1, PROJ1, c // 2 - 1, dst[name], ACT.Gelu if name in ("vv", "u") else ACT.Copy)
                if c == 5:
                    act.wait_ge(od.ssv_ready, 2)
                    nc.scalar.activation(rmsv, ssv, ACT.Sqrt, bias=eps, scale=1.0 / W4).then_inc(od.rmsv_ready, 1)
                if c == 9:
                    for t in range(T):
                        act.wait_ge(od.yc_turned, T)
                        nc.scalar.copy(mixC_hi[:, :, t * P:(t + 1) * P], pairs_view(6 + t)).then_inc(od.mixC_hi_ready, 1)
                split_hi(act, PROJ1 + c + AHEAD)
            block_out(act, 1, PROJ1, 4, v1_in)
            stick_act(act, 0)
            stick_act(act, 1)
            weights_act(act, 0)
            weights_act(act, 1)
            for b in range(2):
                act.wait_ge(od.av_done, 2)
                nc.scalar.copy(mixD_hi[:, 2 * b:2 * b + 2, :], bank(6 + b).rearrange("p (j s) -> p j s", j=2)
                               ).then_inc(od.mixD_hi_ready, 1)
            for c in range(OUT1, OUT1 + 4):
                if c == OUT1 + 3:
                    square_act(act, 3, 0, res_added[1], 0)
                split_hi(act, c + AHEAD)
            square_act(act, 3, 1, res_added[1], 0)

        def odd_dve(dve):
            hg_dve(dve, 2, 0, hg2, m.h_added, 4 * GROUPS - 4)
            hg_dve(dve, 2, 1, hg2, m.h_added, 4 * GROUPS - 4)
            nc.vector.tensor_scalar(bigid[:], ident, -NEG, None, ALU.mult).then_inc(od.big_ready, 1)
            turned_lo(dve, 2, hnT_hi1, hnT_lo1)
            rstd_dve(dve, 2)
            for c in range(2 * len(ODD_BLOCKS)):
                if c == 4:
                    dve.wait_ge(proj_out[1], 2)
                    for t in range(T):
                        nc.vector.tensor_tensor_reduce(soft[:, t * W4:(t + 1) * W4], vv_in[:, t, :], vv_in[:, t, :], 1.0, 0.0,
                                                       ALU.mult, ALU.add, ssv[:, t:t + 1]).then_inc(od.ssv_ready, 1)
                if c == 5:
                    dve.wait_ge(od.rmsv_ready, 1)
                    link(nc.vector.reciprocal(rsv, rmsv))
                    dve.wait_ge(od.vgain_landed, 16)
                    for t in range(T):
                        nc.vector.scalar_tensor_tensor(vv_in[:, t, :], vv_in[:, t, :], rsv[:, t:t + 1], vgain[:],
                                                       ALU.mult, ALU.mult).then_inc(od.vn_ready, 1)
                if c == 7:
                    dve.wait_ge(proj_out[1], 4)
                    for n in range(T):
                        dve.wait_ge(od.gated, n + 1)
                        for g in range(4):
                            cs = slice(g * P, (g + 1) * P)
                            nc.vector.scalar_tensor_tensor(u_in[:, n, cs], psum[:, 4 + n, cs],
                                                           sgu[:, 4 * P + g:4 * P + g + 1], u_in[:, n, cs],
                                                           ALU.add, ALU.mult).then_inc(od.yc_ready, 1)
                if c == 9:
                    for t in range(T):
                        dve.wait_ge(od.mixC_hi_ready, t + 1)
                        nc.vector.tensor_tensor(mixC_lo[:, :, t * P:(t + 1) * P], pairs_view(6 + t),
                                                mixC_hi[:, :, t * P:(t + 1) * P].bitcast(F32), ALU.subtract
                                                ).then_inc(od.mixC_lo_ready, 1)
                split_lo(dve, PROJ1 + c + AHEAD)
            for t in range(T):
                dve.wait_ge(od.qk_turned, t + 1)
                nc.vector.tensor_scalar(qT1[:, :, t * P:(t + 1) * P], pairs_view(4 + t), DH ** -0.5, None,
                                        ALU.mult).then_inc(od.qT_ready, 1)
            for t in range(T):
                dve.wait_ge(od.qk_turned, t + 3)
                nc.vector.tensor_copy(kT1[:, :, t * P:(t + 1) * P], pairs_view(6 + t)).then_inc(od.qT_ready, 1)
            stick_dve(dve, 0)
            stick_dve(dve, 1)
            for b in range(2):
                dve.wait_ge(od.mixD_hi_ready, b + 1)
                nc.vector.tensor_tensor(mixD_lo[:, 2 * b:2 * b + 2, :], bank(6 + b).rearrange("p (j s) -> p j s", j=2),
                                        mixD_hi[:, 2 * b:2 * b + 2, :].bitcast(F32), ALU.subtract
                                        ).then_inc(od.mixD_lo_ready, 1)
            for c in range(OUT1, OUT1 + 4):
                if c == OUT1 + 2:
                    residual(dve, 1, OUT1, 0)
                    hg_dve(dve, 3, 0, hg1, res_added[1])
                split_lo(dve, c + AHEAD)
            residual(dve, 1, OUT1, 1)
            hg_dve(dve, 3, 1, hg1, res_added[1])

        hn_hi, hn_lo = at("hn_hi", [P, T, D], 0, F32R), at("hn_lo", [P, T, D], 8, F32R)
        hgT = at("hgT", [P, KD, S], 16)
        y_hi, y_lo = at("y_hi", [P, D], 16, F32R), at("y_lo", [P, D], 20, F32R)
        hg1 = at("hg1", [P, T, D], 24)
        x_hi, x_lo = at("x_hi", [P, KD, P], 24, F32R), at("x_lo", [P, KD, P], 28, F32R)
        pick, pickT = at("pick", [P, T, P], 32, F32R), at("pickT", [P, S], 33, F32R)
        gate, hid = at("gate", [P, FF], 34), at("hid", [P, FF], 35)
        hidT_hi, hidT_lo = at("hidT_hi", [P, 2, 2, P], 36, F32R), at("hidT_lo", [P, 2, 2, P], 38, F32R)
        rw = at("rw", [P, KD, 36], 40)
        r_small = at("r_small", [P, 512], 41.25)
        top_idx = at("top_idx", [P, T, 8], 43.5, U32)
        spill = at("spill", [P, 2], 43.75, I32)

        def rs(a, n):
            return r_small[:, a:a + n]
        def by_tile(a, n):
            return rs(a, T * n).rearrange("p (t n) -> p t n", t=T)
        logits = by_tile(0, 36)
        gmax, first, ngmax = rs(72, 2), rs(74, 2), rs(76, 2)
        tied, onehot, noh, pos_tmp = by_tile(80, 4), by_tile(88, 4), by_tile(96, 4), by_tile(104, 4)
        e_of_g = rs(120, 64).rearrange("p (t e g) -> p t e g", t=T, e=EXPERTS)
        e8, emax, idx = by_tile(184, 8), by_tile(200, 8), by_tile(216, 8)
        gexp, gsum = rs(250, 8), rs(258, 2)
        ediff, eexp, esum, w1, w2 = rs(260, 2), rs(262, 2), rs(264, 2), rs(266, 2), rs(268, 2)
        comb, comb2 = by_tile(270, 8), by_tile(286, 8)
        pos = rs(302, 2)
        member = rs(304, 10).rearrange("p (g t) -> p g t", t=T)
        slot_of = rs(324, 10).rearrange("p (g t) -> p g t", t=T)
        over, over_g = rs(334, 4), rs(338, 2)
        cg = rs(340, 8)

        moe_names = ("rw_landed", "hn_hi_ready", "hn_lo_ready", "hgT_act", "hgT_dve", "routed", 
                     "ngmax_ready", "gsum_ready", "ediff_ready", "eexp_ready", "onehot_ready", "ranked", "comb_ready",
                     "spill_ready", "pick_ready", "gathered", "x_hi_ready", "x_lo_ready", "pickT_turned",
                     "pickT_ready", "cg_done", "cg_ready", "gate_ready", "hid_ready", "hid_turned", "hidT_hi_ready",
                     "hidT_lo_ready", "y_done", "y_hi_ready", "y_lo_ready", "scattered", "h_added")
        m = sems("moe", *moe_names)
        def group_no(layer, g):
            return g + GROUPS * layer

        sp_names = ("pick_ready", "gathered", "x_hi_ready", "x_lo_ready", "pickT_turned", "pickT_ready", "cg_done",
                    "cg_ready", "landed", "gu_done", "gate_ready", "hid_ready", "hid_turned", "hidT_hi_ready", "hidT_lo_ready",
                    "used", "y_hi_ready", "y_lo_ready", "scattered", "h_added")
        spill_sems = [sems(f"spill{i}", *sp_names) for i in range(2)]
        MOE_C0 = (MOE0, MOE1)

        def pass_sems(layer, gi):
            if isinstance(gi, int) and gi == GROUPS:
                return spill_sems[layer], 0
            return m, group_no(layer, gi)

        def moe_pool_loads(pool, layer):
            pool.wait_ge(norm.hg_ready, 8 * (layer + 1))
            pool.dma_start(rw[:], routers[layer]).then_inc(m.rw_landed, 16)

        def route_pe(pe, layer):
            ph = 2 * layer + 1
            turn_pe(pe, ph, hg1)
            pe.wait_ge(m.rw_landed, 16 * (layer + 1))
            for half in range(2):
                pe.wait_ge(m.hgT_act, 2 * layer + half + 1)
                pe.wait_ge(m.hgT_dve, 2 * layer + half + 1)
                for t in range(T):
                    for k in range(4 * half, 4 * half + 4):
                        mm = nc.tensor.matmul(psum[:, 2 * t, 0:36], hgT[:, k, t * P:(t + 1) * P], rw[:, k, :],
                                              start=(k == 0), stop=(k == KD - 1))
            mm.then_inc(m.routed, 1)
            pe.wait_ge(m.onehot_ready, 2 * layer + 1)
            nc.tensor.matmul(psum[:, 1, 0:4], before, onehot[:, 0, :], start=True, stop=True, skip_group_check=True)
            nc.tensor.matmul(psum[:, 1, 4:8], before, onehot[:, 1, :], start=True, stop=False, skip_group_check=True)
            pe.wait_ge(m.onehot_ready, 2 * layer + 2)
            nc.tensor.matmul(psum[:, 1, 4:8], negones, noh[:, 0, :], start=False, stop=True, skip_group_check=True)
            for t in range(T):
                mm = nc.tensor.matmul(psum[:, 1, 8:12], negones, noh[:, t, :], start=(t == 0), stop=(t == 1),
                                      skip_group_check=True)
            mm.then_inc(m.ranked, 1)

        def route_act(act, layer):
            ph = 2 * layer + 1
            for b in (0, 2):
                act.wait_ge(norm.turned, 4 * ph + b + 1)
                nc.scalar.copy(hgT[:, 2 * b:2 * b + 2, :], bank(4 + b).rearrange("p (j s) -> p j s", j=2)
                               ).then_inc(m.hgT_act, 1)
            rms_act(act, ph)
            act.wait_ge(norm.rstd_ready, ph + 1)
            for t in range(T):
                nc.scalar.activation(hn_hi[:, t, :], hg1[:, t, :], ACT.Copy, scale=rstd[:, t:t + 1]
                                     ).then_inc(m.hn_hi_ready, 1)
            act.wait_ge(m.ngmax_ready, layer + 1)
            for t in range(T):
                nc.scalar.activation(gexp[:, 4 * t:4 * t + 4], logits[:, t, 0:4], ACT.Exp, bias=ngmax[:, t:t + 1],
                                     accum_out=gsum[:, t:t + 1]).then_inc(m.gsum_ready, 1)
            act.wait_ge(m.ediff_ready, layer + 1)
            nc.scalar.activation(eexp, ediff, ACT.Exp).then_inc(m.eexp_ready, 1)

        def route_dve(dve, layer):
            ph = 2 * layer + 1
            for b in (1, 3):
                dve.wait_ge(norm.turned, 4 * ph + b + 1)
                nc.vector.tensor_copy(hgT[:, 2 * b:2 * b + 2, :], bank(4 + b).rearrange("p (j s) -> p j s", j=2)
                                      ).then_inc(m.hgT_dve, 1)
            rstd_dve(dve, ph)
            dve.wait_ge(norm.rstd_ready, ph + 1)
            dve.wait_ge(m.routed, layer + 1)
            for t in range(T):
                ins = nc.vector.tensor_scalar(logits[:, t, :], psum[:, 2 * t, 0:36], rstd[:, t:t + 1], None, ALU.mult)
            link(ins)
            groups_of = logits[:, :, 0:GROUPS]
            link(nc.vector.tensor_reduce(gmax, groups_of, AX.X, ALU.max))
            link(nc.vector.tensor_tensor(tied, groups_of, gmax.unsqueeze(2).to_broadcast([P, T, GROUPS]), ALU.is_equal))
            link(nc.vector.tensor_tensor(tied, tied, falling.unsqueeze(1).to_broadcast([P, T, GROUPS]), ALU.mult))
            link(nc.vector.tensor_reduce(first, tied, AX.X, ALU.max))
            nc.vector.tensor_tensor(onehot, tied, first.unsqueeze(2).to_broadcast([P, T, GROUPS]), ALU.is_equal
                                    ).then_inc(m.onehot_ready, 1)
            dve.wait_ge(m.onehot_ready, 2 * layer + 1)
            nc.vector.tensor_scalar(noh, onehot, -1.0, None, ALU.mult).then_inc(m.onehot_ready, 1)
            nc.vector.tensor_scalar(ngmax, gmax, -1.0, None, ALU.mult).then_inc(m.ngmax_ready, 1)
            link(nc.vector.memset(member[:, GROUPS, :], 1.0))
            link(nc.vector.tensor_copy(member[:, 0:GROUPS, :], onehot.rearrange("p t g -> p g t")))
            dve.wait_ge(m.ranked, layer + 1)
            link(nc.vector.tensor_tensor(pos_tmp, psum[:, 1, 0:8].rearrange("p (t n) -> p t n", t=T), onehot, ALU.mult))
            link(nc.vector.tensor_reduce(pos, pos_tmp, AX.X, ALU.add))
            link(nc.vector.tensor_copy(slot_of[:, 0:GROUPS, :], pos.unsqueeze(1).to_broadcast([P, GROUPS, T])))
            pick_dve(dve, layer, 0)
            for t in range(T):
                dve.wait_ge(m.hn_hi_ready, 2 * layer + t + 1)
                nc.vector.scalar_tensor_tensor(hn_lo[:, t, :], hg1[:, t, :], rstd[:, t:t + 1],
                                               hn_hi[:, t, :].bitcast(F32), ALU.mult, ALU.subtract
                                               ).then_inc(m.hn_lo_ready, 1)
            link(nc.vector.tensor_scalar(slot_of[:, GROUPS, :], pos, -float(P), None, ALU.add))

        def x_and_weights_dve(dve, layer):
            x_copy(dve, layer, 0, "lo", 0)
            x_copy(dve, layer, 0, "lo", 1)
            link(nc.vector.tensor_scalar(over, psum[:, 1, 8:12], float(P), None, ALU.is_gt))
            link(nc.vector.tensor_tensor(e_of_g, logits[:, :, 4:36].rearrange("p t (g e) -> p t e g", g=GROUPS),
                                         onehot.unsqueeze(2).to_broadcast([P, T, EXPERTS, GROUPS]), ALU.mult))
            link(nc.vector.tensor_reduce(e8, e_of_g, AX.X, ALU.add))
            for t in range(T):
                link(nc.vector.max(emax[:, t, :], e8[:, t, :]))
                link(nc.vector.max_index(top_idx[:, t, :], emax[:, t, :], e8[:, t, :]))
            link(nc.vector.tensor_copy(idx, top_idx[:]))
            nc.vector.tensor_tensor(ediff, emax[:, :, 1], emax[:, :, 0], ALU.subtract).then_inc(m.ediff_ready, 1)
            dve.wait_ge(m.eexp_ready, layer + 1)
            dve.wait_ge(m.gsum_ready, 2 * (layer + 1))
            link(nc.vector.scalar_tensor_tensor(esum, eexp, 1.0, gsum, ALU.add, ALU.mult))
            link(nc.vector.reciprocal(w1, esum))
            link(nc.vector.tensor_tensor(w2, eexp, w1, ALU.mult))
            for t in range(T):
                link(nc.vector.tensor_scalar(comb[:, t, :], iota[:, 0:8], idx[:, t, 0:1], w1[:, t:t + 1],
                                             ALU.is_equal, ALU.mult))
                link(nc.vector.tensor_scalar(comb2[:, t, :], iota[:, 0:8], idx[:, t, 1:2], w2[:, t:t + 1],
                                             ALU.is_equal, ALU.mult))
            nc.vector.tensor_tensor(comb, comb, comb2, ALU.add).then_inc(m.comb_ready, 1)

        def spill_flag_dve(dve, layer):
            link(nc.vector.scalar_tensor_tensor(over, iota[:, 0:4], 1.0, over, ALU.add, ALU.mult))
            link(nc.vector.tensor_reduce(over_g[:, 0:1], over, AX.X, ALU.add))
            link(nc.vector.tensor_scalar(over_g[:, 1:2], over_g[:, 0:1], -1.0, 0.0, ALU.add, ALU.max))
            nc.vector.tensor_copy(spill[:], over_g).then_inc(m.spill_ready, 1)

        def pick_dve(dve, layer, gi):
            s, n = pass_sems(layer, gi)
            if not (layer == 0 and isinstance(gi, int) and gi == 0):
                dve.wait_ge(m.cg_done, group_no(layer, gi))
            for t in range(T):
                def entry(a):
                    return a[:, bass.ds(gi, 1), t:t + 1].rearrange("p a t -> p (a t)")
                nc.vector.tensor_scalar(pick[:, t, :], iota, entry(slot_of), entry(member), ALU.is_equal, ALU.mult
                                        ).then_inc(s.pick_ready, 1)

        GATHER = ((5, "hi", 0), (6, "lo", 0), (7, "hi", 1), (0, "lo", 1))

        def gather_pe(pe, layer, gi):
            s, no = pass_sems(layer, gi)
            pe.wait_ge(s.pick_ready, 2 * no + 2)
            for n, (b, part, half) in enumerate(GATHER):
                src = hn_hi if part == "hi" else hn_lo
                for kk in range(4):
                    k = 4 * half + kk
                    for t in range(T):
                        mm = nc.tensor.matmul(psum[:, b, kk * P:(kk + 1) * P], src[:, t, k * P:(k + 1) * P],
                                              pick[:, t, :], start=(t == 0), stop=(t == 1), skip_group_check=True)
                mm.then_inc(s.gathered, 1)

        def x_copy(eng, layer, gi, part, half):
            n = [i for i, (_, p_, h_) in enumerate(GATHER) if (p_, h_) == (part, half)][0]
            s, no = pass_sems(layer, gi)
            eng.wait_ge(s.gathered, 4 * no + n + 1)
            src = bank(GATHER[n][0]).rearrange("p (k s) -> p k s", k=4)
            ks = slice(4 * half, 4 * half + 4)
            if part == "hi":
                nc.scalar.copy(x_hi[:, ks, :], src).then_inc(s.x_hi_ready, 1)
            else:
                nc.vector.tensor_copy(x_lo[:, ks, :], src).then_inc(s.x_lo_ready, 1)

        def pickT_pe(pe, layer, gi):
            s, no = pass_sems(layer, gi)
            for t in range(T):
                mm = nc.tensor.transpose(psum[:, 4, S + t * P:S + (t + 1) * P], pick[:, t, :].bitcast(F32), ident)
            mm.then_inc(s.pickT_turned, 1)
            pe.wait_ge(m.comb_ready, layer + 1)
            for t in range(T):
                mm = nc.tensor.matmul(psum[:, 1, 0:8], pick[:, t, :].bitcast(F32), comb[:, t, :], start=(t == 0),
                                      stop=(t == 1), skip_group_check=True)
            mm.then_inc(s.cg_done, 1)

        def pickT_act(act, layer, gi):
            s, no = pass_sems(layer, gi)
            act.wait_ge(s.pickT_turned, no + 1)
            nc.scalar.copy(pickT[:], psum[:, 4, S:2 * S]).then_inc(s.pickT_ready, 1)

        def cg_dve(dve, layer, gi):
            s, no = pass_sems(layer, gi)
            dve.wait_ge(s.cg_done, no + 1)
            nc.vector.tensor_copy(cg, psum[:, 1, 0:8]).then_inc(s.cg_ready, 1)

        def gate_up_pe(pe, layer, g, e, half):
            c = MOE_C0[layer] + gu_at(e, half)
            pe.wait_ge(lo_done, c + 1 + g * PER_GROUP)
            if half == 0 and e == 1:
                pe.wait_ge(m.cg_ready, group_no(layer, g) + 1)
            for kk in range(4):
                k = 4 * half + kk
                mm = three(bank(e % 2), x_hi[:, k, :], x_lo[:, k, :], c, slice(kk * W4, (kk + 1) * W4),
                           k == 0, k == KD - 1)
            mm.then_inc(w_used, 1)

        def gate_act(act, layer, g, e):
            act.wait_ge(w_used, MOE_C0[layer] + gu_at(e, 1) + 1 + g * PER_GROUP)
            nc.scalar.activation(gate[:], psum[:, e % 2, 0:FF], ACT.Silu).then_inc(m.gate_ready, 1)

        def hid_dve(dve, layer, g, e):
            dve.wait_ge(m.gate_ready, group_no(layer, g) * EXPERTS + e + 1)
            if e == 0:
                dve.wait_ge(m.cg_ready, group_no(layer, g) + 1)
            nc.vector.scalar_tensor_tensor(hid[:], psum[:, e % 2, FF:2 * FF], cg[:, e:e + 1], gate[:], ALU.mult,
                                           ALU.mult).then_inc(m.hid_ready, 1)

        def turn_hid(pe, layer, g, e):
            pe.wait_ge(m.hid_ready, group_no(layer, g) * EXPERTS + e + 1)
            if e == 0:
                pe.wait_ge(m.pickT_ready, group_no(layer, g) + 1)
            for j in range(2):
                mm = nc.tensor.transpose(psum[:, 4, j * P:(j + 1) * P], hid[:, j * P:(j + 1) * P], ident)
            mm.then_inc(m.hid_turned, 1)

        def hidT_act(act, layer, g, e):
            act.wait_ge(m.hid_turned, group_no(layer, g) * EXPERTS + e + 1)
            nc.scalar.copy(hidT_hi[:, e % 2], psum[:, 4, 0:2 * P].rearrange("p (j s) -> p j s", j=2)
                           ).then_inc(m.hidT_hi_ready, 1)

        def hidT_dve(dve, layer, g, e):
            dve.wait_ge(m.hidT_hi_ready, group_no(layer, g) * EXPERTS + e + 1)
            nc.vector.tensor_tensor(hidT_lo[:, e % 2], psum[:, 4, 0:2 * P].rearrange("p (j s) -> p j s", j=2),
                                    hidT_hi[:, e % 2].bitcast(F32), ALU.subtract).then_inc(m.hidT_lo_ready, 1)

        def down_pe(pe, layer, g, e, blocks=(0, 1)):
            c = MOE_C0[layer] + down_at(e)
            if blocks[0] == 0:
                pe.wait_ge(lo_done, c + 1 + g * PER_GROUP)
                pe.wait_ge(m.hidT_lo_ready, group_no(layer, g) * EXPERTS + e + 1)
            for n in blocks:
                for j in range(2):
                    mm = three(bank(2 + n), hidT_hi[:, e % 2, j, :], hidT_lo[:, e % 2, j, :], c,
                               slice(j * D + n * W4, j * D + (n + 1) * W4), e == 0 and j == 0,
                               e == EXPERTS - 1 and j == 1)
                if n == 0 and e == EXPERTS - 1:
                    mm.then_inc(m.y_done, 1)
            if blocks[-1] == 1:
                mm.then_inc(w_used, 1)

        SCATTER = ((0, 0, 5), (1, 0, 6), (0, 1, 7), (1, 1, 5))

        def scatter_pe(pe, layer, g):
            for n, (t, blk, b) in enumerate(SCATTER):
                if n % 2 == 0:
                    pe.wait_ge(m.y_lo_ready, 2 * group_no(layer, g) + blk + 1)
                if n == 3:
                    pe.wait_ge(m.h_added, 4 * group_no(layer, g) + 1)
                cols = slice(blk * W4, (blk + 1) * W4)
                nc.tensor.matmul(bank(b), pickT[:, t * P:(t + 1) * P], y_hi[:, cols], start=True, stop=False)
                nc.tensor.matmul(bank(b), pickT[:, t * P:(t + 1) * P], y_lo[:, cols], start=False, stop=True
                                 ).then_inc(m.scattered, 1)

        def y_act(act, layer, g, n):
            if n == 0:
                act.wait_ge(m.y_done, group_no(layer, g) + 1)
            else:
                act.wait_ge(w_used, MOE_C0[layer] + PER_GROUP + g * PER_GROUP)
            nc.scalar.copy(y_hi[:, n * W4:(n + 1) * W4], bank(2 + n)).then_inc(m.y_hi_ready, 1)

        def y_dve(dve, layer, g, n):
            cols = slice(n * W4, (n + 1) * W4)
            dve.wait_ge(m.y_hi_ready, 2 * group_no(layer, g) + n + 1)
            nc.vector.tensor_tensor(y_lo[:, cols], bank(2 + n), y_hi[:, cols].bitcast(F32), ALU.subtract
                                    ).then_inc(m.y_lo_ready, 1)

        def h_dve(dve, layer, g):
            for n, (t, blk, b) in enumerate(SCATTER):
                dve.wait_ge(m.scattered, 4 * group_no(layer, g) + n + 1)
                cols = slice(blk * W4, (blk + 1) * W4)
                nc.vector.tensor_tensor(h[:, t, cols], bank(b), h[:, t, cols], ALU.add).then_inc(m.h_added, 1)

        LASTE = EXPERTS - 1

        def open_pe(pe, layer, g):
            pe.wait_ge(m.x_hi_ready, 2 * group_no(layer, g) + 2)
            pe.wait_ge(m.x_lo_ready, 2 * group_no(layer, g) + 2)
            gate_up_pe(pe, layer, g, 0, 0)

        def group_pe(pe, layer, g, last):
            pickT_pe(pe, layer, g)
            for e in range(EXPERTS):
                if e > 0:
                    gate_up_pe(pe, layer, g, e, 0)
                    turn_hid(pe, layer, g, e - 1)
                gate_up_pe(pe, layer, g, e, 1)
                if 0 < e < LASTE:
                    down_pe(pe, layer, g, e - 1)
            down_pe(pe, layer, g, LASTE - 1, (0,))
            turn_hid(pe, layer, g, LASTE)
            if not last:
                gather_pe(pe, layer, g + 1)
            down_pe(pe, layer, g, LASTE - 1, (1,))
            down_pe(pe, layer, g, LASTE)
            if not last:
                open_pe(pe, layer, g + 1)
            scatter_pe(pe, layer, g)

        def group_steps(eng, layer, g, last, small, turned, x_of_next, sums, split):
            for i in range(1, PER_GROUP + (0 if last else 1)):
                for e in range(EXPERTS):
                    if i == gu_at(e, 1) + 1:
                        small(eng, layer, g, e)
                    if e < LASTE and i == gu_at(e + 1, 1):
                        turned(eng, layer, g, e)
                if i == down_at(LASTE - 1):
                    turned(eng, layer, g, LASTE)
                if i == PER_GROUP:
                    sums(eng, layer, g)
                if not (last and layer == 1 and i + AHEAD >= PER_GROUP):
                    split(eng, MOE_C0[layer] + i + AHEAD, g)
                if i == down_at(LASTE - 1) and not last:
                    x_of_next(eng, layer, g + 1)
            if last:
                sums(eng, layer, g)

        def x_hi_act(act, layer, gi):
            x_copy(act, layer, gi, "hi", 0)
            x_copy(act, layer, gi, "hi", 1)

        def x_lo_dve(dve, layer, gi):
            x_copy(dve, layer, gi, "lo", 0)
            x_copy(dve, layer, gi, "lo", 1)

        def sums_act(act, layer, g):
            y_act(act, layer, g, 0)
            y_act(act, layer, g, 1)

        def sums_dve(dve, layer, g):
            y_dve(dve, layer, g, 0)
            y_dve(dve, layer, g, 1)
            h_dve(dve, layer, g)

        def group_act(act, layer, g, last):
            pickT_act(act, layer, g)
            group_steps(act, layer, g, last, gate_act, hidT_act, x_hi_act, sums_act, split_hi)

        def group_dve(dve, layer, g, last):
            cg_dve(dve, layer, g)
            if not last:
                pick_dve(dve, layer, g + 1)
            group_steps(dve, layer, g, last, hid_dve, hidT_dve, x_lo_dve, sums_dve, split_lo)

        def groups(eng, layer, body):
            with eng.Fori(0, GROUPS - 1) as g:
                body(eng, layer, g, False)
            body(eng, layer, GROUPS - 1, True)

        SPILL_SLOT = [(MOE_CHUNKS + MOE0 + AHEAD + n) % RAW for n in range(3)]

        def spill_flag(eng, layer):
            eng.wait_ge(m.spill_ready, layer + 1)
            return eng.value_load(spill[0:1, 0:1], min_val=0, max_val=GROUPS)

        def spill_sp(sp, layer):
            flag = spill_flag(sp, layer)
            spl = spill_sems[layer]
            full = sp.value_load(spill[0:1, 1:2], min_val=0, max_val=GROUPS - 1)
            with sp.If(flag > 0):
                sp.wait_ge(lo_done, MOE_C0[layer] + MOE_CHUNKS)
                for e in range(EXPERTS):
                    if e:
                        sp.wait_ge(spl.used, e)
                    for n, at_ in enumerate((gu_at(e, 0), gu_at(e, 1), down_at(e))):
                        index = full * PER_GROUP + (MOE_C0[layer] + at_)
                        sp.dma_start(raw[:, SPILL_SLOT[n], :], stream[bass.ds(index, 1)].rearrange("a p n -> (a p) n")
                                     ).then_inc(spl.landed, 16)
                sp.wait_ge(spl.h_added, 4)
            with sp.Else():
                pass

        def spill_pe(pe, layer):
            flag = spill_flag(pe, layer)
            spl = spill_sems[layer]
            with pe.If(flag > 0):
                pe.wait_ge(m.h_added, 4 * GROUPS * (layer + 1))
                gather_pe(pe, layer, GROUPS)
                pickT_pe(pe, layer, GROUPS)
                pe.wait_ge(spl.x_hi_ready, 2)
                pe.wait_ge(spl.x_lo_ready, 2)
                pe.wait_ge(spl.pickT_ready, 1)
                pe.wait_ge(spl.cg_ready, 1)
                for e in range(EXPERTS):
                    pe.wait_ge(spl.landed, 48 * (e + 1))
                    for k in range(KD):
                        rhs = raw[:, SPILL_SLOT[k // 4], (k % 4) * W4:(k % 4 + 1) * W4]
                        nc.tensor.matmul(bank(0), x_hi[:, k, :].bitcast(F32), rhs, start=(k == 0), stop=False)
                        mm = nc.tensor.matmul(bank(0), x_lo[:, k, :].bitcast(F32), rhs, start=False, stop=(k == KD - 1))
                    mm.then_inc(spl.gu_done, 1)
                    pe.wait_ge(spl.hid_ready, e + 1)
                    for j in range(2):
                        mm = nc.tensor.transpose(psum[:, 4, j * P:(j + 1) * P], hid[:, j * P:(j + 1) * P], ident)
                    mm.then_inc(spl.hid_turned, 1)
                    pe.wait_ge(spl.hidT_lo_ready, e + 1)
                    for n in range(2):
                        for j in range(2):
                            rhs = raw[:, SPILL_SLOT[2], j * D + n * W4:j * D + (n + 1) * W4]
                            nc.tensor.matmul(bank(2 + n), hidT_hi[:, 0, j, :].bitcast(F32), rhs,
                                             start=(e == 0 and j == 0), stop=False)
                            mm = nc.tensor.matmul(bank(2 + n), hidT_lo[:, 0, j, :].bitcast(F32), rhs, start=False,
                                                  stop=(e == LASTE and j == 1))
                    mm.then_inc(spl.used, 1)
                pe.wait_ge(spl.y_lo_ready, 2)
                for n, (t, blk, b) in enumerate(SCATTER):
                    cols = slice(blk * W4, (blk + 1) * W4)
                    if n == 3:
                        pe.wait_ge(spl.h_added, 1)
                    nc.tensor.matmul(bank(b), pickT[:, t * P:(t + 1) * P], y_hi[:, cols], start=True, stop=False)
                    nc.tensor.matmul(bank(b), pickT[:, t * P:(t + 1) * P], y_lo[:, cols], start=False, stop=True
                                     ).then_inc(spl.scattered, 1)
                pe.wait_ge(spl.h_added, 4)
            with pe.Else():
                pass

        def spill_act(act, layer):
            flag = spill_flag(act, layer)
            spl = spill_sems[layer]
            with act.If(flag > 0):
                x_hi_act(act, layer, GROUPS)
                pickT_act(act, layer, GROUPS)
                for e in range(EXPERTS):
                    act.wait_ge(spl.gu_done, e + 1)
                    nc.scalar.activation(gate[:], psum[:, 0, 0:FF], ACT.Silu).then_inc(spl.gate_ready, 1)
                    act.wait_ge(spl.hid_turned, e + 1)
                    if e:
                        act.wait_ge(spl.used, e)
                    nc.scalar.copy(hidT_hi[:, 0], psum[:, 4, 0:2 * P].rearrange("p (j s) -> p j s", j=2)
                                   ).then_inc(spl.hidT_hi_ready, 1)
                act.wait_ge(spl.used, EXPERTS)
                for n in range(2):
                    nc.scalar.copy(y_hi[:, n * W4:(n + 1) * W4], bank(2 + n)).then_inc(spl.y_hi_ready, 1)
                act.wait_ge(spl.h_added, 4)
            with act.Else():
                pass

        def spill_dve(dve, layer):
            flag = spill_flag(dve, layer)
            spl = spill_sems[layer]
            with dve.If(flag > 0):
                pick_dve(dve, layer, GROUPS)
                x_lo_dve(dve, layer, GROUPS)
                cg_dve(dve, layer, GROUPS)
                dve.wait_ge(spl.cg_ready, 1)
                for e in range(EXPERTS):
                    dve.wait_ge(spl.gate_ready, e + 1)
                    nc.vector.scalar_tensor_tensor(hid[:], psum[:, 0, FF:2 * FF], cg[:, e:e + 1], gate[:], ALU.mult,
                                                   ALU.mult).then_inc(spl.hid_ready, 1)
                    dve.wait_ge(spl.hidT_hi_ready, e + 1)
                    nc.vector.tensor_tensor(hidT_lo[:, 0], psum[:, 4, 0:2 * P].rearrange("p (j s) -> p j s", j=2),
                                            hidT_hi[:, 0].bitcast(F32), ALU.subtract).then_inc(spl.hidT_lo_ready, 1)
                for n in range(2):
                    cols = slice(n * W4, (n + 1) * W4)
                    dve.wait_ge(spl.y_hi_ready, n + 1)
                    nc.vector.tensor_tensor(y_lo[:, cols], bank(2 + n), y_hi[:, cols].bitcast(F32), ALU.subtract
                                            ).then_inc(spl.y_lo_ready, 1)
                dve.wait_ge(m.h_added, 4 * GROUPS * (layer + 1))
                for n, (t, blk, b) in enumerate(SCATTER):
                    dve.wait_ge(spl.scattered, n + 1)
                    cols = slice(blk * W4, (blk + 1) * W4)
                    nc.vector.tensor_tensor(h[:, t, cols], bank(b), h[:, t, cols], ALU.add).then_inc(spl.h_added, 1)
                dve.wait_ge(spl.h_added, 4)
            with dve.Else():
                pass

        block = ctx.enter_context(nc.Block())

        @block.sync
        def _(sp):
            sp.dma_start(h[:], x.rearrange("a (t p) d -> p (a t) d", p=P)).then_inc(x_landed, 16)
            sp.dma_start(cst[:], consts).then_inc(cst_landed, 16)
            for c in range(RAW):
                load_chunk(sp, (c, c))
            with sp.Fori(1, PROJ1 // RAW) as turn:
                for i in range(RAW):
                    load_chunk(sp, (i, turn * RAW + i), turn * RAW + (i - RAW + 1))
            for c in range(PROJ1, PROJ1 + AHEAD):
                load_chunk(sp, (c % RAW, c), c - RAW + 1)
            spill_sp(sp, 0)
            for c in range(PROJ1 + AHEAD, PROJ1 + RAW):
                load_chunk(sp, (c % RAW, c), c - RAW + 1)
            with sp.Fori(PROJ1 // RAW + 1, CHUNKS // RAW) as turn:
                for i in range(RAW):
                    load_chunk(sp, (i, turn * RAW + i), turn * RAW + (i - RAW + 1))
            for c in range(CHUNKS // RAW * RAW, CHUNKS):
                load_chunk(sp, (c % RAW, c), c - RAW + 1)
            spill_sp(sp, 1)
            sp.wait_ge(m.h_added, 2 * 4 * GROUPS)
            sp.dma_start(out.rearrange("a (t p) d -> p (a t) d", p=P), h[:]).then_inc(out_written, 16)
            sp.wait_ge(out_written, 16)

        @block.gpsimd
        def _(pool):
            even_pool_loads(pool)
            moe_pool_loads(pool, 0)
            odd_pool_loads(pool)
            moe_pool_loads(pool, 1)

        @block.tensor
        def _(pe):
            even_pe(pe)
            for layer in range(2):
                if layer:
                    odd_pe(pe)
                route_pe(pe, layer)
                pe.wait_ge(m.hn_lo_ready, 2 * (layer + 1))
                gather_pe(pe, layer, 0)
                open_pe(pe, layer, 0)
                groups(pe, layer, group_pe)
                spill_pe(pe, layer)

        @block.scalar
        def _(act):
            even_act(act)
            for layer in range(2):
                if layer:
                    odd_act(act)
                route_act(act, layer)
                x_hi_act(act, layer, 0)
                split_hi(act, MOE_C0[layer] + AHEAD)
                groups(act, layer, group_act)
                spill_act(act, layer)

        @block.vector
        def _(dve):
            even_dve(dve)
            for layer in range(2):
                if layer:
                    odd_dve(dve)
                route_dve(dve, layer)
                x_and_weights_dve(dve, layer)
                split_lo(dve, MOE_C0[layer] + AHEAD)
                spill_flag_dve(dve, layer)
                groups(dve, layer, group_dve)
                spill_dve(dve, layer)


def shape_constants():
    r = np.arange(P)
    c = np.zeros((P, C_N), np.float32)
    c[:, C_ID:C_ID + P] = np.eye(P)
    c[:, C_NTRI:C_NTRI + P] = -(r[:, None] >= r[None, :]).astype(np.float32)
    c[:, C_NONE:C_NONE + P] = -1
    c[:, C_LT:C_LT + P] = r[:, None] < r[None, :]
    c[:, C_IOTA:C_IOTA + P] = r[None, :]
    c[:, C_EPS] = EPS
    c[:, C_REV:C_REV + GROUPS] = GROUPS - np.arange(GROUPS)
    return c


def band_constants():
    s, t = np.arange(S)[:, None], np.arange(S)[None, :]
    full = np.stack([((s <= t) & (s > t - w)) / np.minimum(t + 1, w) - (s == t) for w in WINDOWS], 1)
    full = full.astype(np.float32)
    return full[:P], full[P:, :, P:]


_INS = ["x", "stream", "gains", "consts", "even_pool", "even_bias", "even_cols", "odd_sgu", "odd_vgain", "routers"]


def laid_out(a):
    def tiles(w):
        n = w.shape[1] // W4
        return w.reshape(2, 4, P, n, W4).transpose(3, 0, 2, 1, 4).reshape(n, 2, P, CH)

    stream = np.empty((CHUNKS, P, CH), np.float32)

    def mixer(c0, w_in, order, names, w_out):
        t = tiles(w_in)
        for nb, name in enumerate(order):
            stream[c0 + 2 * nb:c0 + 2 * nb + 2] = t[names.index(name)]
        c1 = c0 + 2 * len(order)
        stream[c1:c1 + 4] = tiles(w_out).reshape(4, P, CH)

    mixer(PROJ0, a["w_in_even"][0], EVEN_BLOCKS, ("q", "k", "v", "p"), a["w_out_even"][0])
    mixer(PROJ1, a["w_in_odd"][0], ODD_BLOCKS, ("u", "vv", "q", "k", "v"), a["w_out_odd"][0])
    for layer, c0 in enumerate((MOE0, MOE1)):
        moe = stream[c0:c0 + MOE_CHUNKS].reshape(GROUPS, PER_GROUP, P, CH)
        for e in range(EXPERTS):
            for half in range(2):
                dst = moe[:, gu_at(e, half)].reshape(GROUPS, P, 4, 2, FF)
                for n, name in enumerate(("w_exp_gate", "w_exp_up")):
                    src = a[name][layer, :, e, half * 512:(half + 1) * 512, :]
                    dst[:, :, :, n, :] = src.reshape(GROUPS, 4, P, FF).transpose(0, 2, 1, 3)
            moe[:, down_at(e)].reshape(GROUPS, P, 2, D)[:] = (
                a["w_exp_down"][layer, :, e].reshape(GROUPS, 2, P, D).transpose(0, 2, 1, 3))

    order = [0, 2, 4, 6, 1, 3, 5, 7]
    q, k = np.arange(S)[:, None], np.arange(S)[None, :]
    bias = a["att_rel_bias"][0][:, np.clip(q - k, -128, 128) + 128][order]
    even_bias = np.concatenate([bias[:, :P, :P].transpose(1, 0, 2).reshape(P, -1),
                                bias[:, P:, :].transpose(1, 0, 2).reshape(P, -1)], 1)
    band0, band1 = band_constants()
    return {
        "x": a["x"],
        "stream": stream,
        "gains": np.stack([a["mix_norm_even"][0], a["ffn_norm"][0], a["mix_norm_odd"][0], a["ffn_norm"][1]]),
        "consts": shape_constants(),
        "even_pool": np.concatenate([band0, band1, a["pool_w"][0].transpose(1, 0, 2)], 2),
        "even_bias": even_bias,
        "even_cols": np.concatenate([np.tile(a["att_q_norm"][0], 2)[:, None], np.tile(a["att_k_norm"][0], 2)[:, None],
                                     a["pool_scale"][0].reshape(4, P).T], 1),
        "odd_sgu": np.concatenate([a["sgu_w"][0].transpose(2, 0, 1).reshape(P, 4 * P), a["sgu_b"][0].T], 1),
        "odd_vgain": a["sgu_v_norm"][0],
        "routers": np.concatenate([a["w_router_group"], a["w_router_expert"]], 2).reshape(2, KD, P, 36)
                   .transpose(0, 2, 1, 3),
    }


def kernel(**inputs):
    import concourse.bacc as _bacc
    from concourse.bass_utils import run_bass_kernel_spmd as _run

    nc = _bacc.Bacc("TRN2", target_bir_lowering=False, num_devices=1)
    data = laid_out({k: np.asarray(v) for k, v in inputs.items()})
    arrays, args = {}, []
    for name in _INS:
        arrays[name] = np.ascontiguousarray(data[name])
        args.append(nc.dram_tensor(name, arrays[name].shape, F32, kind="ExternalInput").ap())
    out = nc.dram_tensor("out", (1, S, D), F32, kind="ExternalOutput").ap()
    hybrid_kernel(nc, *args, out)
    r = _run(nc, [arrays], core_ids=[0])
    return r.results[0]["out"]
```

```python
from collections import namedtuple
from contextlib import ExitStack

import concourse.bass as bass
from concourse import mybir
import numpy as np

F32 = mybir.dt.float32
F32R = mybir.dt.float32r
I32 = mybir.dt.int32
U32 = mybir.dt.uint32
ALU = mybir.AluOpType
ACT = mybir.ActivationFunctionType
AX = mybir.AxisListType

P = 128
S = 256
T = S // P
D = 1024
KD = D // P
HEADS, DH = 8, 64
PAIRS = HEADS // 2
W4 = 512
EPS = 1e-6
WINDOWS = (2, 4, 8, 16)
GROUPS, EXPERTS, FF = 4, 8, 256
NEG = -1e30

CH = 2048
RAW = 12
SPLIT = 3
AHEAD = SPLIT - 1
EVEN_BLOCKS = ("q", "k", "p", "v")
ODD_BLOCKS = ("q", "k", "vv", "u", "v")
EVEN_OUT = ((1, 0), (1, 1), (0, 0), (0, 1))
ODD_OUT = ((0, 1), (0, 0), (1, 0), (1, 1))
PER_GROUP = 3 * EXPERTS
MOE_CHUNKS = GROUPS * PER_GROUP
PROJ0, OUT0 = 0, 2 * len(EVEN_BLOCKS)
MOE0 = OUT0 + 4
PROJ1 = MOE0 + MOE_CHUNKS
OUT1 = PROJ1 + 2 * len(ODD_BLOCKS)
MOE1 = OUT1 + 4
CHUNKS = MOE1 + MOE_CHUNKS


def gu_at(e, half):
    return half if e == 0 else 3 * e - 1 + half


def down_at(e):
    return 3 * e + 4 if e < EXPERTS - 1 else PER_GROUP - 1


C_ID, C_NTRI, C_NONE, C_LT, C_IOTA, C_EPS, C_REV = 0, 128, 256, 384, 512, 640, 641
C_GAIN = 645
C_N = 677


def hybrid_kernel(nc, x, stream, gains, consts, even_pool, even_bias, even_cols, odd_sgu, odd_vgain,
                  routers, out):
    ctx = ExitStack()
    with ctx:
        def sem(name):
            return ctx.enter_context(nc.semaphore(name))

        def sems(tag, *names):
            return namedtuple(tag, names)(*[sem(f"{tag}_{n}") for n in names])

        base = -(-nc.sbuf_base // 32) * 32
        taken = [base]

        def fixed(name, shape, dt=F32):
            t = nc.alloc_sbuf_tensor_at(name, shape, dt, offset=taken[0])
            taken[0] += -(-4 * int(np.prod(shape[1:])) // 32) * 32
            return t

        raw = fixed("raw", [P, RAW, CH])
        whi = fixed("whi", [P, SPLIT, CH], F32R)
        wlo = fixed("wlo", [P, SPLIT, CH], F32R)
        h = fixed("h", [P, T, D])
        gain_at = taken[0]
        gain = fixed("gain", [P, D])
        cst = fixed("cst", [P, C_N])
        stat = fixed("stat", [P, 176])
        zeros = fixed("zeros", [P, P], F32R)
        arena = taken[0]

        def at(name, shape, kib, dt=F32):
            return nc.alloc_sbuf_tensor_at(name, shape, dt, offset=arena + int(kib * 1024))

        ident = cst[:, C_ID:C_ID + P]
        negtri = cst[:, C_NTRI:C_NTRI + P]
        negones = cst[:, C_NONE:C_NONE + P]
        before = cst[:, C_LT:C_LT + P]
        iota = cst[:, C_IOTA:C_IOTA + P]
        eps = cst[:, C_EPS:C_EPS + 1]
        falling = cst[:, C_REV:C_REV + GROUPS]

        psum = ctx.enter_context(nc.psum_tensor("psum", [P, 8, W4], F32))

        def bank(b, n=W4):
            return psum[:, b, 0:n]

        raw_landed = [sem(f"raw_landed{i}") for i in range(RAW)]
        hi_done, lo_done, w_used = sem("hi_done"), sem("lo_done"), sem("w_used")
        x_landed, cst_landed, gain_landed, out_written = (
            sem("x_landed"), sem("cst_landed"), sem("gain_landed"), sem("out_written"))

        def load_chunk(sp, c, wait=None):
            slot, index = c
            if wait is not None:
                sp.wait_ge(lo_done, wait)
            sp.dma_start(raw[:, slot, :], stream[bass.ds(index, 1)].rearrange("a p n -> (a p) n")
                         ).then_inc(raw_landed[slot], 16)

        def split_hi(act, c, g=0):
            act.wait_ge(raw_landed[c % RAW], 16 * (c // RAW + 1) + g * (16 * PER_GROUP // RAW))
            if c >= SPLIT:
                act.wait_ge(w_used, c - SPLIT + 1 + g * PER_GROUP)
            nc.scalar.copy(whi[:, c % SPLIT, :], raw[:, c % RAW, :]).then_inc(hi_done, 1)

        def split_lo(dve, c, g=0):
            dve.wait_ge(hi_done, c + 1 + g * PER_GROUP)
            nc.vector.tensor_tensor(wlo[:, c % SPLIT, :], raw[:, c % RAW, :],
                                    whi[:, c % SPLIT, :].bitcast(F32), ALU.subtract).then_inc(lo_done, 1)

        def three(out_ap, hi, lo, c, cols, first, last):
            nc.tensor.matmul(out_ap, hi, whi[:, c % SPLIT, cols], start=first, stop=False)
            nc.tensor.matmul(out_ap, lo, whi[:, c % SPLIT, cols], start=False, stop=False)
            return nc.tensor.matmul(out_ap, hi, wlo[:, c % SPLIT, cols], start=False, stop=last)

        dve_chain, dve_count = sem("dve_chain"), [0]

        def link(ins):
            dve_count[0] += 1
            ins.then_inc(dve_chain, 1)
            nc.vector.wait_ge(dve_chain, dve_count[0])

        zeros_ready = sem("zeros_ready")

        def keep_warm_pe(n):
            for _ in range(n):
                nc.tensor.matmul(bank(3), zeros[:], zeros[:].unsqueeze(1).to_broadcast([P, 4, P]), start=True,
                                 stop=True, skip_group_check=True)

        ssq, ss, rms, rstd = stat[:, 0:4], stat[:, 4:6], stat[:, 6:8], stat[:, 160:162]
        squared = at("squared", [P, W4], 46)
        norm = sems("norm", "ssq_ready", "ss_ready", "rms_ready", "rstd_ready", "hg_ready", "turned", "hi_ready",
                    "lo_ready")

        def cols_of(nb):
            return slice(nb * W4, (nb + 1) * W4)

        def square_act(act, ph, nb, h_sem, h_before):
            for t in range(T):
                n = 2 * nb + t
                act.wait_ge(h_sem, h_before + n + 1 if ph else h_before + 16)
                if ph or n:
                    act.wait_ge(norm.ssq_ready, 4 * ph + n)
                nc.scalar.activation(squared[:], h[:, t, cols_of(nb)], ACT.Square, accum_out=ssq[:, n:n + 1]
                                     ).then_inc(norm.ssq_ready, 1)

        def rms_act(act, ph):
            act.wait_ge(norm.ss_ready, ph + 1)
            if ph == 0:
                act.wait_ge(cst_landed, 16)
            nc.scalar.activation(rms, ss, ACT.Sqrt, bias=eps, scale=1.0 / D).then_inc(norm.rms_ready, 1)

        def rstd_dve(dve, ph):
            dve.wait_ge(norm.ssq_ready, 4 * (ph + 1))
            nc.vector.tensor_tensor(ss, ssq[:, 0:2], ssq[:, 2:4], ALU.add).then_inc(norm.ss_ready, 1)
            dve.wait_ge(norm.rms_ready, ph + 1)
            nc.vector.reciprocal(rstd, rms).then_inc(norm.rstd_ready, 1)

        def hg_dve(dve, layer, nb):
            dve.wait_ge(res_added[layer], 2 * nb + 2)
            dve.wait_ge(gain_landed, 16 * (layer + 1))
            for t in range(T):
                nc.vector.tensor_tensor(hg[:, t, cols_of(nb)], h[:, t, cols_of(nb)], gain[:, cols_of(nb)], ALU.mult
                                        ).then_inc(norm.hg_ready, 1)

        def turn_pe(pe, h_sem, h_counts):
            for b in range(4):
                if b % 2 == 0:
                    pe.wait_ge(h_sem, h_counts[b // 2])
                for j in range(2):
                    for t in range(T):
                        k = 2 * b + j
                        mm = nc.tensor.transpose(psum[:, 4 + b, j * S + t * P:j * S + (t + 1) * P],
                                                 h[:, t, k * P:(k + 1) * P], ident)
                mm.then_inc(norm.turned, 1)

        def gain_col(ph, k):
            n = C_GAIN + KD * ph + k
            return cst[:, n:n + 1]

        def turned_hi(act, ph, hi, banks=range(4)):
            for b in banks:
                act.wait_ge(norm.turned, 4 * ph + b + 1)
                for j in range(2):
                    ins = nc.scalar.activation(hi[:, 2 * b + j, :], psum[:, 4 + b, j * S:(j + 1) * S], ACT.Copy,
                                               scale=gain_col(ph, 2 * b + j))
                ins.then_inc(norm.hi_ready, 1)

        def turned_lo(dve, ph, hi, lo, banks=range(4)):
            for b in banks:
                dve.wait_ge(norm.hi_ready, 4 * (ph // 2) + b + 1)
                for j in range(2):
                    k = 2 * b + j
                    ins = nc.vector.scalar_tensor_tensor(lo[:, k, :], psum[:, 4 + b, j * S:(j + 1) * S], gain_col(ph, k),
                                                         hi[:, k, :].bitcast(F32), ALU.mult, ALU.subtract)
                ins.then_inc(norm.lo_ready, 1)

        proj_out = [sem("proj_out0"), sem("proj_out1")]

        def project(pe, ph, layer, hi, lo, c0, nb, halves=(0, 1)):
            for kh in halves:
                c = c0 + 2 * nb + kh
                if nb == 0:
                    pe.wait_ge(norm.lo_ready, 4 * layer + 2 * kh + 2)
                pe.wait_ge(lo_done, c + 1)
                if nb >= 2 and kh == 0:
                    pe.wait_ge(proj_out[layer], 2 * (nb - 1))
                for t in range(T):
                    for kk in range(4):
                        k = 4 * kh + kk
                        mm = three(bank(2 * (nb % 2) + t), hi[:, k, t * P:(t + 1) * P],
                                   lo[:, k, t * P:(t + 1) * P], c, slice(kk * W4, (kk + 1) * W4),
                                   k == 0, k == KD - 1)
                mm.then_inc(w_used, 1)

        def block_out(act, layer, c0, nb, dst, func=ACT.Copy):
            act.wait_ge(w_used, c0 + 2 * nb + 2)
            if nb == 0:
                act.wait_ge(norm.rstd_ready, 2 * layer + 1)
            for t in range(T):
                nc.scalar.activation(dst[:, t, :], bank(2 * (nb % 2) + t), func, scale=rstd[:, t:t + 1]
                                     ).then_inc(proj_out[layer], 1)

        res_added = [sem("res_added0"), sem("res_added1")]

        def out_step(pe, c0, order, i, hi, lo):
            (_, nb), c = order[i], c0 + i
            pe.wait_ge(lo_done, c + 1)
            for t in range(T):
                for kk in range(4):
                    mm = three(bank(2 * nb + t), hi[:, kk, t * P:(t + 1) * P], lo[:, kk, t * P:(t + 1) * P], c,
                               slice(kk * W4, (kk + 1) * W4), i < 2 and kk == 0, i >= 2 and kk == 3)
            mm.then_inc(w_used, 1)

        def residual(dve, layer, c0, nb):
            dve.wait_ge(w_used, c0 + nb + 3)
            for t in range(T):
                cols = slice(nb * W4, (nb + 1) * W4)
                nc.vector.tensor_tensor(h[:, t, cols], bank(2 * nb + t), h[:, t, cols], ALU.add
                                        ).then_inc(res_added[layer], 1)

        hnT_hi0, hnT_lo0 = at("hnT_hi0", [P, KD, S], 0, F32R), at("hnT_lo0", [P, KD, S], 8, F32R)
        qT0 = at("qT0", [P, PAIRS, S], 32)
        kT0 = nc.alloc_sbuf_tensor_at("kT0", [P, PAIRS, S], F32, offset=gain_at)
        pooled = at("pooled", [P, 4, S], 0)
        mixA_hi, mixA_lo = at("mixA_hi", [P, 4, S], 4, F32R), at("mixA_lo", [P, 4, S], 0, F32R)
        pt0, att = at("pt0", [P, HEADS, P], 8), at("att", [P, T, W4], 12)
        p_in, q_in = at("p_in", [P, T, W4], 16), at("q_in", [P, T, W4], 20)
        k_in, v_in = at("k_in", [P, T, W4], 24), at("v_in", [P, T, W4], 28)
        mixP_hi, mixP_lo = at("mixP_hi", [P, 4, S], 32, F32R), at("mixP_lo", [P, 4, S], 16, F32R)
        pool_c = at("pool_c", [P, 4, 256 + 128 + 128], 20)
        pt1 = at("pt1", [P, 2, HEADS, P], 20)
        pb = [at("pb0", [P, HEADS, P], 36), at("pb1", [P, HEADS, S], 40)]
        cols0 = stat[:, 8:14]
        hss, hrms, hrs = stat[:, 16:48], stat[:, 48:80], stat[:, 80:112]
        nmax, rsum, rinv = stat[:, 112:128], stat[:, 128:144], stat[:, 144:160]
        ev = sems("even", "pool_c_landed", "cols_landed", "banded", "pooled_ready", "pool_done", "mixP_hi_ready",
                  "mixP_lo_ready", "bias_landed", "bias_masked", "ss_ready", "rms_ready", "qk_ready",
                  "qk_turned", "qT_ready", "scored", "biased", "nmax_ready", "probs_ready", "probs_turned",
                  "pt_act", "pt_dve", "pv_done", "att_ready", "att_turned", "mixA_hi_ready", "mixA_lo_ready")

        def even_pool_loads(pool):
            pool.dma_start(cols0, even_cols).then_inc(ev.cols_landed, 16)
            pool.wait_ge(norm.ssq_ready, 4)
            pool.dma_start(pb[0][:], even_bias[:, 0:HEADS * P].rearrange("p (j k) -> p j k", j=HEADS)
                           ).then_inc(ev.bias_landed, 16)
            pool.dma_start(pb[1][:], even_bias[:, HEADS * P:].rearrange("p (j k) -> p j k", j=HEADS)
                           ).then_inc(ev.bias_landed, 16)
            pool.wait_ge(ev.bias_landed, 32)
            nc.gpsimd.memset(pb[0][0:64, :, 64:128], NEG).then_inc(ev.bias_masked, 1)
            nc.gpsimd.memset(pb[1][0:64, :, 192:256], NEG).then_inc(ev.bias_masked, 1)
            pool.wait_ge(ev.qk_turned, 4)
            pool.dma_start(pool_c[:], even_pool).then_inc(ev.pool_c_landed, 16)
            pool.wait_ge(ev.scored, 6)
            pool.dma_start(gain[:], gains[0].partition_broadcast(P)).then_inc(gain_landed, 16)

        def pool_band_pe(pe):
            pe.wait_ge(ev.pool_c_landed, 16)
            pe.wait_ge(proj_out[0], 8)
            for g in range(4):
                dst = psum[:, 2 + g // 2, (g % 2) * S:(g % 2 + 1) * S]
                nc.tensor.matmul(dst, p_in[:, 0, g * P:(g + 1) * P], pool_c[:, g, 0:256],
                                 start=True, stop=False, skip_group_check=True)
                mm = nc.tensor.matmul(dst[:, P:S], p_in[:, 1, g * P:(g + 1) * P], pool_c[:, g, 256:384],
                                      start=False, stop=True, skip_group_check=True)
                if g % 2:
                    mm.then_inc(ev.banded, 1)

        def pool_weight_pe(pe):
            for g in range(4):
                if g % 2 == 0:
                    pe.wait_ge(ev.pooled_ready, g // 2 + 1)
                mm = nc.tensor.matmul(psum[:, 2 + g // 2, (g % 2) * S:(g % 2 + 1) * S],
                                      pool_c[:, g, 384:512], pooled[:, g, :], start=True, stop=True,
                                      skip_group_check=True)
                if g % 2:
                    mm.then_inc(ev.pool_done, 1)

        def head_squares(dve, src, i, out_count):
            dve.wait_ge(proj_out[0], out_count)
            squares = psum[:, 4 + 2 * i:6 + 2 * i, :]
            link(nc.vector.tensor_tensor(squares, src[:], src[:], ALU.mult))
            nc.vector.tensor_reduce(hss[:, 16 * i:16 * i + 16], squares.rearrange("p t (h d) -> p (t h) d", d=DH),
                                    AX.X, ALU.add).then_inc(ev.ss_ready, 1)

        def head_rms(act, i):
            act.wait_ge(ev.ss_ready, i + 1)
            nc.scalar.activation(hrms[:, 16 * i:16 * i + 16], hss[:, 16 * i:16 * i + 16], ACT.Sqrt, bias=eps,
                                 scale=1.0 / DH).then_inc(ev.rms_ready, 1)

        def head_norm(dve, src, i):
            dve.wait_ge(ev.rms_ready, i + 1)
            r = hrs[:, 16 * i:16 * i + 16]
            link(nc.vector.reciprocal(r, hrms[:, 16 * i:16 * i + 16]))
            view = src[:].rearrange("p t (h d) -> p (t h) d", d=DH)
            nc.vector.tensor_tensor(view, view, r.unsqueeze(2).to_broadcast([P, 16, DH]), ALU.mult
                                    ).then_inc(ev.qk_ready, 1)

        def turn_pairs(pe, src, b0, signal):
            for t in range(T):
                for j in range(PAIRS):
                    mm = nc.tensor.transpose(psum[:, b0 + t, j * P:(j + 1) * P], src[:, t, j * P:(j + 1) * P], ident)
                mm.then_inc(signal, 1)

        def pairs_view(b):
            return bank(b).rearrange("p (j s) -> p j s", j=PAIRS)

        SCORES = ((4, 5), (6, 7, 0, 1))

        def scores_pe(pe, t):
            n = (t + 1) * P
            per = W4 // n
            for par in range(2):
                rows = slice(64 * par, 64 * par + 64)
                for i in range(PAIRS):
                    b = SCORES[t][par if t == 0 else 2 * par + i // per]
                    mm = nc.tensor.matmul(psum[:, b, (i % per) * n:(i % per + 1) * n], qT0[rows, i, t * P:(t + 1) * P],
                                          kT0[rows, i, 0:n], start=True, stop=True, skip_group_check=True)
                    if i % per == per - 1:
                        mm.then_inc(ev.scored, 1)

        def softmax_dve(dve, t):
            n = (t + 1) * P
            per = W4 // n
            for m, b in enumerate(SCORES[t]):
                dve.wait_ge(ev.scored, (0 if t == 0 else 2) + m + 1)
                view = pb[t][:, m * per:(m + 1) * per, :]
                nc.vector.tensor_tensor(view, bank(b).rearrange("p (j k) -> p j k", k=n), view, ALU.add
                                        ).then_inc(ev.biased, 1)
            dve.wait_ge(ev.biased, 2 if t == 0 else 6)
            nc.vector.tensor_reduce(nmax[:, 8 * t:8 * t + 8], pb[t][:], AX.X, ALU.max, negate=True
                                    ).then_inc(ev.nmax_ready, 1)

        def softmax_act(act, t):
            act.wait_ge(ev.nmax_ready, t + 1)
            for j in range(HEADS):
                nc.scalar.activation(pb[t][:, j, :], pb[t][:, j, :], ACT.Exp, bias=nmax[:, 8 * t + j:8 * t + j + 1],
                                     accum_out=rsum[:, 8 * t + j:8 * t + j + 1]).then_inc(ev.probs_ready, 1)

        def turn_probs(pe, t):
            for kt in range(t + 1):
                for j in range(HEADS):
                    b = SCORES[t][2 * kt + j // 4]
                    if kt == 0:
                        pe.wait_ge(ev.probs_ready, 8 * t + j + 1)
                    mm = nc.tensor.transpose(psum[:, b, (j % 4) * P:(j % 4 + 1) * P],
                                             pb[t][:, j, kt * P:(kt + 1) * P], ident)
                    if j % 4 == 3:
                        mm.then_inc(ev.probs_turned, 1)

        def pt_copy(eng, signal, t, m):
            eng.wait_ge(ev.probs_turned, (0 if t == 0 else 2) + m + 1)
            dst = pt0[:, 4 * m:4 * m + 4, :] if t == 0 else pt1[:, m // 2, 4 * (m % 2):4 * (m % 2) + 4, :]
            copy = nc.scalar.copy if eng is nc.scalar else nc.vector.tensor_copy
            copy(dst, bank(SCORES[t][m]).rearrange("p (j s) -> p j s", j=4)).then_inc(signal, 1)

        def pv_pe(pe, t):
            for j in range(HEADS):
                hd = 2 * (j % 4) + j // 4
                for kt in range(t + 1):
                    lhs = pt0[:, j, :] if t == 0 else pt1[:, kt, j, :]
                    mm = nc.tensor.matmul(psum[:, 4 + t, hd * DH:(hd + 1) * DH], lhs, v_in[:, kt, hd * DH:(hd + 1) * DH],
                                          start=(kt == 0), stop=(kt == t), skip_group_check=True)
            mm.then_inc(ev.pv_done, 1)

        def att_dve(dve, t):
            link(nc.vector.reciprocal(rinv[:, 8 * t:8 * t + 8], rsum[:, 8 * t:8 * t + 8]))
            dve.wait_ge(ev.pv_done, t + 1)
            for par in range(2):
                r = rinv[:, 8 * t + 4 * par:8 * t + 4 * par + 4]
                nc.vector.tensor_tensor(att[:, t, :].rearrange("p (i a d) -> p a i d", a=2, d=DH)[:, par],
                                        bank(4 + t).rearrange("p (i a d) -> p a i d", a=2, d=DH)[:, par],
                                        r.unsqueeze(2).to_broadcast([P, 4, DH]), ALU.mult).then_inc(ev.att_ready, 1)

        def turn_att(pe, t):
            pe.wait_ge(ev.att_ready, 2 * t + 2)
            for j in range(4):
                mm = nc.tensor.transpose(psum[:, 6 + t, j * P:(j + 1) * P], att[:, t, j * P:(j + 1) * P], ident)
            mm.then_inc(ev.att_turned, 1)

        def even_pe(pe):
            def even_block(nb, halves=(0, 1)):
                project(pe, 0, 0, hnT_hi0, hnT_lo0, PROJ0, nb, halves)

            pe.wait_ge(zeros_ready, 1)
            keep_warm_pe(12)
            pe.wait_ge(cst_landed, 16)
            turn_pe(pe, x_landed, (16, 16))
            keep_warm_pe(8)
            even_block(0)
            even_block(1)
            pe.wait_ge(ev.qk_ready, 1)
            turn_pairs(pe, q_in, 4, ev.qk_turned)
            even_block(2)
            pe.wait_ge(ev.qk_ready, 2)
            turn_pairs(pe, k_in, 6, ev.qk_turned)
            even_block(3, (0,))
            pe.wait_ge(ev.qT_ready, 4)
            pe.wait_ge(proj_out[0], 6)
            scores_pe(pe, 0)
            scores_pe(pe, 1)
            even_block(3, (1,))
            pe.wait_ge(ev.biased, 2)
            turn_probs(pe, 0)
            pool_band_pe(pe)
            pe.wait_ge(ev.pt_act, 1)
            pe.wait_ge(ev.pt_dve, 1)
            pv_pe(pe, 0)
            pool_weight_pe(pe)
            pe.wait_ge(ev.biased, 6)
            turn_probs(pe, 1)
            pe.wait_ge(ev.mixP_lo_ready, 2)
            pe.wait_ge(ev.pt_act, 3)
            pe.wait_ge(ev.pt_dve, 3)
            pv_pe(pe, 1)
            out_step(pe, OUT0, EVEN_OUT, 0, mixP_hi, mixP_lo)
            turn_att(pe, 0)
            turn_att(pe, 1)
            out_step(pe, OUT0, EVEN_OUT, 1, mixP_hi, mixP_lo)
            pe.wait_ge(ev.mixA_lo_ready, 2)
            out_step(pe, OUT0, EVEN_OUT, 2, mixA_hi, mixA_lo)
            out_step(pe, OUT0, EVEN_OUT, 3, mixA_hi, mixA_lo)

        def even_act(act):
            split_hi(act, 0)
            turned_hi(act, 0, hnT_hi0)
            split_hi(act, 1)
            square_act(act, 0, 0, x_landed, 0)
            square_act(act, 0, 1, x_landed, 0)
            rms_act(act, 0)
            dst = {"p": p_in, "q": q_in, "k": k_in, "v": v_in}
            for c in range(2 * len(EVEN_BLOCKS)):
                if c % 2 == 0 and c > 0:
                    block_out(act, 0, PROJ0, c // 2 - 1, dst[EVEN_BLOCKS[c // 2 - 1]])
                if c in (3, 5):
                    head_rms(act, (c - 3) // 2)
                split_hi(act, PROJ0 + c + AHEAD)
            softmax_act(act, 0)
            block_out(act, 0, PROJ0, 3, v_in)
            pt_copy(act, ev.pt_act, 0, 0)
            softmax_act(act, 1)
            act.wait_ge(ev.cols_landed, 16)
            for b in range(2):
                act.wait_ge(ev.pool_done, b + 1)
                for g in (2 * b, 2 * b + 1):
                    nc.scalar.activation(mixP_hi[:, g, :], psum[:, 2 + b, (g % 2) * S:(g % 2 + 1) * S],
                                         ACT.Copy, scale=cols0[:, 2 + g:3 + g]).then_inc(ev.mixP_hi_ready, 1)
            pt_copy(act, ev.pt_act, 1, 0)
            pt_copy(act, ev.pt_act, 1, 2)
            split_hi(act, OUT0 + AHEAD)
            for t in range(T):
                act.wait_ge(ev.att_turned, t + 1)
                nc.scalar.copy(mixA_hi[:, :, t * P:(t + 1) * P], pairs_view(6 + t)).then_inc(ev.mixA_hi_ready, 1)
            for c in range(OUT0 + 1, OUT0 + 4):
                split_hi(act, c + AHEAD)
            square_act(act, 1, 0, res_added[0], 0)
            square_act(act, 1, 1, res_added[0], 0)

        def even_dve(dve):
            split_lo(dve, 0)
            turned_lo(dve, 0, hnT_hi0, hnT_lo0)
            split_lo(dve, 1)
            rstd_dve(dve, 0)
            for c in range(2 * len(EVEN_BLOCKS)):
                if c == 2:
                    head_squares(dve, q_in, 0, 2)
                if c == 3:
                    head_norm(dve, q_in, 0)
                if c == 4:
                    dve.wait_ge(ev.cols_landed, 16)
                    for t in range(T):
                        dve.wait_ge(ev.qk_turned, t + 1)
                        nc.vector.tensor_scalar(qT0[:, :, t * P:(t + 1) * P], pairs_view(4 + t), cols0[:, 0:1],
                                                DH ** -0.5, ALU.mult, ALU.mult).then_inc(ev.qT_ready, 1)
                    head_squares(dve, k_in, 1, 4)
                if c == 5:
                    head_norm(dve, k_in, 1)
                if c == 6:
                    for t in range(T):
                        dve.wait_ge(ev.qk_turned, t + 3)
                        nc.vector.tensor_scalar(kT0[:, :, t * P:(t + 1) * P], pairs_view(6 + t), cols0[:, 1:2], None,
                                                ALU.mult).then_inc(ev.qT_ready, 1)
                split_lo(dve, PROJ0 + c + AHEAD)
            dve.wait_ge(ev.bias_masked, 2)
            softmax_dve(dve, 0)
            softmax_dve(dve, 1)
            pt_copy(dve, ev.pt_dve, 0, 1)
            for b in range(2):
                dve.wait_ge(ev.banded, b + 1)
                nc.vector.tensor_copy(pooled[:, 2 * b:2 * b + 2, :], bank(2 + b).rearrange("p (j s) -> p j s", j=2)
                                      ).then_inc(ev.pooled_ready, 1)
            att_dve(dve, 0)
            for g in range(4):
                dve.wait_ge(ev.mixP_hi_ready, 2 * (g // 2) + 2)
                ins = nc.vector.scalar_tensor_tensor(
                    mixP_lo[:, g, :], psum[:, 2 + g // 2, (g % 2) * S:(g % 2 + 1) * S], cols0[:, 2 + g:3 + g],
                    mixP_hi[:, g, :].bitcast(F32), ALU.mult, ALU.subtract)
                if g % 2:
                    ins.then_inc(ev.mixP_lo_ready, 1)
            pt_copy(dve, ev.pt_dve, 1, 1)
            pt_copy(dve, ev.pt_dve, 1, 3)
            att_dve(dve, 1)
            split_lo(dve, OUT0 + AHEAD)
            for t in range(T):
                dve.wait_ge(ev.mixA_hi_ready, t + 1)
                nc.vector.tensor_tensor(mixA_lo[:, :, t * P:(t + 1) * P], pairs_view(6 + t),
                                        mixA_hi[:, :, t * P:(t + 1) * P].bitcast(F32), ALU.subtract
                                        ).then_inc(ev.mixA_lo_ready, 1)
            for c in range(OUT0 + 1, OUT0 + 4):
                if c == OUT0 + 3:
                    residual(dve, 0, OUT0, 0)
                    hg_dve(dve, 0, 0)
                split_lo(dve, c + AHEAD)
            residual(dve, 0, OUT0, 1)

        hnT_hi1, hnT_lo1 = at("hnT_hi1", [P, KD, S], 0, F32R), at("hnT_lo1", [P, KD, S], 8, F32R)
        qT1, kT1 = at("qT1", [P, PAIRS, S], 24), at("kT1", [P, PAIRS, S], 28)
        mixD_hi, mixD_lo = at("mixD_hi", [P, 4, S], 0, F32R), at("mixD_lo", [P, 4, S], 4, F32R)
        q1_in, k1_in, v1_in = at("q1_in", [P, T, W4], 16), at("k1_in", [P, T, W4], 20), at("v1_in", [P, T, W4], 32)
        vv_in, u_in = at("vv_in", [P, T, W4], 16), at("u_in", [P, T, W4], 20)
        mixC_hi, mixC_lo = at("mixC_hi", [P, 4, S], 24, F32R), at("mixC_lo", [P, 4, S], 28, F32R)
        HALF = 4 * S + 4 * P
        stick = [at("stick0", [P, HALF], 36), at("stick1", [P, HALF], 42)]
        vgain = at("vgain", [P, W4], 32)
        sgu = nc.alloc_sbuf_tensor_at("sgu", [P, 4 * P + 4], F32, offset=gain_at)
        bigid = nc.alloc_sbuf_tensor_at("bigid", [P, P], F32R, offset=gain_at + 2304)
        tri = nc.alloc_sbuf_tensor_at("tri", [P, P], F32R, offset=gain_at + 2816)
        ssv, rmsv, rsv = stat[:, 16:18], stat[:, 18:20], stat[:, 20:22]
        od = sems("odd", "sgu_landed", "vgain_landed", "ssv_ready", "rmsv_ready", "vn_ready", "gated", "yc_ready",
                  "yc_turned", "mixC_hi_ready", "mixC_lo_ready", "qk_turned", "qT_ready", "z_done", "abs_ready",
                  "exp_ready", "ln_ready", "rest_ready", "sum_done", "stick_ready", "av_done", "mixD_hi_ready",
                  "mixD_lo_ready", "big_ready", "tril_ready")

        def odd_pool_loads(pool):
            pool.wait_ge(norm.hg_ready, 4)
            pool.dma_start(sgu[:], odd_sgu).then_inc(od.sgu_landed, 16)
            pool.wait_ge(norm.lo_ready, 5)
            pool.dma_start(vgain[:], odd_vgain.partition_broadcast(P)).then_inc(od.vgain_landed, 16)
            pool.wait_ge(od.sgu_landed, 16)
            view = sgu[:, 0:4 * P].rearrange("p (g t) -> p g t", g=4)
            nc.gpsimd.affine_select(out=view, in_=view, pattern=[[0, 4], [1, P]], compare_op=ALU.is_ge, fill=0.0,
                                    base=0, channel_multiplier=-1).then_inc(od.tril_ready, 1)
            pool.wait_ge(od.yc_ready, 8)
            pool.wait_ge(od.sum_done, 2)
            pool.dma_start(gain[:], gains[1].partition_broadcast(P)).then_inc(gain_landed, 16)

        def gating_pe(pe):
            pe.wait_ge(od.tril_ready, 1)
            pe.wait_ge(proj_out[1], 8)
            for n in range(T):
                pe.wait_ge(od.vn_ready, n + 1)
                for g in range(4):
                    mm = nc.tensor.matmul(psum[:, 2 + n, g * P:(g + 1) * P], sgu[:, g * P:(g + 1) * P],
                                          vv_in[:, n, g * P:(g + 1) * P], start=True, stop=True, skip_group_check=True)
                mm.then_inc(od.gated, 1)

        def half_parts(view):
            return (view[:, 0:4 * S].rearrange("p (i s) -> p i s", i=4),
                    view[:, 4 * S:HALF].rearrange("p (i s) -> p i s", i=4))

        z_banks = psum[:, 4:7, :].rearrange("p b n -> p (b n)")

        def z_pe(pe, par):
            rows = slice(64 * par, 64 * par + 64)
            z0, z1 = half_parts(z_banks)
            for i in range(PAIRS):
                nc.tensor.matmul(z0[:, i, :], kT1[rows, i, 0:P], qT1[rows, i, :], start=(i % 2 == 0), stop=False,
                                 skip_group_check=True)
            for i in range(PAIRS):
                mm = nc.tensor.matmul(z1[:, i, :], kT1[rows, i, P:S], qT1[rows, i, P:S], start=(i == 0), stop=False,
                                      skip_group_check=True)
            mm.then_inc(od.z_done, 1)

        def sum_pe(pe, par):
            z0, z1 = half_parts(z_banks)
            r0, r1 = half_parts(stick[par][:])
            pe.wait_ge(od.rest_ready, 3 * (par + 1))
            for m in range(2):
                hd = slice(2 * m, 2 * m + 2)
                nc.tensor.matmul(z0[:, hd, :], negtri, r0[:, hd, :], start=False, stop=False, skip_group_check=True)
                nc.tensor.matmul(z0[:, hd, P:S], negones, r1[:, hd, :], start=False, stop=False, skip_group_check=True)
            nc.tensor.matmul(z1[:, :, :], negtri, r1[:, :, :], start=False, stop=False, skip_group_check=True)
            if par == 0:
                pe.wait_ge(od.big_ready, 2)
            for i in range(PAIRS):
                nc.tensor.matmul(z0[:, i, 0:P], bigid[:], tri[:], start=False, stop=True, skip_group_check=True)
                mm = nc.tensor.matmul(z1[:, i, :], bigid[:], tri[:], start=False, stop=True, skip_group_check=True)
            mm.then_inc(od.sum_done, 1)

        def av_pe(pe, par):
            pe.wait_ge(od.stick_ready, par + 1)
            a0, a1 = half_parts(stick[par][:])
            for i in range(PAIRS):
                hd = 2 * i + par
                dst = psum[64 * (i // 2):64 * (i // 2) + 64, 7 - par, (i % 2) * S:(i % 2 + 1) * S]
                nc.tensor.matmul(dst, v1_in[:, 0, hd * DH:(hd + 1) * DH], a0[:, i, :], start=True, stop=False,
                                 skip_group_check=True)
                mm = nc.tensor.matmul(dst[:, P:S], v1_in[:, 1, hd * DH:(hd + 1) * DH], a1[:, i, :],
                                      start=False, stop=True, skip_group_check=True)
            mm.then_inc(od.av_done, 1)

        def odd_pe(pe):
            def odd_block(nb, halves=(0, 1)):
                project(pe, 2, 1, hnT_hi1, hnT_lo1, PROJ1, nb, halves)

            turn_pe(pe, m.h_added, (4 * GROUPS - 2, 4 * GROUPS))
            odd_block(0)
            odd_block(1)
            pe.wait_ge(proj_out[1], 2)
            turn_pairs(pe, q1_in, 4, od.qk_turned)
            odd_block(2, (0,))
            pe.wait_ge(proj_out[1], 4)
            turn_pairs(pe, k1_in, 6, od.qk_turned)
            odd_block(2, (1,))
            pe.wait_ge(od.qT_ready, 4)
            z_pe(pe, 0)
            odd_block(3)
            sum_pe(pe, 0)
            gating_pe(pe)
            odd_block(4, (0,))
            pe.wait_ge(od.stick_ready, 1)
            z_pe(pe, 1)
            pe.wait_ge(od.yc_ready, 8)
            turn_pairs(pe, u_in, 2, od.yc_turned)
            odd_block(4, (1,))
            pe.wait_ge(od.mixC_lo_ready, 2)
            out_step(pe, OUT1, ODD_OUT, 0, mixC_hi, mixC_lo)
            sum_pe(pe, 1)
            pe.wait_ge(proj_out[1], 10)
            av_pe(pe, 0)
            av_pe(pe, 1)
            out_step(pe, OUT1, ODD_OUT, 1, mixC_hi, mixC_lo)
            pe.wait_ge(od.mixD_lo_ready, 2)
            out_step(pe, OUT1, ODD_OUT, 2, mixD_hi, mixD_lo)
            out_step(pe, OUT1, ODD_OUT, 3, mixD_hi, mixD_lo)

        def stick_act(act, par):
            soft = stick[par]
            act.wait_ge(od.z_done, par + 1)
            nc.scalar.activation(soft[:], z_banks, ACT.Abs).then_inc(od.abs_ready, 1)
            act.wait_ge(od.abs_ready, par + 1)
            nc.scalar.activation(soft[:], soft[:], ACT.Exp, scale=-1.0).then_inc(od.exp_ready, 1)
            act.wait_ge(od.exp_ready, par + 1)
            nc.scalar.activation(soft[:], soft[:], ACT.Ln, bias=1.0).then_inc(od.ln_ready, 1)

        def stick_dve(dve, par):
            rest = stick[par]
            r0, r1 = half_parts(rest[:])
            dve.wait_ge(od.ln_ready, par + 1)
            nc.vector.scalar_tensor_tensor(rest[:], z_banks, 0.0, rest[:], ALU.max, ALU.add).then_inc(od.rest_ready, 1)
            dve.wait_ge(od.rest_ready, 3 * par + 1)
            mask = before.unsqueeze(1).to_broadcast([P, 4, P])
            nc.vector.tensor_tensor(r0[:, :, 0:P], r0[:, :, 0:P], mask, ALU.mult).then_inc(od.rest_ready, 1)
            nc.vector.tensor_tensor(r1, r1, mask, ALU.mult).then_inc(od.rest_ready, 1)

        def weights_act(act, par):
            act.wait_ge(od.sum_done, par + 1)
            nc.scalar.activation(stick[par][:], z_banks, ACT.Exp).then_inc(od.stick_ready, 1)

        def mixD_act(act, par):
            act.wait_ge(od.av_done, par + 1)
            nc.scalar.copy(mixD_hi[:, 2 * par:2 * par + 2, :], bank(7 - par).rearrange("p (j s) -> p j s", j=2)
                           ).then_inc(od.mixD_hi_ready, 1)

        def mixD_dve(dve, par):
            dve.wait_ge(od.mixD_hi_ready, par + 1)
            nc.vector.tensor_tensor(mixD_lo[:, 2 * par:2 * par + 2, :],
                                    bank(7 - par).rearrange("p (j s) -> p j s", j=2),
                                    mixD_hi[:, 2 * par:2 * par + 2, :].bitcast(F32), ALU.subtract
                                    ).then_inc(od.mixD_lo_ready, 1)

        def odd_act(act):
            split_hi(act, PROJ1 + 1)
            square_act(act, 2, 0, m.h_added, 4 * GROUPS - 4)
            turned_hi(act, 2, hnT_hi1)
            square_act(act, 2, 1, m.h_added, 4 * GROUPS - 4)
            rms_act(act, 2)
            dst = {"vv": vv_in, "u": u_in, "q": q1_in, "k": k1_in, "v": v1_in}
            for c in range(2 * len(ODD_BLOCKS)):
                if c % 2 == 0 and c > 0:
                    name = ODD_BLOCKS[c // 2 - 1]
                    block_out(act, 1, PROJ1, c // 2 - 1, dst[name], ACT.Gelu if name in ("vv", "u") else ACT.Copy)
                if c == 7:
                    act.wait_ge(od.ssv_ready, 2)
                    nc.scalar.activation(rmsv, ssv, ACT.Sqrt, bias=eps, scale=1.0 / W4).then_inc(od.rmsv_ready, 1)
                if c == 8:
                    weights_act(act, 0)
                if c == 9:
                    stick_act(act, 1)
                    act.wait_ge(od.yc_turned, T)
                    for t in range(T):
                        nc.scalar.copy(mixC_hi[:, :, t * P:(t + 1) * P], pairs_view(2 + t)).then_inc(od.mixC_hi_ready, 1)
                split_hi(act, PROJ1 + c + AHEAD)
                if c == 6:
                    stick_act(act, 0)
            block_out(act, 1, PROJ1, 4, v1_in)
            split_hi(act, OUT1 + AHEAD)
            weights_act(act, 1)
            mixD_act(act, 0)
            mixD_act(act, 1)
            for c in range(OUT1 + 1, OUT1 + 4):
                split_hi(act, c + AHEAD)
            square_act(act, 3, 0, res_added[1], 0)
            square_act(act, 3, 1, res_added[1], 0)

        def odd_dve(dve):
            dve.wait_ge(norm.hg_ready, 4)
            nc.vector.tensor_scalar(bigid[:], ident, -NEG, None, ALU.mult).then_inc(od.big_ready, 1)
            nc.vector.tensor_copy(tri[:], negtri).then_inc(od.big_ready, 1)
            turned_lo(dve, 2, hnT_hi1, hnT_lo1, (0, 1))
            split_lo(dve, PROJ1 + 1)
            turned_lo(dve, 2, hnT_hi1, hnT_lo1, (2, 3))
            rstd_dve(dve, 2)
            for c in range(2 * len(ODD_BLOCKS)):
                if c == 4:
                    for t in range(T):
                        dve.wait_ge(od.qk_turned, t + 1)
                        nc.vector.tensor_scalar(qT1[:, :, t * P:(t + 1) * P], pairs_view(4 + t), DH ** -0.5, None,
                                                ALU.mult).then_inc(od.qT_ready, 1)
                if c == 5:
                    for t in range(T):
                        dve.wait_ge(od.qk_turned, t + 3)
                        nc.vector.tensor_copy(kT1[:, :, t * P:(t + 1) * P], pairs_view(6 + t)).then_inc(od.qT_ready, 1)
                if c == 6:
                    dve.wait_ge(proj_out[1], 6)
                    for t in range(T):
                        nc.vector.tensor_tensor_reduce(u_in[:, t, :], vv_in[:, t, :], vv_in[:, t, :], 1.0, 0.0,
                                                       ALU.mult, ALU.add, ssv[:, t:t + 1]).then_inc(od.ssv_ready, 1)
                if c == 7:
                    stick_dve(dve, 0)
                    dve.wait_ge(od.rmsv_ready, 1)
                    link(nc.vector.reciprocal(rsv, rmsv))
                    dve.wait_ge(od.vgain_landed, 16)
                    for t in range(T):
                        nc.vector.scalar_tensor_tensor(vv_in[:, t, :], vv_in[:, t, :], rsv[:, t:t + 1], vgain[:],
                                                       ALU.mult, ALU.mult).then_inc(od.vn_ready, 1)
                split_lo(dve, PROJ1 + c + AHEAD)
                if c == 8:
                    dve.wait_ge(proj_out[1], 8)
                    for n in range(T):
                        dve.wait_ge(od.gated, n + 1)
                        for g in range(4):
                            cs = slice(g * P, (g + 1) * P)
                            nc.vector.scalar_tensor_tensor(u_in[:, n, cs], psum[:, 2 + n, cs],
                                                           sgu[:, 4 * P + g:4 * P + g + 1], u_in[:, n, cs],
                                                           ALU.add, ALU.mult).then_inc(od.yc_ready, 1)
                    for t in range(T):
                        dve.wait_ge(od.mixC_hi_ready, t + 1)
                        nc.vector.tensor_tensor(mixC_lo[:, :, t * P:(t + 1) * P], pairs_view(2 + t),
                                                mixC_hi[:, :, t * P:(t + 1) * P].bitcast(F32), ALU.subtract
                                                ).then_inc(od.mixC_lo_ready, 1)
            stick_dve(dve, 1)
            split_lo(dve, OUT1 + AHEAD)
            mixD_dve(dve, 0)
            mixD_dve(dve, 1)
            for c in range(OUT1 + 1, OUT1 + 4):
                if c == OUT1 + 3:
                    residual(dve, 1, OUT1, 0)
                    hg_dve(dve, 1, 0)
                split_lo(dve, c + AHEAD)
            residual(dve, 1, OUT1, 1)

        hn_hi, hn_lo = at("hn_hi", [P, T, D], 0, F32R), at("hn_lo", [P, T, D], 8, F32R)
        hgT = at("hgT", [P, KD, S], 16)
        y_hi, y_lo = at("y_hi", [P, D], 16, F32R), at("y_lo", [P, D], 20, F32R)
        hg = at("hg", [P, T, D], 24)
        x_hi, x_lo = at("x_hi", [P, KD, P], 24, F32R), at("x_lo", [P, KD, P], 28, F32R)
        pick, pickT = at("pick", [P, T, P], 32, F32R), at("pickT", [P, S], 33, F32R)
        gate, hid = at("gate", [P, FF], 34), at("hid", [P, FF], 35)
        hidT_hi, hidT_lo = at("hidT_hi", [P, 2, 2, P], 36, F32R), at("hidT_lo", [P, 2, 2, P], 38, F32R)
        rw = at("rw", [P, KD, 36], 40)
        LOGITS = GROUPS * (EXPERTS + 1)
        logitsT = at("logitsT", [LOGITS, S], 44)
        r_small = at("r_small", [P, 512], 41.25)
        top_idx = at("top_idx", [P, T, 8], 43.5, U32)
        spill = at("spill", [P, 2], 43.75, I32)

        def rs(a, n):
            return r_small[:, a:a + n]
        def by_tile(a, n):
            return rs(a, T * n).rearrange("p (t n) -> p t n", t=T)
        logits = by_tile(0, 36)
        gmax, first, ngmax = rs(72, 2), rs(74, 2), rs(76, 2)
        tied, onehot, noh, pos_tmp = by_tile(80, 4), by_tile(88, 4), by_tile(96, 4), by_tile(104, 4)
        e_of_g = rs(120, 64).rearrange("p (t e g) -> p t e g", t=T, e=EXPERTS)
        e8, emax, idx = by_tile(184, 8), by_tile(200, 8), by_tile(216, 8)
        gexp, gsum = rs(250, 8), rs(258, 2)
        ediff, eexp, esum, w1, w2 = rs(260, 2), rs(262, 2), rs(264, 2), rs(266, 2), rs(268, 2)
        comb, comb2 = by_tile(270, 8), by_tile(286, 8)
        pos = rs(302, 2)
        member = rs(304, 10).rearrange("p (g t) -> p g t", t=T)
        slot_of = rs(324, 10).rearrange("p (g t) -> p g t", t=T)
        over, over_g = rs(334, 4), rs(338, 2)
        cg = rs(340, 8)

        moe_names = ("rw_landed", "hn_hi_ready", "hn_lo_ready", "hgT_act", "hgT_dve", "logits_done", "logitsT_ready", "routed",
                     "ngmax_ready", "gsum_ready", "ediff_ready", "eexp_ready", "onehot_ready", "ranked", "comb_ready",
                     "spill_ready", "pick_ready", "gathered", "x_hi_ready", "x_lo_ready", "pickT_turned",
                     "pickT_ready", "cg_done", "cg_ready", "gate_ready", "hid_ready", "hid_turned", "hidT_hi_ready",
                     "hidT_lo_ready", "y_done", "y_hi_ready", "y_lo_ready", "scattered", "h_added")
        m = sems("moe", *moe_names)
        def group_no(layer, g):
            return g + GROUPS * layer

        sp_names = ("pick_ready", "gathered", "x_hi_ready", "x_lo_ready", "pickT_turned", "pickT_ready", "cg_done",
                    "cg_ready", "landed", "gu_done", "gate_ready", "hid_ready", "hid_turned", "hidT_hi_ready", "hidT_lo_ready",
                    "used", "y_hi_ready", "y_lo_ready", "scattered", "h_added")
        spill_sems = [sems(f"spill{i}", *sp_names) for i in range(2)]
        MOE_C0 = (MOE0, MOE1)

        def pass_sems(layer, gi):
            if isinstance(gi, int) and gi == GROUPS:
                return spill_sems[layer], 0
            return m, group_no(layer, gi)

        def moe_pool_loads(pool, layer):
            if layer == 0:
                pool.wait_ge(ev.probs_turned, 6)
            else:
                pool.wait_ge(od.av_done, 2)
            pool.dma_start(rw[:], routers[layer]).then_inc(m.rw_landed, 16)

        def route_pe(pe, layer):
            turn_pe(pe, res_added[layer], (2, 4))
            pe.wait_ge(m.rw_landed, 16 * (layer + 1))
            for half in range(2):
                pe.wait_ge(m.hgT_act, 2 * layer + half + 1)
                pe.wait_ge(m.hgT_dve, 2 * layer + half + 1)
                for k in range(4 * half, 4 * half + 4):
                    mm = nc.tensor.matmul(psum[0:LOGITS, 0, 0:S], rw[:, k, :], hgT[:, k, :], start=(k == 0),
                                          stop=(k == KD - 1))
            mm.then_inc(m.logits_done, 1)
            keep_warm_pe(2)
            pe.wait_ge(m.logitsT_ready, layer + 1)
            for t in range(T):
                mm = nc.tensor.transpose(psum[:, 2, LOGITS * t:LOGITS * (t + 1)], logitsT[:, t * P:(t + 1) * P],
                                         ident[0:LOGITS, 0:LOGITS])
            mm.then_inc(m.routed, 1)
            keep_warm_pe(6)
            pe.wait_ge(m.onehot_ready, 2 * layer + 1)
            nc.tensor.matmul(psum[:, 1, 0:4], before, onehot[:, 0, :], start=True, stop=True, skip_group_check=True)
            nc.tensor.matmul(psum[:, 1, 4:8], before, onehot[:, 1, :], start=True, stop=False, skip_group_check=True)
            pe.wait_ge(m.onehot_ready, 2 * layer + 2)
            nc.tensor.matmul(psum[:, 1, 4:8], negones, noh[:, 0, :], start=False, stop=True, skip_group_check=True)
            for t in range(T):
                mm = nc.tensor.matmul(psum[:, 1, 8:12], negones, noh[:, t, :], start=(t == 0), stop=(t == 1),
                                      skip_group_check=True)
            mm.then_inc(m.ranked, 1)
            keep_warm_pe(6)

        def route_act(act, layer):
            ph = 2 * layer + 1
            for b in (0, 2):
                act.wait_ge(norm.turned, 4 * ph + b + 1)
                for j in range(2):
                    ins = nc.scalar.activation(hgT[:, 2 * b + j, :], psum[:, 4 + b, j * S:(j + 1) * S], ACT.Copy,
                                               scale=gain_col(ph, 2 * b + j))
                ins.then_inc(m.hgT_act, 1)
            rms_act(act, ph)
            act.wait_ge(norm.rstd_ready, ph + 1)
            act.wait_ge(norm.hg_ready, 4 * (layer + 1))
            for t in range(T):
                nc.scalar.activation(hn_hi[:, t, :], hg[:, t, :], ACT.Copy, scale=rstd[:, t:t + 1]
                                     ).then_inc(m.hn_hi_ready, 1)
            act.wait_ge(m.ngmax_ready, layer + 1)
            for t in range(T):
                nc.scalar.activation(gexp[:, 4 * t:4 * t + 4], logits[:, t, 0:4], ACT.Exp, bias=ngmax[:, t:t + 1],
                                     accum_out=gsum[:, t:t + 1]).then_inc(m.gsum_ready, 1)

        def hn_lo_dve(dve, layer, t):
            dve.wait_ge(m.hn_hi_ready, 2 * layer + t + 1)
            nc.vector.scalar_tensor_tensor(hn_lo[:, t, :], hg[:, t, :], rstd[:, t:t + 1], hn_hi[:, t, :].bitcast(F32),
                                           ALU.mult, ALU.subtract).then_inc(m.hn_lo_ready, 1)

        def route_dve(dve, layer):
            ph = 2 * layer + 1
            for b in (1, 3):
                dve.wait_ge(norm.turned, 4 * ph + b + 1)
                for j in range(2):
                    ins = nc.vector.tensor_scalar(hgT[:, 2 * b + j, :], psum[:, 4 + b, j * S:(j + 1) * S],
                                                  gain_col(ph, 2 * b + j), None, ALU.mult)
                ins.then_inc(m.hgT_dve, 1)
            hg_dve(dve, layer, 1)
            rstd_dve(dve, ph)
            dve.wait_ge(norm.rstd_ready, ph + 1)
            dve.wait_ge(m.logits_done, layer + 1)
            nc.vector.tensor_copy(logitsT[:], psum[0:LOGITS, 0, 0:S]).then_inc(m.logitsT_ready, 1)
            dve.wait_ge(m.routed, layer + 1)
            for t in range(T):
                ins = nc.vector.tensor_scalar(logits[:, t, :], psum[:, 2, LOGITS * t:LOGITS * (t + 1)],
                                              rstd[:, t:t + 1], None, ALU.mult)
            link(ins)
            groups_of = logits[:, :, 0:GROUPS]
            link(nc.vector.tensor_reduce(gmax, groups_of, AX.X, ALU.max))
            link(nc.vector.tensor_tensor(tied, groups_of, gmax.unsqueeze(2).to_broadcast([P, T, GROUPS]), ALU.is_equal))
            link(nc.vector.tensor_tensor(tied, tied, falling.unsqueeze(1).to_broadcast([P, T, GROUPS]), ALU.mult))
            link(nc.vector.tensor_reduce(first, tied, AX.X, ALU.max))
            nc.vector.tensor_tensor(onehot, tied, first.unsqueeze(2).to_broadcast([P, T, GROUPS]), ALU.is_equal
                                    ).then_inc(m.onehot_ready, 1)
            dve.wait_ge(m.onehot_ready, 2 * layer + 1)
            nc.vector.tensor_scalar(noh, onehot, -1.0, None, ALU.mult).then_inc(m.onehot_ready, 1)
            nc.vector.tensor_scalar(ngmax, gmax, -1.0, None, ALU.mult).then_inc(m.ngmax_ready, 1)
            hn_lo_dve(dve, layer, 0)
            link(nc.vector.memset(member[:, GROUPS, :], 1.0))
            link(nc.vector.tensor_copy(member[:, 0:GROUPS, :], onehot.rearrange("p t g -> p g t")))
            dve.wait_ge(m.ranked, layer + 1)
            link(nc.vector.tensor_tensor(pos_tmp, psum[:, 1, 0:8].rearrange("p (t n) -> p t n", t=T), onehot, ALU.mult))
            link(nc.vector.tensor_reduce(pos, pos_tmp, AX.X, ALU.add))
            link(nc.vector.tensor_copy(slot_of[:, 0:GROUPS, :], pos.unsqueeze(1).to_broadcast([P, GROUPS, T])))
            pick_dve(dve, layer, 0)
            hn_lo_dve(dve, layer, 1)
            link(nc.vector.tensor_scalar(slot_of[:, GROUPS, :], pos, -float(P), None, ALU.add))

        def x_and_weights_dve(dve, layer):
            link(nc.vector.tensor_scalar(over, psum[:, 1, 8:12], float(P), None, ALU.is_gt))
            link(nc.vector.tensor_tensor(e_of_g, logits[:, :, 4:36].rearrange("p t (g e) -> p t e g", g=GROUPS),
                                         onehot.unsqueeze(2).to_broadcast([P, T, EXPERTS, GROUPS]), ALU.mult))
            link(nc.vector.tensor_reduce(e8, e_of_g, AX.X, ALU.add))
            for t in range(T):
                link(nc.vector.max(emax[:, t, :], e8[:, t, :]))
                link(nc.vector.max_index(top_idx[:, t, :], emax[:, t, :], e8[:, t, :]))
            link(nc.vector.tensor_copy(idx, top_idx[:]))
            nc.vector.tensor_tensor(ediff, emax[:, :, 1], emax[:, :, 0], ALU.subtract).then_inc(m.ediff_ready, 1)
            x_of_dve(dve, layer, 0)
            dve.wait_ge(m.eexp_ready, layer + 1)
            dve.wait_ge(m.gsum_ready, 2 * (layer + 1))
            link(nc.vector.scalar_tensor_tensor(esum, eexp, 1.0, gsum, ALU.add, ALU.mult))
            link(nc.vector.reciprocal(w1, esum))
            link(nc.vector.tensor_tensor(w2, eexp, w1, ALU.mult))
            for t in range(T):
                link(nc.vector.tensor_scalar(comb[:, t, :], iota[:, 0:8], idx[:, t, 0:1], w1[:, t:t + 1],
                                             ALU.is_equal, ALU.mult))
                link(nc.vector.tensor_scalar(comb2[:, t, :], iota[:, 0:8], idx[:, t, 1:2], w2[:, t:t + 1],
                                             ALU.is_equal, ALU.mult))
            nc.vector.tensor_tensor(comb, comb, comb2, ALU.add).then_inc(m.comb_ready, 1)

        def spill_flag_dve(dve, layer):
            link(nc.vector.scalar_tensor_tensor(over, iota[:, 0:4], 1.0, over, ALU.add, ALU.mult))
            link(nc.vector.tensor_reduce(over_g[:, 0:1], over, AX.X, ALU.add))
            link(nc.vector.tensor_scalar(over_g[:, 1:2], over_g[:, 0:1], -1.0, 0.0, ALU.add, ALU.max))
            nc.vector.tensor_copy(spill[:], over_g).then_inc(m.spill_ready, 1)

        def pick_dve(dve, layer, gi):
            s, n = pass_sems(layer, gi)
            if not (layer == 0 and isinstance(gi, int) and gi == 0):
                dve.wait_ge(m.cg_done, group_no(layer, gi))
            for t in range(T):
                def entry(a):
                    return a[:, bass.ds(gi, 1), t:t + 1].rearrange("p a t -> p (a t)")
                nc.vector.tensor_scalar(pick[:, t, :], iota, entry(slot_of), entry(member), ALU.is_equal, ALU.mult
                                        ).then_inc(s.pick_ready, 1)

        GATHER = ((5, "hi", 0), (6, "hi", 1), (7, "lo", 0), (0, "lo", 1))

        def gather_pe(pe, layer, gi, parts=("hi", "lo")):
            s, no = pass_sems(layer, gi)
            pe.wait_ge(s.pick_ready, 2 * no + 2)
            for n, (b, part, half) in enumerate(GATHER):
                if part not in parts:
                    continue
                if n == 0:
                    pe.wait_ge(m.hn_hi_ready, 2 * (layer + 1))
                if n == 2:
                    pe.wait_ge(m.hn_lo_ready, 2 * (layer + 1))
                src = hn_hi if part == "hi" else hn_lo
                for kk in range(4):
                    k = 4 * half + kk
                    for t in range(T):
                        mm = nc.tensor.matmul(psum[:, b, kk * P:(kk + 1) * P], src[:, t, k * P:(k + 1) * P],
                                              pick[:, t, :], start=(t == 0), stop=(t == 1), skip_group_check=True)
                mm.then_inc(s.gathered, 1)

        def x_copy(eng, layer, gi, part, half):
            n = [i for i, (_, p_, h_) in enumerate(GATHER) if (p_, h_) == (part, half)][0]
            s, no = pass_sems(layer, gi)
            eng.wait_ge(s.gathered, 4 * no + n + 1)
            src = bank(GATHER[n][0]).rearrange("p (k s) -> p k s", k=4)
            ks = slice(4 * half, 4 * half + 4)
            dst, signal = (x_hi, s.x_hi_ready) if part == "hi" else (x_lo, s.x_lo_ready)
            copy = nc.scalar.copy if eng is nc.scalar else nc.vector.tensor_copy
            copy(dst[:, ks, :], src).then_inc(signal, 1)

        def pickT_pe(pe, layer, gi):
            s, no = pass_sems(layer, gi)
            for t in range(T):
                mm = nc.tensor.transpose(psum[:, 4, S + t * P:S + (t + 1) * P], pick[:, t, :].bitcast(F32), ident)
            mm.then_inc(s.pickT_turned, 1)
            pe.wait_ge(m.comb_ready, layer + 1)
            for t in range(T):
                mm = nc.tensor.matmul(psum[:, 1, 0:8], pick[:, t, :].bitcast(F32), comb[:, t, :], start=(t == 0),
                                      stop=(t == 1), skip_group_check=True)
            mm.then_inc(s.cg_done, 1)

        def pickT_act(act, layer, gi):
            s, no = pass_sems(layer, gi)
            act.wait_ge(s.pickT_turned, no + 1)
            nc.scalar.copy(pickT[:], psum[:, 4, S:2 * S]).then_inc(s.pickT_ready, 1)

        def cg_act(act, layer, gi):
            s, no = pass_sems(layer, gi)
            act.wait_ge(s.cg_done, no + 1)
            nc.scalar.copy(cg, psum[:, 1, 0:8]).then_inc(s.cg_ready, 1)

        def gate_up_pe(pe, layer, g, e, half):
            c = MOE_C0[layer] + gu_at(e, half)
            pe.wait_ge(lo_done, c + 1 + g * PER_GROUP)
            if half == 0 and e == 1:
                pe.wait_ge(m.cg_ready, group_no(layer, g) + 1)
            for kk in range(4):
                k = 4 * half + kk
                mm = three(bank(e % 2), x_hi[:, k, :], x_lo[:, k, :], c, slice(kk * W4, (kk + 1) * W4),
                           k == 0, k == KD - 1)
            mm.then_inc(w_used, 1)

        def gate_act(act, layer, g, e):
            act.wait_ge(w_used, MOE_C0[layer] + gu_at(e, 1) + 1 + g * PER_GROUP)
            nc.scalar.activation(gate[:], psum[:, e % 2, 0:FF], ACT.Silu).then_inc(m.gate_ready, 1)

        def hid_dve(dve, layer, g, e):
            dve.wait_ge(m.gate_ready, group_no(layer, g) * EXPERTS + e + 1)
            if e == 0:
                dve.wait_ge(m.cg_ready, group_no(layer, g) + 1)
            nc.vector.scalar_tensor_tensor(hid[:], psum[:, e % 2, FF:2 * FF], cg[:, e:e + 1], gate[:], ALU.mult,
                                           ALU.mult).then_inc(m.hid_ready, 1)

        def turn_hid(pe, layer, g, e):
            pe.wait_ge(m.hid_ready, group_no(layer, g) * EXPERTS + e + 1)
            if e == 0:
                pe.wait_ge(m.pickT_ready, group_no(layer, g) + 1)
            for j in range(2):
                mm = nc.tensor.transpose(psum[:, 4, j * P:(j + 1) * P], hid[:, j * P:(j + 1) * P], ident)
            mm.then_inc(m.hid_turned, 1)

        def hidT_act(act, layer, g, e):
            act.wait_ge(m.hid_turned, group_no(layer, g) * EXPERTS + e + 1)
            nc.scalar.copy(hidT_hi[:, e % 2], psum[:, 4, 0:2 * P].rearrange("p (j s) -> p j s", j=2)
                           ).then_inc(m.hidT_hi_ready, 1)

        def hidT_dve(dve, layer, g, e):
            dve.wait_ge(m.hidT_hi_ready, group_no(layer, g) * EXPERTS + e + 1)
            nc.vector.tensor_tensor(hidT_lo[:, e % 2], psum[:, 4, 0:2 * P].rearrange("p (j s) -> p j s", j=2),
                                    hidT_hi[:, e % 2].bitcast(F32), ALU.subtract).then_inc(m.hidT_lo_ready, 1)

        def down_pe(pe, layer, g, e, blocks=(0, 1)):
            c = MOE_C0[layer] + down_at(e)
            if blocks[0] == 0:
                pe.wait_ge(lo_done, c + 1 + g * PER_GROUP)
                pe.wait_ge(m.hidT_lo_ready, group_no(layer, g) * EXPERTS + e + 1)
            for n in blocks:
                for j in range(2):
                    mm = three(bank(2 + n), hidT_hi[:, e % 2, j, :], hidT_lo[:, e % 2, j, :], c,
                               slice(j * D + n * W4, j * D + (n + 1) * W4), e == 0 and j == 0,
                               e == EXPERTS - 1 and j == 1)
                if n == 0 and e == EXPERTS - 1:
                    mm.then_inc(m.y_done, 1)
            if blocks[-1] == 1:
                mm.then_inc(w_used, 1)

        SCATTER = ((0, 0, 6), (1, 0, 5), (0, 1, 7), (1, 1, 6))

        def scatter_pe(pe, layer, g):
            for n, (t, blk, b) in enumerate(SCATTER):
                if n % 2 == 0:
                    pe.wait_ge(m.y_lo_ready, 2 * group_no(layer, g) + blk + 1)
                if n == 3:
                    pe.wait_ge(m.h_added, 4 * group_no(layer, g) + 1)
                cols = slice(blk * W4, (blk + 1) * W4)
                nc.tensor.matmul(bank(b), pickT[:, t * P:(t + 1) * P], y_hi[:, cols], start=True, stop=False)
                nc.tensor.matmul(bank(b), pickT[:, t * P:(t + 1) * P], y_lo[:, cols], start=False, stop=True
                                 ).then_inc(m.scattered, 1)

        def y_act(act, layer, g, n):
            if n == 0:
                act.wait_ge(m.y_done, group_no(layer, g) + 1)
            else:
                act.wait_ge(w_used, MOE_C0[layer] + PER_GROUP + g * PER_GROUP)
            nc.scalar.copy(y_hi[:, n * W4:(n + 1) * W4], bank(2 + n)).then_inc(m.y_hi_ready, 1)

        def y_dve(dve, layer, g, n):
            cols = slice(n * W4, (n + 1) * W4)
            dve.wait_ge(m.y_hi_ready, 2 * group_no(layer, g) + n + 1)
            nc.vector.tensor_tensor(y_lo[:, cols], bank(2 + n), y_hi[:, cols].bitcast(F32), ALU.subtract
                                    ).then_inc(m.y_lo_ready, 1)

        def h_dve(dve, layer, g, which=range(4)):
            for n, (t, blk, b) in enumerate(SCATTER):
                if n not in which:
                    continue
                dve.wait_ge(m.scattered, 4 * group_no(layer, g) + n + 1)
                cols = slice(blk * W4, (blk + 1) * W4)
                nc.vector.tensor_tensor(h[:, t, cols], bank(b), h[:, t, cols], ALU.add).then_inc(m.h_added, 1)

        LASTE = EXPERTS - 1

        def open_pe(pe, layer, g):
            pe.wait_ge(m.x_hi_ready, 2 * group_no(layer, g) + 2)
            pe.wait_ge(m.x_lo_ready, 2 * group_no(layer, g) + 2)
            gate_up_pe(pe, layer, g, 0, 0)

        def group_pe(pe, layer, g, last):
            pickT_pe(pe, layer, g)
            for e in range(EXPERTS):
                if e > 0:
                    gate_up_pe(pe, layer, g, e, 0)
                    turn_hid(pe, layer, g, e - 1)
                gate_up_pe(pe, layer, g, e, 1)
                if 0 < e < LASTE:
                    down_pe(pe, layer, g, e - 1)
            down_pe(pe, layer, g, LASTE - 1, (0,))
            if not last:
                gather_pe(pe, layer, g + 1, ("hi",))
            turn_hid(pe, layer, g, LASTE)
            if not last:
                gather_pe(pe, layer, g + 1, ("lo",))
            down_pe(pe, layer, g, LASTE - 1, (1,))
            down_pe(pe, layer, g, LASTE)
            if not last:
                open_pe(pe, layer, g + 1)
            scatter_pe(pe, layer, g)

        def group_steps(eng, layer, g, last, small, turned, x_of_next, sums, late, split):
            for i in range(1, PER_GROUP + (0 if last else 1)):
                for e in range(EXPERTS):
                    if i == gu_at(e, 1) + 1:
                        small(eng, layer, g, e)
                    if e < LASTE and i == gu_at(e + 1, 1):
                        turned(eng, layer, g, e)
                if i == down_at(LASTE - 1):
                    turned(eng, layer, g, LASTE)
                if i == PER_GROUP:
                    sums(eng, layer, g)
                if not (last and i + AHEAD >= PER_GROUP + 1 - layer):
                    split(eng, MOE_C0[layer] + i + AHEAD, g)
                if i == down_at(LASTE - 1) and not last:
                    x_of_next(eng, layer, g + 1)
                if i == PER_GROUP:
                    late(eng, layer, g)
            if last:
                sums(eng, layer, g)
                late(eng, layer, g)

        def x_of_act(act, layer, gi):
            x_copy(act, layer, gi, "hi", 0)
            x_copy(act, layer, gi, "hi", 1)
            x_copy(act, layer, gi, "lo", 1)

        def x_of_dve(dve, layer, gi):
            x_copy(dve, layer, gi, "lo", 0)

        def sums_act(act, layer, g):
            y_act(act, layer, g, 0)
            y_act(act, layer, g, 1)

        def sums_dve(dve, layer, g):
            y_dve(dve, layer, g, 0)
            y_dve(dve, layer, g, 1)
            h_dve(dve, layer, g, (0,))

        def late_dve(dve, layer, g):
            h_dve(dve, layer, g, (1, 2, 3))

        def late_act(act, layer, g):
            pass

        def group_act(act, layer, g, last):
            pickT_act(act, layer, g)
            cg_act(act, layer, g)
            group_steps(act, layer, g, last, gate_act, hidT_act, x_of_act, sums_act, late_act, split_hi)

        def group_dve(dve, layer, g, last):
            def hid_and_pick(dve, layer, g, e):
                hid_dve(dve, layer, g, e)
                if e == 1 and not last:
                    pick_dve(dve, layer, g + 1)

            group_steps(dve, layer, g, last, hid_and_pick, hidT_dve, x_of_dve, sums_dve, late_dve, split_lo)

        def groups(eng, layer, body):
            with eng.Fori(0, GROUPS - 1) as g:
                body(eng, layer, g, False)
            body(eng, layer, GROUPS - 1, True)

        SPILL_SLOT = [(MOE_CHUNKS + MOE0 + AHEAD + n) % RAW for n in range(3)]

        def spill_flag(eng, layer):
            eng.wait_ge(m.spill_ready, layer + 1)
            return eng.value_load(spill[0:1, 0:1], min_val=0, max_val=GROUPS)

        def spill_sp(sp, layer):
            flag = spill_flag(sp, layer)
            spl = spill_sems[layer]
            full = sp.value_load(spill[0:1, 1:2], min_val=0, max_val=GROUPS - 1)
            with sp.If(flag > 0):
                sp.wait_ge(lo_done, MOE_C0[layer] + MOE_CHUNKS)
                for e in range(EXPERTS):
                    if e:
                        sp.wait_ge(spl.used, e)
                    for n, at_ in enumerate((gu_at(e, 0), gu_at(e, 1), down_at(e))):
                        index = full * PER_GROUP + (MOE_C0[layer] + at_)
                        sp.dma_start(raw[:, SPILL_SLOT[n], :], stream[bass.ds(index, 1)].rearrange("a p n -> (a p) n")
                                     ).then_inc(spl.landed, 16)
                sp.wait_ge(spl.h_added, 4)
            with sp.Else():
                pass

        def spill_pe(pe, layer):
            flag = spill_flag(pe, layer)
            spl = spill_sems[layer]
            with pe.If(flag > 0):
                pe.wait_ge(m.h_added, 4 * GROUPS * (layer + 1))
                gather_pe(pe, layer, GROUPS)
                pickT_pe(pe, layer, GROUPS)
                pe.wait_ge(spl.x_hi_ready, 2)
                pe.wait_ge(spl.x_lo_ready, 2)
                pe.wait_ge(spl.pickT_ready, 1)
                pe.wait_ge(spl.cg_ready, 1)
                for e in range(EXPERTS):
                    pe.wait_ge(spl.landed, 48 * (e + 1))
                    for k in range(KD):
                        rhs = raw[:, SPILL_SLOT[k // 4], (k % 4) * W4:(k % 4 + 1) * W4]
                        nc.tensor.matmul(bank(0), x_hi[:, k, :].bitcast(F32), rhs, start=(k == 0), stop=False)
                        mm = nc.tensor.matmul(bank(0), x_lo[:, k, :].bitcast(F32), rhs, start=False, stop=(k == KD - 1))
                    mm.then_inc(spl.gu_done, 1)
                    pe.wait_ge(spl.hid_ready, e + 1)
                    for j in range(2):
                        mm = nc.tensor.transpose(psum[:, 4, j * P:(j + 1) * P], hid[:, j * P:(j + 1) * P], ident)
                    mm.then_inc(spl.hid_turned, 1)
                    pe.wait_ge(spl.hidT_lo_ready, e + 1)
                    for n in range(2):
                        for j in range(2):
                            rhs = raw[:, SPILL_SLOT[2], j * D + n * W4:j * D + (n + 1) * W4]
                            nc.tensor.matmul(bank(2 + n), hidT_hi[:, 0, j, :].bitcast(F32), rhs,
                                             start=(e == 0 and j == 0), stop=False)
                            mm = nc.tensor.matmul(bank(2 + n), hidT_lo[:, 0, j, :].bitcast(F32), rhs, start=False,
                                                  stop=(e == LASTE and j == 1))
                    mm.then_inc(spl.used, 1)
                pe.wait_ge(spl.y_lo_ready, 2)
                for n, (t, blk, b) in enumerate(SCATTER):
                    cols = slice(blk * W4, (blk + 1) * W4)
                    if n == 3:
                        pe.wait_ge(spl.h_added, 1)
                    nc.tensor.matmul(bank(b), pickT[:, t * P:(t + 1) * P], y_hi[:, cols], start=True, stop=False)
                    nc.tensor.matmul(bank(b), pickT[:, t * P:(t + 1) * P], y_lo[:, cols], start=False, stop=True
                                     ).then_inc(spl.scattered, 1)
                pe.wait_ge(spl.h_added, 4)
            with pe.Else():
                pass

        def spill_act(act, layer):
            flag = spill_flag(act, layer)
            spl = spill_sems[layer]
            with act.If(flag > 0):
                x_of_act(act, layer, GROUPS)
                pickT_act(act, layer, GROUPS)
                cg_act(act, layer, GROUPS)
                for e in range(EXPERTS):
                    act.wait_ge(spl.gu_done, e + 1)
                    nc.scalar.activation(gate[:], psum[:, 0, 0:FF], ACT.Silu).then_inc(spl.gate_ready, 1)
                    act.wait_ge(spl.hid_turned, e + 1)
                    if e:
                        act.wait_ge(spl.used, e)
                    nc.scalar.copy(hidT_hi[:, 0], psum[:, 4, 0:2 * P].rearrange("p (j s) -> p j s", j=2)
                                   ).then_inc(spl.hidT_hi_ready, 1)
                act.wait_ge(spl.used, EXPERTS)
                for n in range(2):
                    nc.scalar.copy(y_hi[:, n * W4:(n + 1) * W4], bank(2 + n)).then_inc(spl.y_hi_ready, 1)
                act.wait_ge(spl.h_added, 4)
            with act.Else():
                pass

        def spill_dve(dve, layer):
            flag = spill_flag(dve, layer)
            spl = spill_sems[layer]
            with dve.If(flag > 0):
                pick_dve(dve, layer, GROUPS)
                x_of_dve(dve, layer, GROUPS)
                dve.wait_ge(spl.cg_ready, 1)
                for e in range(EXPERTS):
                    dve.wait_ge(spl.gate_ready, e + 1)
                    nc.vector.scalar_tensor_tensor(hid[:], psum[:, 0, FF:2 * FF], cg[:, e:e + 1], gate[:], ALU.mult,
                                                   ALU.mult).then_inc(spl.hid_ready, 1)
                    dve.wait_ge(spl.hidT_hi_ready, e + 1)
                    nc.vector.tensor_tensor(hidT_lo[:, 0], psum[:, 4, 0:2 * P].rearrange("p (j s) -> p j s", j=2),
                                            hidT_hi[:, 0].bitcast(F32), ALU.subtract).then_inc(spl.hidT_lo_ready, 1)
                for n in range(2):
                    cols = slice(n * W4, (n + 1) * W4)
                    dve.wait_ge(spl.y_hi_ready, n + 1)
                    nc.vector.tensor_tensor(y_lo[:, cols], bank(2 + n), y_hi[:, cols].bitcast(F32), ALU.subtract
                                            ).then_inc(spl.y_lo_ready, 1)
                dve.wait_ge(m.h_added, 4 * GROUPS * (layer + 1))
                for n, (t, blk, b) in enumerate(SCATTER):
                    dve.wait_ge(spl.scattered, n + 1)
                    cols = slice(blk * W4, (blk + 1) * W4)
                    nc.vector.tensor_tensor(h[:, t, cols], bank(b), h[:, t, cols], ALU.add).then_inc(spl.h_added, 1)
                dve.wait_ge(spl.h_added, 4)
            with dve.Else():
                pass

        block = ctx.enter_context(nc.Block())

        @block.sync
        def _(sp):
            load_chunk(sp, (0, 0))
            sp.dma_start(cst[:], consts).then_inc(cst_landed, 16)
            sp.dma_start(h[:], x.rearrange("a (t p) d -> p (a t) d", p=P)).then_inc(x_landed, 16)
            for c in range(1, RAW):
                load_chunk(sp, (c, c))
            for c in range(RAW, 2 * RAW):
                if c == RAW + 3:
                    sp.wait_ge(ev.pool_c_landed, 16)
                load_chunk(sp, (c % RAW, c), c - RAW + 1)
            with sp.Fori(2, PROJ1 // RAW) as turn:
                for i in range(RAW):
                    load_chunk(sp, (i, turn * RAW + i), turn * RAW + (i - RAW + 1))
            for c in range(PROJ1, PROJ1 + AHEAD):
                load_chunk(sp, (c % RAW, c), c - RAW + 1)
            spill_sp(sp, 0)
            for c in range(PROJ1 + AHEAD, PROJ1 + RAW):
                load_chunk(sp, (c % RAW, c), c - RAW + 1)
            with sp.Fori(PROJ1 // RAW + 1, CHUNKS // RAW) as turn:
                for i in range(RAW):
                    load_chunk(sp, (i, turn * RAW + i), turn * RAW + (i - RAW + 1))
            for c in range(CHUNKS // RAW * RAW, CHUNKS):
                load_chunk(sp, (c % RAW, c), c - RAW + 1)
            spill_sp(sp, 1)
            for nb in range(2):
                sp.wait_ge(m.h_added, 2 * 4 * GROUPS - 2 + 2 * nb)
                sp.dma_start(out.rearrange("a (t p) d -> p (a t) d", p=P)[:, :, cols_of(nb)], h[:, :, cols_of(nb)]
                             ).then_inc(out_written, 16)
            sp.wait_ge(out_written, 32)

        @block.gpsimd
        def _(pool):
            nc.gpsimd.memset(zeros[:].bitcast(F32), 0.0).then_inc(zeros_ready, 1)
            even_pool_loads(pool)
            moe_pool_loads(pool, 0)
            odd_pool_loads(pool)
            moe_pool_loads(pool, 1)

        @block.tensor
        def _(pe):
            even_pe(pe)
            for layer in range(2):
                if layer:
                    odd_pe(pe)
                route_pe(pe, layer)
                gather_pe(pe, layer, 0)
                open_pe(pe, layer, 0)
                groups(pe, layer, group_pe)
                spill_pe(pe, layer)

        @block.scalar
        def _(act):
            even_act(act)
            for layer in range(2):
                if layer:
                    odd_act(act)
                route_act(act, layer)
                x_of_act(act, layer, 0)
                act.wait_ge(m.ediff_ready, layer + 1)
                nc.scalar.activation(eexp, ediff, ACT.Exp).then_inc(m.eexp_ready, 1)
                split_hi(act, MOE_C0[layer] + AHEAD)
                groups(act, layer, group_act)
                spill_act(act, layer)

        @block.vector
        def _(dve):
            even_dve(dve)
            for layer in range(2):
                if layer:
                    odd_dve(dve)
                route_dve(dve, layer)
                x_and_weights_dve(dve, layer)
                split_lo(dve, MOE_C0[layer] + AHEAD)
                spill_flag_dve(dve, layer)
                groups(dve, layer, group_dve)
                spill_dve(dve, layer)


def shape_constants():
    r = np.arange(P)
    c = np.zeros((P, C_N), np.float32)
    c[:, C_ID:C_ID + P] = np.eye(P)
    c[:, C_NTRI:C_NTRI + P] = -(r[:, None] >= r[None, :]).astype(np.float32)
    c[:, C_NONE:C_NONE + P] = -1
    c[:, C_LT:C_LT + P] = r[:, None] < r[None, :]
    c[:, C_IOTA:C_IOTA + P] = r[None, :]
    c[:, C_EPS] = EPS
    c[:, C_REV:C_REV + GROUPS] = GROUPS - np.arange(GROUPS)
    return c


def band_constants():
    s, t = np.arange(S)[:, None], np.arange(S)[None, :]
    full = np.stack([((s <= t) & (s > t - w)) / np.minimum(t + 1, w) - (s == t) for w in WINDOWS], 1)
    full = full.astype(np.float32)
    return full[:P], full[P:, :, P:]


_INS = ["x", "stream", "gains", "consts", "even_pool", "even_bias", "even_cols", "odd_sgu", "odd_vgain", "routers"]


def laid_out(a):
    def tiles(w):
        n = w.shape[1] // W4
        return w.reshape(2, 4, P, n, W4).transpose(3, 0, 2, 1, 4).reshape(n, 2, P, CH)

    stream = np.empty((CHUNKS, P, CH), np.float32)

    def mixer(c0, w_in, order, names, w_out, out_order):
        t = tiles(w_in)
        for nb, name in enumerate(order):
            stream[c0 + 2 * nb:c0 + 2 * nb + 2] = t[names.index(name)]
        t = tiles(w_out)
        for i, (half, nb) in enumerate(out_order):
            stream[c0 + 2 * len(order) + i] = t[nb, half]

    r = np.arange(512)
    tile, row = r // P, r % P
    head = 2 * (2 * (row // DH) + tile % 2) + tile // 2
    w_out_odd = a["w_out_odd"][0][np.concatenate([r, 512 + head * DH + row % DH])]
    mixer(PROJ0, a["w_in_even"][0], EVEN_BLOCKS, ("q", "k", "v", "p"), a["w_out_even"][0], EVEN_OUT)
    mixer(PROJ1, a["w_in_odd"][0], ODD_BLOCKS, ("u", "vv", "q", "k", "v"), w_out_odd, ODD_OUT)
    for layer, c0 in enumerate((MOE0, MOE1)):
        moe = stream[c0:c0 + MOE_CHUNKS].reshape(GROUPS, PER_GROUP, P, CH)
        for e in range(EXPERTS):
            for half in range(2):
                dst = moe[:, gu_at(e, half)].reshape(GROUPS, P, 4, 2, FF)
                for n, name in enumerate(("w_exp_gate", "w_exp_up")):
                    src = a[name][layer, :, e, half * 512:(half + 1) * 512, :]
                    dst[:, :, :, n, :] = src.reshape(GROUPS, 4, P, FF).transpose(0, 2, 1, 3)
            moe[:, down_at(e)].reshape(GROUPS, P, 2, D)[:] = (
                a["w_exp_down"][layer, :, e].reshape(GROUPS, 2, P, D).transpose(0, 2, 1, 3))

    order = [0, 2, 4, 6, 1, 3, 5, 7]
    q, k = np.arange(S)[:, None], np.arange(S)[None, :]
    bias = a["att_rel_bias"][0][:, np.clip(q - k, -128, 128) + 128][order]
    even_bias = np.concatenate([bias[:, :P, :P].transpose(1, 0, 2).reshape(P, -1),
                                bias[:, P:, :].transpose(1, 0, 2).reshape(P, -1)], 1)
    band0, band1 = band_constants()
    return {
        "x": a["x"],
        "stream": stream,
        "gains": a["ffn_norm"],
        "consts": np.concatenate([shape_constants()[:, :C_GAIN]] + [
            a[name][i].reshape(KD, P).T for name, i in
            (("mix_norm_even", 0), ("ffn_norm", 0), ("mix_norm_odd", 0), ("ffn_norm", 1))], 1),
        "even_pool": np.concatenate([band0, band1, a["pool_w"][0].transpose(1, 0, 2)], 2),
        "even_bias": even_bias,
        "even_cols": np.concatenate([np.tile(a["att_q_norm"][0], 2)[:, None], np.tile(a["att_k_norm"][0], 2)[:, None],
                                     a["pool_scale"][0].reshape(4, P).T], 1),
        "odd_sgu": np.concatenate([a["sgu_w"][0].transpose(2, 0, 1).reshape(P, 4 * P), a["sgu_b"][0].T], 1),
        "odd_vgain": a["sgu_v_norm"][0],
        "routers": np.concatenate([a["w_router_group"], a["w_router_expert"]], 2).reshape(2, KD, P, 36)
                   .transpose(0, 2, 1, 3),
    }


def kernel(**inputs):
    import concourse.bacc as _bacc
    from concourse.bass_utils import run_bass_kernel_spmd as _run

    nc = _bacc.Bacc("TRN2", target_bir_lowering=False, num_devices=1)
    data = laid_out({k: np.asarray(v) for k, v in inputs.items()})
    arrays, args = {}, []
    for name in _INS:
        arrays[name] = np.ascontiguousarray(data[name])
        args.append(nc.dram_tensor(name, arrays[name].shape, F32, kind="ExternalInput").ap())
    out = nc.dram_tensor("out", (1, S, D), F32, kind="ExternalOutput").ap()
    hybrid_kernel(nc, *args, out)
    r = _run(nc, [arrays], core_ids=[0])
    return r.results[0]["out"]
```
